# Optimizing a Trainium2 kernel written in Bass

```python
import math
import numpy as np
import jax
import jax.numpy as jnp
from jax import lax
import jax, jax.numpy as jnp

D_MODEL = 2048
BATCH = 1
SEQ = 256
DEPTH = 1

D_MIX = D_MODEL
SSD_WIDTH = D_MIX // 2
ATT_WIDTH = D_MIX - SSD_WIDTH

SSD_HEAD_DIM = 64
SSD_HEADS = SSD_WIDTH // SSD_HEAD_DIM
SSD_GROUPS = 2
SSD_STATE = 128
SSD_CHUNK = 128
CONV_WIDTH = 4
CONV_CH = SSD_WIDTH + 2 * SSD_GROUPS * SSD_STATE

ATT_HEAD_DIM = 64
ATT_HEADS = ATT_WIDTH // ATT_HEAD_DIM
ATT_KV_HEADS = 4
ATT_GROUP = ATT_HEADS // ATT_KV_HEADS
KV_WIDTH = ATT_KV_HEADS * ATT_HEAD_DIM
CMP_BLOCK = 32
CMP_STRIDE = 16
CMP_HIDDEN = 256
SEL_BLOCK = 64
N_SELECT = 16
WINDOW = 512
Q_BLOCK = 128
N_BRANCH = 3

ROPE_THETA = 500000.0
ROPE_DIM = ATT_HEAD_DIM // 4

D_FF = -((-8 * D_MODEL) // (3 * 256)) * 256

NORM_EPS = 1e-6
NEG_INF = -1e30
FORCE_SCORE = 1e4

IN_WIDTHS = (SSD_WIDTH, CONV_CH, SSD_HEADS, ATT_WIDTH, KV_WIDTH, KV_WIDTH, KV_WIDTH, KV_WIDTH, KV_WIDTH, KV_WIDTH, ATT_HEADS * N_BRANCH)
D_IN = sum(IN_WIDTHS)


def rmsnorm(x, w):
    xf = x.astype(jnp.float32)
    xf = xf * lax.rsqrt(jnp.mean(xf * xf, axis=-1, keepdims=True) + NORM_EPS)
    return xf.astype(x.dtype) * w

def rope_tables(seq, dtype):
    inv = 1.0 / (ROPE_THETA ** (jnp.arange(0, ROPE_DIM, 2, dtype=jnp.float32) / ROPE_DIM))
    ang = jnp.arange(seq, dtype=jnp.float32)[:, None] * inv[None, :]
    return jnp.cos(ang).astype(dtype), jnp.sin(ang).astype(dtype)

def partial_rope(x, cos, sin):
    half = ROPE_DIM // 2
    c = cos[None, :, None, :]
    s = sin[None, :, None, :]
    x1 = x[..., :half]
    x2 = x[..., half:ROPE_DIM]
    return jnp.concatenate([x1 * c - x2 * s, x2 * c + x1 * s, x[..., ROPE_DIM:]], axis=-1)

def causal_depthwise_conv(u, w, b):
    y = lax.conv_general_dilated(u, w[:, None, :].astype(u.dtype), window_strides=(1,), padding=((CONV_WIDTH - 1, 0),), dimension_numbers=('NWC', 'WIO', 'NWC'), feature_group_count=u.shape[-1])
    return y + b

def ssd_chunked(xdt, adt, bm, cm):
    bsz, seq = xdt.shape[:2]
    nc = seq // SSD_CHUNK
    hg = SSD_HEADS // SSD_GROUPS
    x = xdt.reshape(bsz, nc, SSD_CHUNK, SSD_GROUPS, hg, SSD_HEAD_DIM)
    a = adt.reshape(bsz, nc, SSD_CHUNK, SSD_GROUPS, hg)
    b = bm.reshape(bsz, nc, SSD_CHUNK, SSD_GROUPS, SSD_STATE)
    c = cm.reshape(bsz, nc, SSD_CHUNK, SSD_GROUPS, SSD_STATE)
    a_cum = jnp.cumsum(a, axis=2)
    causal = jnp.tril(jnp.ones((SSD_CHUNK, SSD_CHUNK), dtype=bool))[:, :, None, None]
    seg = a_cum[:, :, :, None] - a_cum[:, :, None, :]
    decay = jnp.exp(jnp.where(causal, seg, -jnp.inf))
    cb = jnp.einsum('bclgn,bcsgn->bclsg', c, b)
    y_diag = jnp.einsum('bclsgh,bcsghp->bclghp', cb[..., None] * decay, x)
    decay_states = jnp.exp(a_cum[:, :, -1:] - a_cum)
    states = jnp.einsum('bclgn,bclghp->bcghpn', b, x * decay_states[..., None])
    chunk_decay = jnp.exp(a_cum[:, :, -1])

    def step(h, inp):
        st, dec = inp
        return h * dec[..., None, None] + st, h

    h0 = jnp.zeros_like(states[:, 0])
    _, prev = lax.scan(step, h0, (jnp.moveaxis(states, 1, 0), jnp.moveaxis(chunk_decay, 1, 0)))
    prev = jnp.moveaxis(prev, 0, 1)
    y_off = jnp.einsum('bclgn,bcghpn->bclghp', c, prev) * jnp.exp(a_cum)[..., None]
    return (y_diag + y_off).reshape(bsz, seq, SSD_HEADS, SSD_HEAD_DIM)

def ssd_mixer(z, xbc, dt_raw, conv_w, conv_b, dt_bias, a_log, d_skip, norm_w):
    bsz, seq = z.shape[:2]
    xbc = jax.nn.silu(causal_depthwise_conv(xbc, conv_w, conv_b))
    xs, bm, cm = jnp.split(xbc, [SSD_WIDTH, SSD_WIDTH + SSD_GROUPS * SSD_STATE], axis=-1)
    xh = xs.reshape(bsz, seq, SSD_HEADS, SSD_HEAD_DIM)
    dt = jax.nn.softplus(dt_raw.astype(jnp.float32) + dt_bias.astype(jnp.float32))
    a = -jnp.exp(a_log.astype(jnp.float32))
    y = ssd_chunked(xh * dt[..., None], a * dt, bm.reshape(bsz, seq, SSD_GROUPS, SSD_STATE), cm.reshape(bsz, seq, SSD_GROUPS, SSD_STATE))
    y = y + d_skip[:, None] * xh
    y = y.reshape(bsz, seq, SSD_WIDTH).astype(z.dtype)
    return rmsnorm(y * jax.nn.silu(z), norm_w)

def selection_overlap(n_cmp, n_sel):
    cs = np.arange(n_cmp)[:, None] * CMP_STRIDE
    ce = cs + CMP_BLOCK
    ss = np.arange(n_sel)[None, :] * SEL_BLOCK
    se = ss + SEL_BLOCK
    ov = np.clip(np.minimum(ce, se) - np.maximum(cs, ss), 0, None)
    return (ov / CMP_BLOCK).astype(np.float32)

def compress_tokens(kv, w1, w2, pe):
    bsz, seq = kv.shape[:2]
    n_cmp = (seq - CMP_BLOCK) // CMP_STRIDE + 1
    idx = np.arange(n_cmp)[:, None] * CMP_STRIDE + np.arange(CMP_BLOCK)[None, :]
    blocks = kv[:, idx] + pe[None, None, :, None, :]
    flat = jnp.swapaxes(blocks, 2, 3).reshape(bsz, n_cmp, ATT_KV_HEADS, CMP_BLOCK * ATT_HEAD_DIM)
    return jax.nn.silu(flat @ w1) @ w2

def nsa_mixer(q, kc, vc, ks, vs, kw, vw, gate_raw, cmp_w1_k, cmp_w2_k, cmp_w1_v, cmp_w2_v, cmp_pe_k, cmp_pe_v, cos, sin):
    bsz, seq = q.shape[:2]
    hd = ATT_HEAD_DIM
    scale = hd ** -0.5
    q = q.reshape(bsz, seq, ATT_HEADS, hd)
    kc, vc, ks, vs, kw, vw = [t.reshape(bsz, seq, ATT_KV_HEADS, hd) for t in (kc, vc, ks, vs, kw, vw)]
    q_grp = q.reshape(bsz, seq, ATT_KV_HEADS, ATT_GROUP, hd)
    q_rot = partial_rope(q, cos, sin).reshape(bsz, seq, ATT_KV_HEADS, ATT_GROUP, hd)
    ks = partial_rope(ks, cos, sin)
    kw = partial_rope(kw, cos, sin)
    t_pos = jnp.arange(seq)

    k_cmp = compress_tokens(kc, cmp_w1_k, cmp_w2_k, cmp_pe_k)
    v_cmp = compress_tokens(vc, cmp_w1_v, cmp_w2_v, cmp_pe_v)
    n_cmp = k_cmp.shape[1]
    cmp_end = jnp.arange(n_cmp) * CMP_STRIDE + CMP_BLOCK - 1
    cmp_mask = cmp_end[None, :] <= t_pos[:, None]
    s_cmp = jnp.einsum('bshgd,bihd->bhgsi', q_grp, k_cmp).astype(jnp.float32) * scale
    p_cmp = jax.nn.softmax(jnp.where(cmp_mask, s_cmp, NEG_INF), axis=-1) * cmp_mask
    o_cmp = jnp.einsum('bhgsi,bihd->bshgd', p_cmp.astype(v_cmp.dtype), v_cmp)

    n_sel = seq // SEL_BLOCK
    k_top = min(N_SELECT, n_sel)
    overlap = jnp.asarray(selection_overlap(n_cmp, n_sel))
    imp = jnp.einsum('bhgsi,ij->bhsj', p_cmp, overlap)
    blk = jnp.arange(n_sel)[None, :]
    cur = (t_pos // SEL_BLOCK)[:, None]
    imp = jnp.where((blk == 0) | (blk == cur) | (blk == cur - 1), FORCE_SCORE, imp)
    imp = jnp.where(blk <= cur, imp, -1.0)
    top_val, top_idx = lax.top_k(imp, k_top)
    top_valid = top_val >= 0.0

    ks_blocks = ks.reshape(bsz, n_sel, SEL_BLOCK, ATT_KV_HEADS, hd).transpose(0, 3, 1, 2, 4)
    vs_blocks = vs.reshape(bsz, n_sel, SEL_BLOCK, ATT_KV_HEADS, hd).transpose(0, 3, 1, 2, 4)
    kw_pad = jnp.pad(kw, ((0, 0), (WINDOW, 0), (0, 0), (0, 0)))
    vw_pad = jnp.pad(vw, ((0, 0), (WINDOW, 0), (0, 0), (0, 0)))
    gather_blocks = jax.vmap(jax.vmap(lambda blocks, ix: blocks[ix]))
    q_offs = jnp.arange(Q_BLOCK)
    w_offs = jnp.arange(WINDOW + Q_BLOCK)
    s_offs = jnp.arange(SEL_BLOCK)

    def query_block(qb):
        s0 = qb * Q_BLOCK
        tq = s0 + q_offs
        qblk = lax.dynamic_slice_in_dim(q_rot, s0, Q_BLOCK, axis=1)
        ib = lax.dynamic_slice_in_dim(top_idx, s0, Q_BLOCK, axis=2)
        vb = lax.dynamic_slice_in_dim(top_valid, s0, Q_BLOCK, axis=2)
        kg = gather_blocks(ks_blocks, ib)
        vg = gather_blocks(vs_blocks, ib)
        kpos = ib[..., None] * SEL_BLOCK + s_offs
        m_sel = (kpos <= tq[:, None, None]) & vb[..., None]
        s_sel = jnp.einsum('bqhgd,bhqjkd->bhgqjk', qblk, kg).astype(jnp.float32) * scale
        s_sel = jnp.where(m_sel[:, :, None], s_sel, NEG_INF).reshape(bsz, ATT_KV_HEADS, ATT_GROUP, Q_BLOCK, k_top * SEL_BLOCK)
        p_sel = jax.nn.softmax(s_sel, axis=-1).astype(vg.dtype)
        o_sel = jnp.einsum('bhgqn,bhqnd->bqhgd', p_sel, vg.reshape(bsz, ATT_KV_HEADS, Q_BLOCK, k_top * SEL_BLOCK, hd))
        kwb = lax.dynamic_slice_in_dim(kw_pad, s0, WINDOW + Q_BLOCK, axis=1)
        vwb = lax.dynamic_slice_in_dim(vw_pad, s0, WINDOW + Q_BLOCK, axis=1)
        kp = s0 - WINDOW + w_offs
        dist = tq[:, None] - kp[None, :]
        m_win = (dist >= 0) & (dist < WINDOW) & (kp[None, :] >= 0)
        s_win = jnp.einsum('bqhgd,bkhd->bhgqk', qblk, kwb).astype(jnp.float32) * scale
        p_win = jax.nn.softmax(jnp.where(m_win, s_win, NEG_INF), axis=-1).astype(vwb.dtype)
        o_win = jnp.einsum('bhgqk,bkhd->bqhgd', p_win, vwb)
        return o_sel, o_win

    o_sel, o_win = lax.map(query_block, jnp.arange(seq // Q_BLOCK))
    o_sel = jnp.moveaxis(o_sel, 0, 1).reshape(bsz, seq, ATT_KV_HEADS, ATT_GROUP, hd)
    o_win = jnp.moveaxis(o_win, 0, 1).reshape(bsz, seq, ATT_KV_HEADS, ATT_GROUP, hd)
    g = jax.nn.sigmoid(gate_raw.astype(jnp.float32)).reshape(bsz, seq, ATT_KV_HEADS, ATT_GROUP, N_BRANCH, 1).astype(q.dtype)
    o = g[..., 0, :] * o_cmp + g[..., 1, :] * o_sel + g[..., 2, :] * o_win
    return o.reshape(bsz, seq, ATT_WIDTH)

def first_inputs(seed: int = 0) -> dict:
    key = jax.random.key(seed)
    k = jax.random.split(key, 24)
    f32 = jnp.float32
    L = DEPTH

    def dense(kk, shape, fan_in):
        return jax.random.normal(kk, shape, f32) * fan_in ** -0.5

    def gain(kk, shape):
        return 1.0 + 0.05 * jax.random.normal(kk, shape, f32)

    dt = jnp.exp(jax.random.uniform(k[5], (L, SSD_HEADS), f32, math.log(1e-3), math.log(1e-1)))
    return {
        'x': jax.random.normal(k[0], (BATCH, SEQ, D_MODEL), f32),
        'attn_norm_w': gain(k[1], (L, D_MODEL)),
        'w_in': dense(k[2], (L, D_MODEL, D_IN), D_MODEL),
        'conv_w': dense(k[3], (L, CONV_WIDTH, CONV_CH), CONV_WIDTH),
        'conv_b': 0.01 * jax.random.normal(k[4], (L, CONV_CH), f32),
        'dt_bias': dt + jnp.log(-jnp.expm1(-dt)),
        'a_log': jnp.log(jax.random.uniform(k[6], (L, SSD_HEADS), f32, 1.0, 16.0)),
        'd_skip': 1.0 + 0.1 * jax.random.normal(k[7], (L, SSD_HEADS), f32),
        'ssd_norm_w': gain(k[8], (L, SSD_WIDTH)),
        'cmp_w1_k': dense(k[9], (L, CMP_BLOCK * ATT_HEAD_DIM, CMP_HIDDEN), CMP_BLOCK * ATT_HEAD_DIM),
        'cmp_w2_k': dense(k[10], (L, CMP_HIDDEN, ATT_HEAD_DIM), CMP_HIDDEN),
        'cmp_w1_v': dense(k[11], (L, CMP_BLOCK * ATT_HEAD_DIM, CMP_HIDDEN), CMP_BLOCK * ATT_HEAD_DIM),
        'cmp_w2_v': dense(k[12], (L, CMP_HIDDEN, ATT_HEAD_DIM), CMP_HIDDEN),
        'cmp_pe_k': 0.1 * jax.random.normal(k[13], (L, CMP_BLOCK, ATT_HEAD_DIM), f32),
        'cmp_pe_v': 0.1 * jax.random.normal(k[14], (L, CMP_BLOCK, ATT_HEAD_DIM), f32),
        'w_out': dense(k[15], (L, D_MIX, D_MODEL), D_MIX),
        'ffn_norm_w': gain(k[16], (L, D_MODEL)),
        'w_gate': dense(k[17], (L, D_MODEL, D_FF), D_MODEL),
        'w_up': dense(k[18], (L, D_MODEL, D_FF), D_MODEL),
        'w_down': dense(k[19], (L, D_FF, D_MODEL), D_FF),
        'final_norm_w': gain(k[20], (D_MODEL,)),
    }

def first_block(x, attn_norm_w, w_in, conv_w, conv_b, dt_bias, a_log, d_skip, ssd_norm_w, cmp_w1_k, cmp_w2_k, cmp_w1_v, cmp_w2_v, cmp_pe_k, cmp_pe_v, w_out, ffn_norm_w, w_gate, w_up, w_down, final_norm_w):
    cos, sin = rope_tables(x.shape[1], x.dtype)
    split_at = np.cumsum(IN_WIDTHS)[:-1].tolist()
    h = x
    for l in range(DEPTH):
        u = rmsnorm(h, attn_norm_w[l])
        z, xbc, dt_raw, q, kc, vc, ks, vs, kw, vw, gate_raw = jnp.split(u @ w_in[l], split_at, axis=-1)
        y_ssd = ssd_mixer(z, xbc, dt_raw, conv_w[l], conv_b[l], dt_bias[l], a_log[l], d_skip[l], ssd_norm_w[l])
        y_att = nsa_mixer(q, kc, vc, ks, vs, kw, vw, gate_raw, cmp_w1_k[l], cmp_w2_k[l], cmp_w1_v[l], cmp_w2_v[l], cmp_pe_k[l], cmp_pe_v[l], cos, sin)
        mixed = jnp.concatenate([y_ssd.astype(h.dtype), y_att.astype(h.dtype)], axis=-1)
        h = h + mixed @ w_out[l]
        v = rmsnorm(h, ffn_norm_w[l])
        h = h + (jax.nn.silu(v @ w_gate[l]) * (v @ w_up[l])) @ w_down[l]
    return rmsnorm(h, final_norm_w)


D_MIX_2 = D_MODEL
D_FOX = D_MIX_2 // 2
D_HGRN = D_MIX_2 - D_FOX
FOX_HEADS = 8
FOX_HEAD_DIM = D_FOX // FOX_HEADS
HGRN_EXPAND = 128
HGRN_HEADS = D_HGRN // HGRN_EXPAND
HGRN_DV = D_HGRN // HGRN_HEADS
D_FF_2 = 5632
CONV_WIDTH_2 = 3
PLE_DIM = 256
CHUNK = 64
EPS = 1e-6

OFF_FOX_K = D_FOX
OFF_FOX_V = 2 * D_FOX
OFF_FOX_F = 3 * D_FOX
OFF_HG_Q = OFF_FOX_F + FOX_HEADS
OFF_HG_F = OFF_HG_Q + D_HGRN
OFF_HG_I = OFF_HG_F + D_HGRN
OFF_HG_G = OFF_HG_I + D_HGRN
N_IN = OFF_HG_G + D_HGRN


def rms_norm(x, g):
    xf = x.astype(jnp.float32)
    y = xf * lax.rsqrt(jnp.mean(xf * xf, axis=-1, keepdims=True) + EPS)
    return (y * g.astype(jnp.float32)).astype(x.dtype)

def forgetting_attention(q, k, v, f_logit):
    b, s, h, dh = q.shape
    scale = dh ** -0.5
    c = jnp.cumsum(jax.nn.log_sigmoid(f_logit.astype(jnp.float32)), axis=1).transpose(0, 2, 1)
    qh = q.transpose(0, 2, 1, 3)
    kh = k.transpose(0, 2, 1, 3)
    vh = v.transpose(0, 2, 1, 3)
    outs = []
    for blk in range(s // Q_BLOCK):
        q0 = blk * Q_BLOCK
        q1 = q0 + Q_BLOCK
        logits = jnp.einsum('bhqd,bhkd->bhqk', qh[:, :, q0:q1], kh[:, :, :q1]).astype(jnp.float32) * scale
        logits = logits + c[:, :, q0:q1, None] - c[:, :, None, :q1]
        causal = (q0 + jnp.arange(Q_BLOCK))[:, None] >= jnp.arange(q1)[None, :]
        probs = jax.nn.softmax(jnp.where(causal, logits, -jnp.inf), axis=-1)
        outs.append(jnp.einsum('bhqk,bhkd->bhqd', probs.astype(v.dtype), vh[:, :, :q1]))
    o = jnp.concatenate(outs, axis=2)
    return o.transpose(0, 2, 1, 3).reshape(b, s, h * dh)

def hgrn2_recurrence(q, k, v, log_f):
    b, s, h, dk = q.shape
    dv = v.shape[-1]
    n = s // CHUNK

    def to_chunks(t):
        return t.astype(jnp.float32).reshape(b, n, CHUNK, h, t.shape[-1]).transpose(1, 0, 3, 2, 4)

    tri = jnp.arange(CHUNK)[:, None] >= jnp.arange(CHUNK)[None, :]

    def step(state, xs):
        qc, kc, vc, gc = xs
        cum = jnp.cumsum(gc, axis=2)
        o_inter = jnp.einsum('bhtk,bhkv->bhtv', qc * jnp.exp(cum), state)
        rel = jnp.where(tri[:, :, None], cum[:, :, :, None, :] - cum[:, :, None, :, :], -jnp.inf)
        scores = jnp.einsum('bhtk,bhsk,bhtsk->bhts', qc, kc, jnp.exp(rel))
        o_intra = jnp.einsum('bhts,bhsv->bhtv', scores, vc)
        last = cum[:, :, -1:, :]
        new_state = jnp.exp(last[:, :, 0, :])[..., None] * state + jnp.einsum('bhsk,bhsv->bhkv', kc * jnp.exp(last - cum), vc)
        return new_state, o_inter + o_intra

    state0 = jnp.zeros((b, h, dk, dv), jnp.float32)
    _, o = lax.scan(step, state0, (to_chunks(q), to_chunks(k), to_chunks(v), to_chunks(log_f)))
    return o.transpose(1, 0, 3, 2, 4).reshape(b, s, h, dv).astype(q.dtype)

def hgrn_lower_bounds(w_lb):
    cum = jnp.cumsum(jax.nn.softmax(w_lb.astype(jnp.float32), axis=0), axis=0)
    return cum - cum[0:1]

def token_mixer(h, w_in, b_f, lb, g_o, w_out):
    b, s, _ = h.shape
    z = h @ w_in
    fox_shape = (b, s, FOX_HEADS, FOX_HEAD_DIM)
    q_a = z[..., :OFF_FOX_K].reshape(fox_shape)
    k_a = z[..., OFF_FOX_K:OFF_FOX_V].reshape(fox_shape)
    v_a = z[..., OFF_FOX_V:OFF_FOX_F].reshape(fox_shape)
    f_a = z[..., OFF_FOX_F:OFF_HG_Q] + b_f
    y_fox = forgetting_attention(q_a, k_a, v_a, f_a)

    hg_shape = (b, s, HGRN_HEADS, HGRN_EXPAND)
    hv_shape = (b, s, HGRN_HEADS, HGRN_DV)
    q_b = z[..., OFF_HG_Q:OFF_HG_F]
    f_b = z[..., OFF_HG_F:OFF_HG_I].astype(jnp.float32)
    i_b = z[..., OFF_HG_I:OFF_HG_G]
    g_b = z[..., OFF_HG_G:]
    log_f = jnp.logaddexp(jnp.log(lb), jnp.log1p(-lb) + jax.nn.log_sigmoid(f_b))
    k_b = (1.0 - lb) * jax.nn.sigmoid(-f_b)
    o_b = hgrn2_recurrence(q_b.reshape(hg_shape), k_b.reshape(hg_shape), i_b.reshape(hv_shape), log_f.reshape(hg_shape))
    o_b = rms_norm(o_b, g_o) * jax.nn.silu(g_b.reshape(hv_shape))
    y = jnp.concatenate([y_fox, o_b.reshape(b, s, D_HGRN)], axis=-1)
    return y @ w_out

def conv_ffn(h, w_up, conv_w, conv_b, w_down):
    s = h.shape[1]
    u = h @ w_up
    u_pad = jnp.pad(u, ((0, 0), (CONV_WIDTH_2 - 1, 0), (0, 0)))
    u = sum(conv_w[j] * u_pad[:, j:j + s] for j in range(CONV_WIDTH_2)) + conv_b
    gate, up = jnp.split(u, 2, axis=-1)
    return (jax.nn.silu(gate) * up) @ w_down

def second_inputs(seed: int = 0) -> dict:
    key = jax.random.key(seed)
    ks = jax.random.split(key, 20)
    f32 = jnp.float32

    def nrm(k, shape, fan_in):
        return jax.random.normal(k, shape, f32) * fan_in ** -0.5

    def gain(k, shape):
        return 1.0 + 0.01 * jax.random.normal(k, shape, f32)

    return {
        'x': jax.random.normal(ks[0], (BATCH, SEQ, D_MODEL), f32),
        'p': jax.random.normal(ks[1], (DEPTH, BATCH, SEQ, PLE_DIM), f32),
        'g_mix_pre': gain(ks[2], (DEPTH, D_MODEL)),
        'w_in': nrm(ks[3], (DEPTH, D_MODEL, N_IN), D_MODEL),
        'b_fox_f': jax.random.uniform(ks[4], (DEPTH, FOX_HEADS), f32, minval=1.0, maxval=4.0),
        'w_hgrn_lb': 0.1 * jax.random.normal(ks[5], (DEPTH, D_HGRN), f32),
        'g_hgrn_out': gain(ks[6], (DEPTH, HGRN_DV)),
        'w_out': nrm(ks[7], (DEPTH, D_MIX_2, D_MODEL), D_MIX_2),
        'g_mix_post': gain(ks[8], (DEPTH, D_MODEL)),
        'g_ffn_pre': gain(ks[9], (DEPTH, D_MODEL)),
        'w_up': nrm(ks[10], (DEPTH, D_MODEL, 2 * D_FF_2), D_MODEL),
        'conv_w': nrm(ks[11], (DEPTH, CONV_WIDTH_2, 2 * D_FF_2), CONV_WIDTH_2),
        'conv_b': 0.01 * jax.random.normal(ks[12], (DEPTH, 2 * D_FF_2), f32),
        'w_down': nrm(ks[13], (DEPTH, D_FF_2, D_MODEL), D_FF_2),
        'g_ffn_post': gain(ks[14], (DEPTH, D_MODEL)),
        'g_ple_in': gain(ks[15], (DEPTH, D_MODEL)),
        'w_ple_gate': nrm(ks[16], (DEPTH, D_MODEL, D_MODEL), D_MODEL),
        'w_ple_proj': nrm(ks[17], (DEPTH, PLE_DIM, D_MODEL), PLE_DIM),
        'g_ple_post': gain(ks[18], (DEPTH, D_MODEL)),
    }

def second_block(x, p, g_mix_pre, w_in, b_fox_f, w_hgrn_lb, g_hgrn_out, w_out, g_mix_post,
              g_ffn_pre, w_up, conv_w, conv_b, w_down, g_ffn_post,
              g_ple_in, w_ple_gate, w_ple_proj, g_ple_post):
    lbs = hgrn_lower_bounds(w_hgrn_lb)
    h = x
    for i in range(DEPTH):
        mix = token_mixer(rms_norm(h, g_mix_pre[i]), w_in[i], b_fox_f[i], lbs[i], g_hgrn_out[i], w_out[i])
        h = h + rms_norm(mix, g_mix_post[i])
        ff = conv_ffn(rms_norm(h, g_ffn_pre[i]), w_up[i], conv_w[i], conv_b[i], w_down[i])
        h = h + rms_norm(ff, g_ffn_post[i])
        e = p[i] @ w_ple_proj[i]
        gate = jax.nn.sigmoid(rms_norm(h, g_ple_in[i]) @ w_ple_gate[i])
        h = h + rms_norm(e * gate, g_ple_post[i])
    return h


def setup_inputs(seed=0):
    out = dict(first_inputs(seed))
    for name, value in second_inputs(seed + 1).items():
        if name != "x":
            out[name + "_2"] = value
    return out


def reference(
    x, attn_norm_w, w_in, conv_w, conv_b, dt_bias, a_log, d_skip, ssd_norm_w, cmp_w1_k,
    cmp_w2_k, cmp_w1_v, cmp_w2_v, cmp_pe_k, cmp_pe_v, w_out, ffn_norm_w, w_gate, w_up, w_down,
    final_norm_w, p_2, g_mix_pre_2, w_in_2, b_fox_f_2, w_hgrn_lb_2, g_hgrn_out_2, w_out_2,
    g_mix_post_2, g_ffn_pre_2, w_up_2, conv_w_2, conv_b_2, w_down_2, g_ffn_post_2, g_ple_in_2,
    w_ple_gate_2, w_ple_proj_2, g_ple_post_2,
):
    x = first_block(
        x, attn_norm_w, w_in, conv_w, conv_b, dt_bias, a_log, d_skip, ssd_norm_w, cmp_w1_k,
        cmp_w2_k, cmp_w1_v, cmp_w2_v, cmp_pe_k, cmp_pe_v, w_out, ffn_norm_w, w_gate, w_up,
        w_down, final_norm_w,
    )
    return second_block(
        x, p_2, g_mix_pre_2, w_in_2, b_fox_f_2, w_hgrn_lb_2, g_hgrn_out_2, w_out_2,
        g_mix_post_2, g_ffn_pre_2, w_up_2, conv_w_2, conv_b_2, w_down_2, g_ffn_post_2,
        g_ple_in_2, w_ple_gate_2, w_ple_proj_2, g_ple_post_2,
    )


_drawn_inputs = setup_inputs


def setup_inputs(seed=0):
    import zlib

    import numpy as np

    out = dict(_drawn_inputs(seed))
    spreads = {}
    factors = {'conv_b': 2.723,
     'cmp_pe_k': 8.0,
     'g_mix_pre_2': 2.698,
     'g_hgrn_out_2': 34.892,
     'g_mix_post_2': 32.732,
     'g_ffn_pre_2': 41.439,
     'conv_b_2': 40.329,
     'g_ffn_post_2': 187.303,
     'g_ple_in_2': 189.705,
     'g_ple_post_2': 200.0}
    for name, (base, spread) in spreads.items():
        noise = np.random.default_rng([zlib.crc32(name.encode()), seed]).standard_normal(out[name].shape)
        drawn = base * np.exp(spread * noise) if base else spread * noise
        out[name] = jnp.asarray(drawn.astype(out[name].dtype))
    for name, factor in factors.items():
        out[name] = (out[name] * factor).astype(out[name].dtype)
    return out
```

```python
from contextlib import ExitStack

import numpy as np

import concourse.bass as bass
from concourse import mybir

F32 = mybir.dt.float32
F32R = mybir.dt.float32r
U8 = mybir.dt.uint8
ALU = mybir.AluOpType
ACT = mybir.ActivationFunctionType
AX = mybir.AxisListType
ds = bass.ds

P = 128
TOK = 256
NT = TOK // P
D = 2048
KT = D // P
EPS = 1e-6
NEG = -1e30

SSD_W = 1024
SSD_H = 16
SSD_G = 2
CONV1 = 1536
CK1 = CONV1 // P
HD = 64
NH = 16
NKV = 4
CMP_BLOCK, CMP_STRIDE, CMP_HID = 32, 16, 256
NCMP = (TOK - CMP_BLOCK) // CMP_STRIDE + 1
ROPE_HALF = HD // 4 // 2
O_Z, O_XBC = 0, SSD_W
O_DT = O_XBC + CONV1
O_Q = O_DT + SSD_H
O_KC = O_Q + NH * HD
O_VC, O_KS, O_VS, O_KW, O_VW = (O_KC + i * NKV * HD for i in range(1, 6))
O_GATE = O_KC + 6 * NKV * HD
D_IN1 = O_GATE + 3 * NH
FF = 5632
FKT = FF // P
W2 = 1024
FH_N = 8
HG_N = 8
O2_K, O2_V, O2_F = W2, 2 * W2, 3 * W2
O2_HQ = O2_F + FH_N
O2_HF, O2_HI, O2_HG = (O2_HQ + i * W2 for i in range(1, 4))
D_IN2 = O2_HG + W2
PLE = 256

CW = 512
SK = 2
RING = 4
NFF = FF // CW

C_ID, C_TRI, C_TRI64, C_ZC, C_NEGT, C_CMP = 0, 128, 256, 384, 640, 768
C_COS = C_CMP + NT * NCMP
C_SIN = C_COS + NT * ROPE_HALF
C_BLK = C_SIN + NT * ROPE_HALF
C_N = C_BLK + 4
LEVELS = (64, 32, 16, 8, 4, 2, 1, 0)

V_ATTN, V_FFN, V_GMIX, V_GFFN, V_GPLE, V_SSD, V_CB = 0, 16, 32, 48, 64, 80, 88
V_CW, V_PEK, V_PEV, V_CW2, V_CB2 = 100, 148, 164, 180, 444
V_N = 532
B_DT, B_ALOG, B_DSK, B_BF, B_GO, B_N = 0, 16, 32, 48, 56, 184


def constants():
    c = np.zeros((P, C_N), np.float32)
    i = np.arange(P)
    c[:, C_ID:C_ID + P] = np.eye(P)
    le = i[:, None] <= i[None, :]
    c[:, C_TRI:C_TRI + P] = le
    c[:, C_TRI64:C_TRI64 + P] = le & (i[:, None] // 64 == i[None, :] // 64)
    c[:, C_ZC + P:C_ZC + 2 * P] = np.where(i[:, None] >= i[None, :], 0.0, NEG)
    c[:, C_NEGT:C_NEGT + P] = np.where(le, 0.0, NEG)
    inv = 1.0 / (np.float32(500000.0) ** (np.arange(0, 2 * ROPE_HALF, 2, dtype=np.float32) / np.float32(2 * ROPE_HALF)))
    for t in range(NT):
        pos = t * P + i
        end = np.arange(NCMP) * CMP_STRIDE + CMP_BLOCK - 1
        c[:, C_CMP + t * NCMP:C_CMP + (t + 1) * NCMP] = end[None, :] <= pos[:, None]
        ang = pos.astype(np.float32)[:, None] * inv[None, :].astype(np.float32)
        c[:, C_COS + t * ROPE_HALF:C_COS + (t + 1) * ROPE_HALF] = np.cos(ang)
        c[:, C_SIN + t * ROPE_HALF:C_SIN + (t + 1) * ROPE_HALF] = np.sin(ang)
    c[:, C_BLK:C_BLK + 4] = i[:, None] // 32 == np.arange(4)[None, :]
    m = np.zeros((P, len(LEVELS), P), np.float32)
    s, t = i[:, None], i[None, :]
    for n, b in enumerate(LEVELS):
        if b:
            m[:, n] = (s // (2 * b) == t // (2 * b)) & (s % (2 * b) < b) & (t % (2 * b) >= b)
        else:
            m[:, n] = s == t
    return c, m.reshape(P, len(LEVELS) * P)


def plan():
    full = lambda w, n: [(w, c * CW, CW) for c in range(n)]
    tail = lambda w, c0, n: [(w, c0, (n - c0) // 2), (w, c0 + (n - c0) // 2, (n - c0) // 2)]
    pairs = lambda a, b, off: [x for c in range(NFF) for x in ((a, c * CW, CW), (b, off + c * CW, CW))]
    table = [
        ("in1", full("w_in", 9) + tail("w_in", 9 * CW, D_IN1), KT),
        ("out1", full("w_out", 4), KT),
        ("ffn1", pairs("w_gate", "w_up", 0), KT),
        ("down1", full("w_down", 4), FKT),
        ("in2", full("w_in_2", 13) + tail("w_in_2", 13 * CW, D_IN2), KT),
        ("out2", full("w_out_2", 4), KT),
        ("ffn2", pairs("w_up_2", "w_up_2", FF), KT),
        ("down2", full("w_down_2", 4), FKT),
        ("proj", full("w_ple_proj_2", 4), PLE // P),
        ("ple", full("w_ple_gate_2", 4), KT),
    ]
    out, chunk, step = {}, 0, 0
    for name, chunks, kt in table:
        s = kt // SK
        out[name] = dict(chunks=chunks, S=s, C=chunk, N=step, end=step + s * len(chunks))
        chunk += len(chunks)
        step += s * len(chunks)
    widths = [c[2] for g in out.values() for c in g["chunks"] for _ in range(g["S"])]
    return out, widths


def two_blocks(nc, a, upto=99):
    G, WIDTH = plan()
    NSTEP = len(WIDTH)

    ctx = ExitStack()
    with ctx:
        def at(name, shape, dt, offset):
            size = int(np.prod(shape[1:])) * (1 if dt == U8 else 4)
            assert offset % 32 == 0 and offset + size <= nc.sbuf_usable_end, (name, offset + size)
            return nc.alloc_sbuf_tensor_at(name, shape, dt, offset=offset)

        STEP_B = SK * CW * 4
        o_ring = (nc.sbuf_base + 63) // 64 * 64
        raw = at("raw", [P, RING, SK * CW], F32, o_ring)
        whi = at("whi", [P, RING, SK * CW], F32R, o_ring + RING * STEP_B)
        wlo = at("wlo", [P, RING, SK * CW], F32R, o_ring + 2 * RING * STEP_B)
        o_h = o_ring + 3 * RING * STEP_B
        H = at("H", [P, NT, D], F32, o_h)
        o_a = o_h + NT * D * 4
        AH = at("AH", [P, KT, TOK], F32R, o_a)
        AL = at("AL", [P, KT, TOK], F32R, o_a + KT * TOK * 4)
        o_c = o_a + 2 * KT * TOK * 4
        C = at("C", [P, C_N], F32, o_c)
        o_c += (C_N * 4 + 31) // 32 * 32
        MK = at("MK", [P, len(LEVELS) * P], U8, o_c)
        o_c += len(LEVELS) * P
        VT = at("VT", [P, V_N], F32, o_c)
        o_c += (V_N * 4 + 31) // 32 * 32
        BV = at("BV", [P, B_N], F32, o_c)
        o_c += B_N * 4
        PIN = at("PIN", [P, NT, PLE], F32, o_c)
        o_c += NT * PLE * 4
        ONES = at("ONES", [P, P], F32, o_c)
        o_c += P * 4
        SM = at("SM", [P, 16], F32, o_c)
        o_c += 64
        EPSC = at("EPSC", [P, 8], F32, o_c)
        o_c += 32
        GP = at("GP", [P, D], F32, o_c)
        o_gp = o_c
        o_b = o_gp + D * 4

        XN = at("XN", [P, NT, D], F32, o_b)
        Z1 = at("Z1", [P, NT, D_IN1], F32, o_b)
        o_w = o_b + NT * D_IN1 * 4
        VR = at("VR", [P, 6, P], F32, o_w + 2 * 16384)
        W1K = at("W1K", [P, KT, CMP_HID], F32, o_w)
        W1V = at("W1V", [P, KT, CMP_HID], F32, o_w + 16384)
        XC = at("XC", [P, CK1, TOK], F32, o_w)
        XT = at("XT", [P, NT, SSD_W], F32, o_w + 12288)
        BT = at("BT", [P, SSD_G, P], F32, o_w + 20480)
        YOFF = at("YOFF", [P, SSD_W], F32, o_w + 21504)
        KSD = at("KSD", [P, 2, NT, NKV, 2, HD], F32, o_w)
        JUNK = at("JUNK", [P, NT, SSD_W], F32, o_w)
        YS = at("YS", [P, NT, SSD_W], F32, o_w + 2 * 16384)
        MF = at("MF", [P, len(LEVELS) * P], F32, o_w + 2 * 16384 + 8192)
        YA = at("YA", [P, NT, NH * HD], F32, o_w + 2 * 16384 + 8192)
        o_m = o_w + 2 * 16384 + 2 * 8192
        HK = at("HK", [P, 2, 60], F32, o_m)
        HV = at("HV", [P, 2, NKV, 4, 32], F32, o_a + 16384)
        KCT = at("KCT", [P, 60], F32, o_m + 512)
        W2K = at("W2K", [P, 2, 2, HD], F32, o_m + 768)
        W2V = at("W2V", [P, 2, HD], F32, o_m + 1792)
        BD = at("BD", [P, NKV, 4, HD], F32, o_w + 25600)
        SD = at("SD", [P, 16, 16], F32, o_w + 29696)
        AT = at("AT", [P, 256], F32, o_w + 30720)
        KFK = at("KFK", [P, KT, 60], F32, o_a)
        KFV = at("KFV", [P, KT, 60], F32, o_a + 3840)
        KVD = at("KVD", [P, 2, NT, NKV, 2, HD], F32, o_a + 8192)
        M = at("M", [P, NT, SSD_H, P], F32, o_a)
        XD = at("XD", [P, NT, SSD_W], F32, o_a + 16384)
        XS = at("XS", [P, SSD_W], F32, o_a + 24576)
        STA = at("STA", [P, SSD_G, CW], F32, o_a + 28672)
        QT = at("QT", [P, 8, TOK], F32, o_a)
        KTT = at("KTT", [P, 2, NKV, TOK], F32, o_a + 8192)
        S = at("S", [P, 2, 2, 2, TOK], F32, o_a + 16384)
        PT = at("PT", [P, 2, 2, 4, P], F32, o_a + 24576)
        SC = at("SC", [P, NT, NH, NCMP], F32, o_a + 16384)
        PC = at("PC", [P, NT, NH, 32], F32, o_a + 20480)
        PCT = at("PCT", [P, NT, NKV, P], F32, o_a + 24576)
        FH = at("FH", [P, FKT, TOK], F32R, o_b)
        FL = at("FL", [P, FKT, TOK], F32R, o_b + FKT * TOK * 4)
        SG = at("SG", [P, NT, CW], F32, o_gp)
        HT = at("HT", [P, NT, CW], F32, o_gp + 4096)
        UT = at("UT", [P, NT, CW], F32, o_gp)
        GC = at("GC", [P, 4, TOK], F32, o_gp + 4096)
        UC = at("UC", [P, 4, TOK], F32, o_b + 2 * FKT * TOK * 4)
        FO = at("FO", [P, NT, D], F32, o_a)
        Z2 = at("Z2", [P, NT, D_IN2], F32, o_b)
        o_y = o_b + NT * D_IN2 * 4
        YF = at("YF", [P, NT, W2], F32, o_y)
        YG = at("YG", [P, NT, W2], F32, o_y + 8192)
        o_t = o_y + 16384
        CB = at("CB", [P, FH_N, TOK], F32, o_a + 16384)
        KF2 = at("KF2", [P, FH_N, TOK], F32, o_a + 8192)
        SF = at("SF", [P, 2, 2, TOK], F32, o_t)
        PF = at("PF", [P, 2, 2, 2, P], F32, o_t + 4096)
        SF_ = at("SF_", [P, 128], F32, o_t + 8192)
        CUM = at("CUM", [P, HG_N * TOK], F32, o_a)
        HQ = at("HQ", [P, HG_N, TOK], F32, o_a + 8192)
        HKT = at("HKT", [P, HG_N, TOK], F32, o_a + 16384)
        LG0 = at("LG0", [P, HG_N * TOK], F32, o_a + 24576)
        LG1 = at("LG1", [P, HG_N * TOK], F32, o_t + 12288)
        LG = [LG0, LG1]
        HS = at("HS", [P, NT, HG_N, P], F32, o_t)
        HX = at("HX", [P, HG_N, P], F32, o_t + 8192)
        HN = at("HN", [P, 64], F32, o_t + 20480)
        MIX = at("MIX", [P, NT, D], F32, o_b)
        E = at("E", [P, NT, D], F32, o_b + 16384)
        PH = at("PH", [P, 2, TOK], F32R, o_b + 32768)
        PL = at("PL", [P, 2, TOK], F32R, o_b + 32768 + 2048)
        GS = at("GS", [P, NT, CW], F32, o_b + 32768 + 4096)

        pg = ctx.enter_context(nc.psum_tensor("pg", [P, 4, CW], F32))
        pt = ctx.enter_context(nc.psum_tensor("pt", [P, 4, CW], F32))

        def sem(name):
            return ctx.enter_context(nc.semaphore(name))

        raw_landed = [sem(f"raw_landed{i}") for i in range(RING)]
        hi_ready, lo_ready, step_used = sem("hi_ready"), sem("lo_ready"), sem("step_used")
        chunk_out = [sem("chunk_out0"), sem("chunk_out1")]
        dve_chain, act_chain = sem("dve_chain"), sem("act_chain")
        x_landed, const_landed, vec_landed = sem("x_landed"), sem("const_landed"), sem("vec_landed")
        bc_landed, cmpw_landed, gain_landed = sem("bc_landed"), sem("cmpw_landed"), sem("gain_landed")
        gain_used, out_landed = sem("gain_used"), sem("out_landed")
        consts_set, vec_turned, vec_ready = sem("consts_set"), sem("vec_turned"), sem("vec_ready")
        ss0, ss1, root, rstd_ready = sem("ss0"), sem("ss1"), sem("root"), sem("rstd_ready")
        xn0, xn1 = sem("xn0"), sem("xn1")
        turned, a_hi, a_lo = sem("turned"), sem("a_hi"), sem("a_lo")
        h_ready = sem("h_ready")
        kv_twice, k_twice = sem("kv_twice"), sem("k_twice")
        kc_turned, kflat, hid_sum, hid_act = sem("kc_turned"), sem("kflat"), sem("hid_sum"), sem("hid_act")
        cmp_sum, cmp_kv = sem("cmp_sum"), sem("cmp_kv")
        cv_turned, cv_first, cv_sum, cv_act = sem("cv_turned"), sem("cv_first"), sem("cv_sum"), sem("cv_act")
        xt_turned, xt_a, xt_d = sem("xt_turned"), sem("xt_a"), sem("xt_d")
        dt_exp, dt_u, dt_ln, alog_exp, adt_ready = sem("dt_exp"), sem("dt_u"), sem("dt_ln"), sem("alog_exp"), sem("adt_ready")
        acum_sum, acum_ready, decay_col = sem("acum_sum"), sem("acum_ready"), sem("decay_col")
        row_sum, seg_ready, seg_exp = sem("row_sum"), sem("seg_ready"), sem("seg_exp")
        cb_sum, m_ready, xs_ready = sem("cb_sum"), sem("m_ready"), sem("xs_ready")
        yd_sum, st_sum, st_ready, yo_sum, z_silu, ys_ready = (
            sem("yd_sum"), sem("st_sum"), sem("st_ready"), sem("yo_sum"), sem("z_silu"), sem("ys_ready"))
        q_turned, q_out, cs_sum, cs_ready, cs_exp = sem("q_turned"), sem("q_out"), sem("cs_sum"), sem("cs_ready"), sem("cs_exp")
        pc_ready, pc_turned, pct_ready, oc_sum, oc_out = sem("pc_ready"), sem("pc_turned"), sem("pct_ready"), sem("oc_sum"), sem("oc_out")
        gates, roped, k_turned, k_out = sem("gates"), sem("roped"), sem("k_turned"), sem("k_out")
        s_sum, s_masked, s_max, s_exp = sem("s_sum"), sem("s_masked"), sem("s_max"), sem("s_exp")
        p_turned, p_out0, p_out1, o_sum, o_out = sem("p_turned"), sem("p_out0"), sem("p_out1"), sem("o_sum"), sem("o_out")
        f_turned, f_hi, f_lo = sem("f_turned"), sem("f_hi"), sem("f_lo")
        c_turned, c_first, c_part, c_sum, c_silu, c_prod = (
            sem("c_turned"), sem("c_first"), sem("c_part"), sem("c_sum"), sem("c_silu"), sem("c_prod"))
        lf_exp, lf_ln, lf_ready = sem("lf_exp"), sem("lf_ln"), sem("lf_ready")
        fq_turned, fq_out, fk_out, fc_sum, fc_out = sem("fq_turned"), sem("fq_out"), sem("fk_out"), sem("fc_sum"), sem("fc_out")
        fs_sum, fs_ready, fs_max, fs_exp = sem("fs_sum"), sem("fs_ready"), sem("fs_max"), sem("fs_exp")
        fp_turned, fp_out, fo_sum, fo_out = sem("fp_turned"), sem("fp_out"), sem("fo_sum"), sem("fo_out")
        hg_ln, hg_sig, hg_lf = sem("hg_ln"), sem("hg_sig"), sem("hg_lf")
        hc_sum, hc_out, hq_turned, hq_out, hk_turned, hk_out = (
            sem("hc_sum"), sem("hc_out"), sem("hq_turned"), sem("hq_out"), sem("hk_turned"), sem("hk_out"))
        lv_diff, lv_exp, lv_mul, lv_sum, lv_out = sem("lv_diff"), sem("lv_exp"), sem("lv_mul"), sem("lv_sum"), sem("lv_out")
        ho_sum, ho_out, hg_silu, yg_ready, hn_sq, hn_root = (
            sem("ho_sum"), sem("ho_out"), sem("hg_silu"), sem("yg_ready"), sem("hn_sq"), sem("hn_root"))
        p_tr, p_hi, p_lo, g_sig, e_ready = sem("p_tr"), sem("p_hi"), sem("p_lo"), sem("g_sig"), sem("e_ready")

        ident = C[:, C_ID:C_ID + P]
        tri = C[:, C_TRI:C_TRI + P]
        tri64 = C[:, C_TRI64:C_TRI64 + P]

        def bank4(n):
            return pt[:, n, :].rearrange("p (b c) -> p b c", c=P)

        def bc(ap, *shape):
            return ap.to_broadcast([P, *shape])

        def chunks_read(eng, n):
            for t in range(NT):
                eng.wait_ge(chunk_out[t], n)

        def lv_units(l):
            return 1 + 2 * l

        def lv_banks(u):
            src = (pg, pt)[(u // 2) % 2]
            b = 2 * (u % 2)
            return src[:, b:b + 2, :].rearrange("p b (h n) -> p (b h) n", n=P)

        block = ctx.enter_context(nc.Block())

        @block.sync
        def _(sp):
            def load(dst, src, s):
                sp.dma_start(dst, src).then_inc(s, 16)

            load(H[:], a["x"][0].rearrange("(t p) d -> p t d", p=P), x_landed)
            load(C[:], a["consts"], const_landed)
            load(MF[:], a["masks"], const_landed)
            rows = lambda w, r: w.rearrange("(r p) -> r p", p=P)
            r0 = 0
            for w in ("attn_norm_w", "ffn_norm_w", "g_mix_pre_2", "g_ffn_pre_2", "g_ple_in_2", "ssd_norm_w", "conv_b"):
                n = a[w].shape[-1] // P
                load(VR[r0:r0 + n, 0, :], rows(a[w][0], n), vec_landed)
                r0 += n
            load(VR[0:48, 1, :], a["conv_w"][0].rearrange("j (r p) -> (j r) p", p=P), vec_landed)
            load(VR[48:64, 1, :], a["cmp_pe_k"][0].rearrange("(t l) d -> t (l d)", l=2), vec_landed)
            load(VR[64:80, 1, :], a["cmp_pe_v"][0].rearrange("(t l) d -> t (l d)", l=2), vec_landed)
            for j in range(3):
                load(VR[0:88, 2 + j, :], rows(a["conv_w_2"][0, j], 88), vec_landed)
            load(VR[0:88, 5, :], rows(a["conv_b_2"][0], 88), vec_landed)

            def chunk(w, c0, width, j0, j1, s, d):
                for j in range(j0, j1):
                    n = s + j
                    if n >= RING:
                        sp.wait_ge(lo_ready, n - RING + 1 + d)
                    src = a[w][0, j * SK * P:(j + 1) * SK * P, ds(c0, width)].rearrange("(k p) n -> p k n", p=P)
                    dst = raw[:, n % RING, 0:SK * width].rearrange("p (k n) -> p k n", k=SK)
                    load(dst, src, raw_landed[n % RING])

            for name, g in G.items():
                ch, S_, N = g["chunks"], g["S"], g["N"]
                if name in ("ffn1", "ffn2"):
                    (wa, ca, _), (wb, cb, _) = ch[0], ch[1]
                    with sp.Fori(0, NFF) as i:
                        chunk(wa, i * CW + ca, CW, 0, S_, N, i * (2 * S_))
                        chunk(wb, i * CW + cb, CW, 0, S_, N + S_, i * (2 * S_))
                elif name in ("in1", "in2"):
                    n = len(ch) - 2
                    chunk(ch[0][0], 0, CW, 0, S_, N, 0)
                    with sp.Fori(0, n - 1) as i:
                        chunk(ch[0][0], i * CW + CW, CW, 0, S_, N + S_, i * S_)
                    for c in (n, n + 1):
                        chunk(*ch[c], 0, S_, N + c * S_, 0)
                elif S_ == FKT // SK:
                    with sp.Fori(0, 2) as i:
                        chunk(ch[0][0], i * (2 * CW), CW, 0, S_, N, i * (2 * S_))
                        chunk(ch[0][0], i * (2 * CW) + CW, CW, 0, S_, N + S_, i * (2 * S_))
                elif S_ % RING == 0:
                    with sp.Fori(0, len(ch)) as i:
                        chunk(ch[0][0], i * CW, CW, 0, S_, N, i * S_)
                else:
                    for c in range(len(ch)):
                        chunk(*ch[c], 0, S_, N + c * S_, 0)
            if upto >= 99:
                sp.wait_ge(h_ready, 10)
                load(a["out"][0].rearrange("(t p) d -> p t d", p=P), H[:], out_landed)
                sp.wait_ge(out_landed, 16)

        @block.gpsimd
        def _(pool):
            def load(dst, src, s):
                pool.dma_start(dst, src).then_inc(s, 16)

            pool.memset(ONES[:], 1.0).then_inc(consts_set, 1)
            pool.memset(EPSC[:], EPS).then_inc(consts_set, 1)
            pool.wait_ge(const_landed, 32)
            pool.tensor_copy(MK[:], MF[:]).then_inc(consts_set, 1)
            load(PIN[:], a["p_2"][0, 0].rearrange("(t p) d -> p t d", p=P), bc_landed)
            for w, o in (("dt_bias", B_DT), ("a_log", B_ALOG), ("d_skip", B_DSK), ("b_fox_f_2", B_BF), ("g_hgrn_out_2", B_GO)):
                n = a[w].shape[-1]
                load(BV[:, o:o + n], a[w][0].partition_broadcast(P), bc_landed)
            load(W1K[:], a["cmp_w1_k"][0].rearrange("(k p) n -> p k n", p=P), cmpw_landed)
            load(W1V[:], a["cmp_w1_v"][0].rearrange("(k p) n -> p k n", p=P), cmpw_landed)
            for i in range(2):
                load(W2K[:, :, i, :], a["cmp_w2_k"][0].rearrange("(k p) n -> p k n", p=P), cmpw_landed)
            load(W2V[:], a["cmp_w2_v"][0].rearrange("(k p) n -> p k n", p=P), cmpw_landed)
            def twice(dst, c0):
                for t in range(NT):
                    for h in range(NKV):
                        src = Z1[:, t, c0 + h * HD:c0 + (h + 1) * HD].unsqueeze(1).to_broadcast([P, 2, HD])
                        ins = pool.tensor_copy(dst[:, t, h], src)
                return ins

            if upto >= 2:
                chunks_read(pool, G["out1"]["C"])
                twice(KVD[:, 0], O_KC)
                twice(KVD[:, 1], O_VC).then_inc(kv_twice, 1)
            if upto >= 4:
                pool.wait_ge(roped, 1)
                twice(KSD[:, 0], O_KS)
                twice(KSD[:, 1], O_KW).then_inc(k_twice, 1)
            if upto >= 10:
                pool.wait_ge(f_lo, NFF)
                load(GP[:], a["final_norm_w"].partition_broadcast(P), gain_landed)
                pool.wait_ge(h_ready, 3)
                load(GP[:], a["g_mix_post_2"][0].partition_broadcast(P), gain_landed)
            if upto >= 18:
                pool.wait_ge(f_lo, 2 * NFF)
                load(GP[:], a["g_ffn_post_2"][0].partition_broadcast(P), gain_landed)
                pool.wait_ge(h_ready, 8)
                load(GP[:], a["g_ple_post_2"][0].partition_broadcast(P), gain_landed)

        @block.scalar
        def _(act):
            A = nc.scalar.activation
            chain = [0]

            def link(ins):
                chain[0] += 1
                ins.then_inc(act_chain, 1)
                act.wait_ge(act_chain, chain[0])

            def split(n, d=0, w=None):
                if n >= NSTEP:
                    return
                w = SK * (w or WIDTH[n])
                act.wait_ge(raw_landed[n % RING], 16 * (n // RING + 1) + d * (16 // RING))
                if n >= RING:
                    act.wait_ge(step_used, n - RING + 1 + d)
                A(whi[:, n % RING, 0:w], raw[:, n % RING, 0:w], ACT.Copy).then_inc(hi_ready, 1)

            def stream(g, evac):
                S_, N, n = g["S"], g["N"], len(g["chunks"])

                def one(c, dc, dn):
                    for j in range(S_):
                        split(N + c * S_ + RING + j, dn)
                    evac(c, dc, N + (c + 1) * S_ + dn)

                loops = uniform_pairs(g)
                if loops > 1:
                    with act.Fori(0, loops) as i:
                        for c in range(2):
                            one(c, i * 2, i * (2 * S_))
                    done = 2 * loops
                else:
                    done = 0
                for c in range(done, n):
                    one(c, 0, 0)

            def evac_copy(dst, g):
                def f(c, dc, used):
                    b = 2 * ((g["C"] + c) % 2)
                    w = g["chunks"][c][2]
                    act.wait_ge(step_used, used)
                    A(dst[:, 0, ds(dc * CW + g["chunks"][c][1], w)], pg[:, b, 0:w], ACT.Copy).then_inc(chunk_out[0], 1)
                return f

            def norm(i, src, n, junk, dst):
                link(A(junk, src, ACT.Square, accum_out=SM[:, 0:1]))
                act.wait_ge(ss1, i + 1)
                A(SM[:, 2:4], SM[:, 0:2], ACT.Sqrt, scale=1.0 / n, bias=EPSC[:, 0:1]).then_inc(root, 1)
                if dst is not None:
                    act.wait_ge(rstd_ready, i + 1)
                    A(dst, src, ACT.Copy, scale=SM[:, 4:5]).then_inc(xn0, 1)

            def prep(p, cols):
                for g in range(KT // 2):
                    act.wait_ge(turned, p * 8 + g + 1)
                    src = pt[:, g % 4, :].rearrange("p (k n) -> p k n", k=2)
                    for k in range(2):
                        kt = 2 * g + k
                        w = cols(kt)
                        sc = 1.0 if w is None else VT[:, w:w + 1]
                        ins = A(AH[:, kt, :], src[:, k, :], ACT.Copy, scale=sc)
                    ins.then_inc(a_hi, 1)

            def cmp_tokens():
                act.wait_ge(hid_sum, 1)
                hid = pg[:, 0, 0:256].rearrange("p (b c) -> p b c", c=64)
                A(HK[:], hid[:, 0:2, 0:60], ACT.Silu).then_inc(hid_act, 1)
                act.wait_ge(kflat, 1)
                for m in range(2):
                    for h in range(NKV):
                        x = hid[:, 2 + m, h * NCMP:(h + 1) * NCMP].unsqueeze(1).to_broadcast([P, 4, NCMP])
                        ins = A(HV[:, m, h, :, 0:NCMP], x, ACT.Silu)
                ins.then_inc(hid_act, 1)
                act.wait_ge(cmp_sum, 1)
                A(KCT[:], pg[:, 1, 0:60], ACT.Copy).then_inc(cmp_kv, 1)

            def ssd():
                act.wait_ge(cmp_kv, 5)
                def silu(g):
                    act.wait_ge(cv_sum, g + 1)
                    A(XC[:, 2 * g:2 * g + 2, :], XC[:, 2 * g:2 * g + 2, :], ACT.Silu).then_inc(cv_act, 1)

                for g in range(CK1 // 2):
                    act.wait_ge(cv_turned, g + 1)
                    for k in range(2):
                        kt = 2 * g + k
                        ins = A(XC[:, kt, :], pt[:, g % 4, k * TOK:(k + 1) * TOK], ACT.Identity,
                                bias=VT[:, V_CB + kt:V_CB + kt + 1], scale=VT[:, V_CW + 3 * CK1 + kt:V_CW + 3 * CK1 + kt + 1])
                    ins.then_inc(cv_first, 1)
                    if g:
                        silu(g - 1)
                silu(CK1 // 2 - 1)
                A(Z1[:, :, O_Z:O_Z + SSD_W], Z1[:, :, O_Z:O_Z + SSD_W], ACT.Silu).then_inc(z_silu, 1)
                act.wait_ge(xt_turned, 1)
                for b in range(2):
                    ins = A(XT[:, 0, b * CW:(b + 1) * CW], pg[:, b, :], ACT.Copy)
                ins.then_inc(xt_a, 1)
                act.wait_ge(dt_u, 1)
                A(SD[:, 2:4, :], SD[:, 2:4, :], ACT.Exp, scale=-1.0).then_inc(dt_exp, 1)
                A(SD[:, 14, :], BV[:, B_ALOG:B_ALOG + 16], ACT.Exp).then_inc(alog_exp, 1)
                act.wait_ge(dt_u, 2)
                A(SD[:, 6:8, :], SD[:, 4:6, :], ACT.Ln).then_inc(dt_ln, 1)
                act.wait_ge(acum_ready, 1)
                A(SD[:, 11:13, :], SD[:, 11:13, :], ACT.Exp).then_inc(decay_col, 1)
                for t in range(NT):
                    act.wait_ge(seg_ready, t + 1)
                    A(M[:, t, :, :], M[:, t, :, :], ACT.Exp).then_inc(seg_exp, 1)
                act.wait_ge(st_sum, 1)
                A(STA[:], pg[:, 0:2, :], ACT.Copy).then_inc(st_ready, 1)
                act.wait_ge(ys_ready, 1)
                norm(1, YS[:, 0, :], SSD_W, JUNK[:, 0, :], YS[:, 0, :])

            def nsa():
                A(AT[:, 0:96].rearrange("p (t g) -> p t g", t=2), Z1[:, :, O_GATE:O_GATE + 48], ACT.Sigmoid).then_inc(gates, 1)
                act.wait_ge(q_turned, 1)
                A(QT[:, 0:4, :], pt[:, 0:2, :].rearrange("p b (c n) -> p (b c) n", n=TOK), ACT.Copy).then_inc(q_out, 1)
                act.wait_ge(cs_ready, 1)
                A(SC[:], SC[:], ACT.Exp).then_inc(cs_exp, 1)
                act.wait_ge(pc_turned, 1)
                A(PCT[:, 0], bank4(0), ACT.Copy).then_inc(pct_ready, 1)
                act.wait_ge(oc_sum, 1)
                A(YA[:, 0, :].rearrange("p (b n) -> p b n", b=2), pg[:, 2:4, :], ACT.Copy).then_inc(oc_out, 1)
                act.wait_ge(q_turned, 2)
                A(QT[:, 0:4, :], pg[:, 0:2, :].rearrange("p b (c n) -> p (b c) n", n=TOK), ACT.Copy).then_inc(q_out, 1)
                act.wait_ge(k_turned, 1)
                A(KTT[:, 0, :, :], pt[:, 0:2, :].rearrange("p b (c n) -> p (b c) n", n=TOK), ACT.Copy).then_inc(k_out, 1)
                for u in range(17):
                    if u < 16:
                        nk = P * (1 + units[u][1])
                        act.wait_ge(s_max, u + 1)
                        for j in range(4):
                            x = S[:, u % 2, j // 2, j % 2, 0:nk]
                            ins = A(x, x, ACT.Exp, bias=NM[:, 4 * u + j:4 * u + j + 1], scale=HD ** -0.5,
                                    accum_out=SUM[:, 4 * u + j:4 * u + j + 1])
                        ins.then_inc(s_exp, 1)
                    if u >= 1:
                        act.wait_ge(p_turned, u)
                        if u >= 3:
                            act.wait_ge(o_sum, u - 2)
                        A(PT[:, (u - 1) % 2, 0], bank4(0), ACT.Copy).then_inc(p_out0, 1)

            units = [(b, t, kv) for b in range(2) for t in range(NT) for kv in range(NKV)]
            NM = AT[:, 96:160]
            SUM = AT[:, 160:224]

            def ffn(g, hooks):
                N, S_ = g["N"], g["S"]

                def pair(c, d):
                    for h in range(4):
                        hooks[h](c, d)
                        for j in range(4):
                            split(N + c * 16 + 4 * (h + 1) + j, d * 16, CW)

                pair(0, 0)
                with act.Fori(0, NFF - 1) as i:
                    pair(1, i)

            def down(g, hooks, evac):
                N, S_, n = g["N"], g["S"], len(g["chunks"])
                for c in range(n):
                    for j in range(S_):
                        if c == 0 and j % 4 == 0 and j // 4 < len(hooks):
                            hooks[j // 4]()
                        split(N + c * S_ + RING + j)
                    evac(c, 0, N + (c + 1) * S_)

            F1, F2 = G["ffn1"], G["ffn2"]

            def f1_hi(c, d):
                act.wait_ge(f_turned, c + d)
                A(FH[:, ds((d + c - 1) * 4, 4), :], pt[:, 0:2, :].rearrange("p b (c n) -> p (b c) n", n=TOK), ACT.Copy)\
                    .then_inc(f_hi, 1)

            def f1_silu(c, d):
                b = 2 * (F1["C"] % 2)
                act.wait_ge(step_used, F1["N"] + 16 * c + 8 + d * 16)
                if c:
                    chunks_read(act, F1["C"] + 2 * c + d * 2)
                for t in range(NT):
                    A(SG[:, t, :], pg[:, b + t, :], ACT.Silu).then_inc(chunk_out[t], 1)

            no = lambda *_: None

            def f2_up(c, d):
                b = 2 * ((F2["C"] + 1) % 2)
                act.wait_ge(step_used, F2["N"] + 16 * c + d * 16)
                act.wait_ge(c_turned, 2 * c - 1 + d * 2)
                A(UT[:, 0, :], pg[:, b, :], ACT.Copy).then_inc(chunk_out[0], 1)
                act.wait_ge(c_sum, 2 * c - 1 + d * 2)
                A(GC[:], GC[:], ACT.Silu).then_inc(c_silu, 1)

            def conv_first(src, dst, k0):
                for k in range(4):
                    ins = A(dst[:, k, :], src[:, k, :], ACT.Identity, bias=VT[:, ds(k0 + V_CB2 + k, 1)],
                            scale=VT[:, ds(k0 + V_CW2 + 2 * 88 + k, 1)])
                ins.then_inc(c_first, 1)

            def f2_conv_up(c, d):
                act.wait_ge(c_turned, 2 * c + d * 2)
                conv_first(pt[:, 2:4, :].rearrange("p b (c n) -> p (b c) n", n=TOK), UC, d * 4 + (c - 1) * 4 + FKT)

            def f2_gate(c, d):
                b = 2 * (F2["C"] % 2)
                act.wait_ge(step_used, F2["N"] + 16 * c + 8 + d * 16)
                if c:
                    act.wait_ge(c_turned, 2 * c + d * 2)
                A(UT[:, 0, :], pg[:, b, :], ACT.Copy).then_inc(chunk_out[0], 1)

            def f2_hi(c, d):
                act.wait_ge(c_prod, c + d)
                A(FH[:, ds((d + c - 1) * 4, 4), :], UC[:], ACT.Copy).then_inc(f_hi, 1)

            def f2_conv_gate(c, d):
                act.wait_ge(c_turned, 2 * c + 1 + d * 2)
                if c:
                    act.wait_ge(c_prod, c + d)
                conv_first(pt[:, 0:2, :].rearrange("p b (c n) -> p (b c) n", n=TOK), GC, d * 4 + c * 4)

            def after(f):
                return lambda c, d: f(c, d) if c else None

            def fox():
                act.wait_ge(lf_ready, 1)
                A(SF_[:, 16:32], SF_[:, 16:32], ACT.Exp, scale=-1.0).then_inc(lf_exp, 1)
                act.wait_ge(lf_exp, 1)
                A(SF_[:, 16:32], SF_[:, 16:32], ACT.Ln, bias=1.0).then_inc(lf_ln, 1)
                act.wait_ge(fq_turned, 1)
                A(QT[:], pt[:].rearrange("p b (c n) -> p (b c) n", n=TOK), ACT.Copy).then_inc(fq_out, 1)
                act.wait_ge(fc_sum, 1)
                A(CB[:], pt[:].rearrange("p b (c n) -> p (b c) n", n=TOK), ACT.Copy, scale=-1.0).then_inc(fc_out, 1)
                for u in range(9):
                    if u < 8:
                        nk = P * (1 + u // 4)
                        act.wait_ge(fs_max, u + 1)
                        for j in range(2):
                            x = SF[:, u % 2, j, 0:nk]
                            ins = A(x, x, ACT.Exp, bias=SF_[:, 64 + 2 * u + j:65 + 2 * u + j], scale=1.0,
                                    accum_out=SF_[:, 80 + 2 * u + j:81 + 2 * u + j])
                        ins.then_inc(fs_exp, 1)
                    if u >= 1:
                        t = (u - 1) // 4
                        act.wait_ge(fp_turned, u)
                        if u >= 3:
                            act.wait_ge(fo_sum, u - 2)
                        A(PF[:, (u - 1) % 2, :, 0:t + 1, :],
                          bank4((u - 1) % 2).rearrange("p (j k) n -> p j k n", j=2)[:, :, 0:t + 1, :], ACT.Copy).then_inc(fp_out, 1)

            def hgrn():
                f = Z2[:, :, O2_HF:O2_HF + W2]
                act.wait_ge(fo_out, 8)
                A(YG[:], f, ACT.Sigmoid, scale=-1.0).then_inc(hg_sig, 1)
                tmp = LG1[:].rearrange("p (t n) -> p t n", t=2)
                link(A(tmp, f, ACT.Abs))
                link(A(tmp, tmp, ACT.Exp, scale=-1.0))
                A(tmp, tmp, ACT.Ln, bias=1.0).then_inc(hg_ln, 1)
                A(Z2[:, :, O2_HG:O2_HG + W2], Z2[:, :, O2_HG:O2_HG + W2], ACT.Silu).then_inc(hg_silu, 1)
                act.wait_ge(hk_turned, 1)
                A(HKT[:], pt[:].rearrange("p b (c n) -> p (b c) n", n=TOK), ACT.Copy).then_inc(hk_out, 1)
                act.wait_ge(hc_sum, 1)
                A(CUM[:].rearrange("p (b n) -> p b n", b=4), pt[:], ACT.Copy).then_inc(hc_out, 1)
                for l in range(8):
                    act.wait_ge(lv_diff, l + 1)
                    if l == 0:
                        q2 = lambda x: x[:].rearrange("p (h a n) -> p h a n", h=8, a=4)[:, :, 2, :]
                        A(q2(LG0), q2(CUM), ACT.Exp)
                        x = LG0[:].rearrange("p (h a n) -> p h a n", h=8, a=4)
                        A(x[:, :, 0:2, :], x[:, :, 0:2, :], ACT.Exp)
                        A(x[:, :, 3, :], x[:, :, 3, :], ACT.Exp).then_inc(lv_exp, 1)
                    elif l == 1:
                        x = LG1[:].rearrange("p (h t a n) -> p (h t) a n", h=8, t=2, a=2)
                        y = CUM[:].rearrange("p (h t a n) -> p (h t) a n", h=8, t=2, a=2)
                        A(x[:, :, 0, :], x[:, :, 0, :], ACT.Exp)
                        A(x[:, :, 1, :], y[:, :, 1, :], ACT.Exp).then_inc(lv_exp, 1)
                    else:
                        A(LG[l % 2][:], LG[l % 2][:], ACT.Exp).then_inc(lv_exp, 1)
                act.wait_ge(ho_sum, 1)
                A(YG[:], pt[:].rearrange("p (t b) n -> p t (b n)", t=2), ACT.Copy).then_inc(ho_out, 1)
                act.wait_ge(hn_sq, 1)
                A(HN[:, 16:32], HN[:, 0:16], ACT.Sqrt, scale=1.0 / P, bias=EPSC[:, 0:1]).then_inc(hn_root, 1)

            for n in range(RING):
                split(n)
            act.wait_ge(consts_set, 2)
            act.wait_ge(x_landed, 16)
            norm(0, H[:, 0, :], D, XN[:, 0, :], XN[:, 0, :])
            act.wait_ge(vec_ready, 2)
            prep(0, lambda k: V_ATTN + k)
            stream(G["in1"], evac_copy(Z1, G["in1"]))
            if upto < 2: return
            chunks_read(act, G["out1"]["C"])
            cmp_tokens()
            if upto < 3: return
            act.wait_ge(bc_landed, 96)
            ssd()
            if upto < 4: return
            nsa()
            if upto < 5: return
            act.wait_ge(step_used, G["in1"]["end"])
            act.wait_ge(o_out, 16)
            prep(1, lambda k: V_SSD + k if k < 8 else None)
            stream(G["out1"], no)
            act.wait_ge(h_ready, 1)
            norm(2, H[:, 0, :], D, XN[:, 0, :], XN[:, 0, :])
            act.wait_ge(step_used, G["out1"]["end"])
            prep(2, lambda k: V_FFN + k)
            if upto < 8: return
            ffn(F1, [no, after(f1_hi), f1_silu, no])
            if upto < 9: return
            down(G["down1"], [no, lambda: f1_hi(NFF, 0)], no)
            act.wait_ge(h_ready, 2)
            norm(3, H[:, 0, :], D, XN[:, 0, :], None)
            if upto < 10: return
            act.wait_ge(h_ready, 3)
            norm(4, H[:, 0, :], D, XN[:, 0, :], XN[:, 0, :])
            prep(3, lambda k: V_GMIX + k)
            stream(G["in2"], evac_copy(Z2, G["in2"]))
            if upto < 12: return
            chunks_read(act, G["out2"]["C"])
            fox()
            if upto < 13: return
            hgrn()
            if upto < 14: return
            act.wait_ge(step_used, G["in2"]["end"])
            act.wait_ge(yg_ready, 1)
            prep(4, lambda k: None)
            stream(G["out2"], evac_copy(MIX, G["out2"]))
            chunks_read(act, G["ffn2"]["C"])
            norm(5, MIX[:, 0, :], D, E[:, 0, :], None)
            act.wait_ge(h_ready, 6)
            norm(6, H[:, 0, :], D, XN[:, 0, :], XN[:, 0, :])
            prep(5, lambda k: V_GFFN + k)
            if upto < 17: return
            ffn(F2, [after(f2_up), after(f2_conv_up), lambda c, d: (f2_gate(c, d), after(f2_hi)(c, d)), f2_conv_gate])
            down(G["down2"], [lambda: f2_up(NFF, 0), lambda: f2_conv_up(NFF, 0), no, lambda: f2_hi(NFF, 0)],
                 evac_copy(FO, G["down2"]))
            if upto < 18: return
            chunks_read(act, G["proj"]["C"])
            norm(7, FO[:, 0, :], D, E[:, 0, :], None)
            act.wait_ge(h_ready, 8)
            norm(8, H[:, 0, :], D, XN[:, 0, :], XN[:, 0, :])
            act.wait_ge(p_tr, 1)
            A(PH[:], pt[:, 3, :].rearrange("p (k n) -> p k n", k=2), ACT.Copy).then_inc(p_hi, 1)
            prep(6, lambda k: V_GPLE + k)
            stream(G["proj"], evac_copy(E, G["proj"]))

            def ple_gate(c, dc, used):
                g = G["ple"]
                b = 2 * ((g["C"] + c) % 2)
                act.wait_ge(step_used, used)
                if c:
                    act.wait_ge(e_ready, 2 * c + dc * 2)
                for t in range(NT):
                    A(GS[:, t, :], pg[:, b + t, :], ACT.Sigmoid).then_inc(chunk_out[t], 1)

            for c in range(4):
                for j in range(8):
                    split(G["ple"]["N"] + c * 8 + RING + j)
                ple_gate(c, 0, G["ple"]["N"] + (c + 1) * 8)
            act.wait_ge(e_ready, 8)
            norm(9, E[:, 0, :], D, XN[:, 0, :], None)

        @block.vector
        def _(dve):
            V = nc.vector
            chain = [0]

            def link(ins):
                chain[0] += 1
                ins.then_inc(dve_chain, 1)
                dve.wait_ge(dve_chain, chain[0])

            def split(n, d=0, w=None):
                if n >= NSTEP:
                    return
                w = SK * (w or WIDTH[n])
                dve.wait_ge(hi_ready, n + 1 + d)
                V.tensor_tensor(wlo[:, n % RING, 0:w], raw[:, n % RING, 0:w], whi[:, n % RING, 0:w].bitcast(F32),
                                ALU.subtract).then_inc(lo_ready, 1)

            def stream(g, evac):
                S_, N, n = g["S"], g["N"], len(g["chunks"])

                def one(c, dc, dn):
                    for j in range(S_):
                        split(N + c * S_ + RING + j, dn)
                    evac(c, dc, N + (c + 1) * S_ + dn)

                loops = uniform_pairs(g)
                if loops > 1:
                    with dve.Fori(0, loops) as i:
                        for c in range(2):
                            one(c, i * 2, i * (2 * S_))
                    done = 2 * loops
                else:
                    done = 0
                for c in range(done, n):
                    one(c, 0, 0)

            def evac_copy(dst, g):
                def f(c, dc, used):
                    b = 2 * ((g["C"] + c) % 2)
                    w = g["chunks"][c][2]
                    dve.wait_ge(step_used, used)
                    V.tensor_copy(dst[:, 1, ds(dc * CW + g["chunks"][c][1], w)], pg[:, b + 1, 0:w]).then_inc(chunk_out[1], 1)
                return f

            def evac_add(g):
                def f(c, dc, used):
                    b = 2 * ((g["C"] + c) % 2)
                    dve.wait_ge(step_used, used)
                    for t in range(NT):
                        x = H[:, t, ds(dc * CW + c * CW, CW)]
                        V.tensor_tensor(x, pg[:, b + t, :], x, ALU.add).then_inc(chunk_out[t], 1)
                return f

            def refine(y, aa, root_, t1):
                link(V.reciprocal(y, root_))
                link(V.tensor_tensor(t1, y, y, ALU.mult))
                link(V.tensor_tensor(t1, t1, aa, ALU.mult))
                link(V.tensor_scalar(t1, t1, -0.5, 1.5, ALU.mult, ALU.add))

            def norm(i, src, n, junk, dst):
                V.tensor_tensor_reduce(junk, src, src, 1.0, 0.0, ALU.mult, ALU.add, SM[:, 1:2]).then_inc(ss1, 1)
                dve.wait_ge(root, i + 1)
                link(V.tensor_scalar(SM[:, 6:8], SM[:, 0:2], 1.0 / n, EPS, ALU.mult, ALU.add))
                refine(SM[:, 8:10], SM[:, 6:8], SM[:, 2:4], SM[:, 10:12])
                V.tensor_tensor(SM[:, 4:6], SM[:, 8:10], SM[:, 10:12], ALU.mult).then_inc(rstd_ready, 1)
                dve.wait_ge(rstd_ready, i + 1)
                if dst is not None:
                    V.tensor_scalar(dst, src, SM[:, 5:6], None, ALU.mult).then_inc(xn1, 1)

            def prep(p, cols):
                for g in range(KT // 2):
                    dve.wait_ge(a_hi, p * 8 + g + 1)
                    src = pt[:, g % 4, :].rearrange("p (k n) -> p k n", k=2)
                    for k in range(2):
                        kt = 2 * g + k
                        w = cols(kt)
                        sc = 1.0 if w is None else VT[:, w:w + 1]
                        ins = V.scalar_tensor_tensor(AL[:, kt, :], src[:, k, :], sc, AH[:, kt, :].bitcast(F32),
                                                     ALU.mult, ALU.subtract)
                    ins.then_inc(a_lo, 1)

            def add_normed(x, gains):
                dve.wait_ge(gain_landed, gains)
                for t in range(NT):
                    link(V.scalar_tensor_tensor(x[:, t, :], x[:, t, :], SM[:, 4 + t:5 + t], GP[:], ALU.mult, ALU.mult))
                for t in range(NT):
                    ins = V.tensor_tensor(H[:, t, :], H[:, t, :], x[:, t, :], ALU.add)
                    if t == 0:
                        link(ins)
                ins.then_inc(h_ready, 1)

            def cmp_tokens():
                dve.wait_ge(consts_set, 2)
                chunks_read(dve, G["out1"]["C"])
                V.memset(HV[:], 0.0).then_inc(kflat, 1)
                for b in range(4):
                    dst, pe_ = (KFK, V_PEK) if b < 2 else (KFV, V_PEV)
                    h0 = 2 * (b % 2)
                    dve.wait_ge(kc_turned, b + 1)
                    for l in range(2):
                        pr = slice(64 * l, 64 * l + 64)
                        src = pt[pr, b, :].rearrange("p (h a t l) -> p l h t a", h=2, l=2, t=8)[:, l]
                        for th in range(2):
                            for h in range(2):
                                o = dst[pr, 8 * th:8 * th + 8, (h0 + h) * NCMP:(h0 + h + 1) * NCMP]
                                pe2 = VT[pr, pe_ + 8 * th:pe_ + 8 * th + 8].unsqueeze(2).to_broadcast([64, 8, NCMP])
                                ins = V.tensor_tensor(o, src[:, h, :, th:th + NCMP], pe2, ALU.add)
                    ins.then_inc(kflat, 1)
                dve.wait_ge(cmp_sum, 1)
                for h in range(NKV):
                    V.tensor_tensor(BD[:, h, :, :], bc(pg[:, 2, h * HD:(h + 1) * HD].unsqueeze(1), 4, HD),
                                    bc(C[:, C_BLK:C_BLK + 4].unsqueeze(2), 4, HD), ALU.mult).then_inc(cmp_kv, 1)

            def ssd():
                for g in range(CK1 // 2):
                    dve.wait_ge(cv_first, g + 1)
                    for j in (2, 1, 0):
                        for k in range(2):
                            kt = 2 * g + k
                            w = V_CW + j * CK1 + kt
                            x = XC[:, kt, 3 - j:TOK]
                            ins = V.scalar_tensor_tensor(x, pt[:, g % 4, k * TOK:k * TOK + TOK - 3 + j], VT[:, w:w + 1], x,
                                                         ALU.mult, ALU.add)
                        if j:
                            link(ins)
                    ins.then_inc(cv_sum, 1)
                dt2 = lambda o: SD[:, o:o + 2, :]
                bias = bc(BV[:, B_DT:B_DT + 16].unsqueeze(1), 2, 16)
                link(V.tensor_tensor(dt2(0), Z1[:, :, O_DT:O_DT + 16], bias, ALU.add))
                V.scalar_tensor_tensor(dt2(2), dt2(0), -1.0, dt2(0), ALU.mult, ALU.max).then_inc(dt_u, 1)
                link(V.tensor_scalar(dt2(0), dt2(0), 0.0, None, ALU.max))
                dve.wait_ge(dt_exp, 1)
                V.tensor_scalar(dt2(4), dt2(2), 1.0, None, ALU.add).then_inc(dt_u, 1)
                dve.wait_ge(dt_u, 2)
                link(V.tensor_scalar(dt2(8), dt2(4), -1.0, None, ALU.add))
                dve.wait_ge(dt_ln, 1)
                link(V.tensor_scalar(dt2(4), dt2(8), 0.0, None, ALU.is_equal))
                link(V.tensor_tensor(dt2(8), dt2(8), dt2(4), ALU.add))
                link(V.tensor_tensor(dt2(6), dt2(6), dt2(4), ALU.add))
                link(V.reciprocal(dt2(8), dt2(8)))
                link(V.tensor_tensor(dt2(6), dt2(6), dt2(8), ALU.mult))
                link(V.tensor_tensor(dt2(6), dt2(6), dt2(2), ALU.mult))
                link(V.tensor_tensor(dt2(0), dt2(0), dt2(6), ALU.add))
                dve.wait_ge(alog_exp, 1)
                link(V.tensor_scalar(dt2(4), dt2(0), -1.0, None, ALU.mult))
                V.tensor_tensor(dt2(2), dt2(4), bc(SD[:, 14, :].unsqueeze(1), 2, 16), ALU.mult).then_inc(adt_ready, 1)
                dve.wait_ge(xt_turned, 2)
                V.tensor_copy(BT[:].rearrange("p g n -> p (g n)"), pt[:, 0, 0:256])
                for b in range(2):
                    ins = V.tensor_copy(XT[:, 1, b * CW:(b + 1) * CW], pg[:, 2 + b, :])
                ins.then_inc(xt_d, 1)
                dve.wait_ge(acum_sum, 1)
                link(V.tensor_copy(dt2(8), pt[:, 1, 0:32].rearrange("p (t h) -> p t h", t=2)))
                link(V.tensor_copy(SD[:, 12, :], SD[:, 9, :]))
                V.tensor_tensor(SD[:, 11, :], pt[:, 1, 32:48], SD[:, 8, :], ALU.subtract).then_inc(acum_ready, 1)
                dve.wait_ge(xt_a, 1)
                dve.wait_ge(xt_d, 1)
                for t in range(NT):
                    ins = V.tensor_tensor(XD[:, t, :].rearrange("p (h d) -> p h d", d=HD),
                                          XT[:, t, :].rearrange("p (h d) -> p h d", d=HD),
                                          bc(SD[:, t, :].unsqueeze(2), 16, HD), ALU.mult)
                link(ins)
                dve.wait_ge(decay_col, 1)
                V.tensor_tensor(XS[:].rearrange("p (h d) -> p h d", d=HD), XD[:, 0, :].rearrange("p (h d) -> p h d", d=HD),
                                bc(SD[:, 11, :].unsqueeze(2), 16, HD), ALU.mult).then_inc(xs_ready, 1)
                for t in range(NT):
                    dve.wait_ge(row_sum, t + 1)
                    src = (pg, pt)[t]
                    for b in range(4):
                        ins = V.tensor_tensor(M[:, t, 4 * b:4 * b + 4, :], src[:, b, :].rearrange("p (h n) -> p h n", h=4),
                                              bc(C[:, C_NEGT:C_NEGT + P].unsqueeze(1), 4, P), ALU.add)
                    link(ins)
                    V.tensor_tensor(M[:, t, :, :], M[:, t, :, :], bc(SD[:, 8 + t, :].unsqueeze(2), 16, P), ALU.subtract)\
                        .then_inc(seg_ready, 1)
                dve.wait_ge(cb_sum, 1)
                for t in range(NT):
                    dve.wait_ge(seg_exp, t + 1)
                    for g in range(SSD_G):
                        cb = pg[:, 2, (2 * t + g) * P:(2 * t + g + 1) * P]
                        ins = V.tensor_tensor(M[:, t, 8 * g:8 * g + 8, :], M[:, t, 8 * g:8 * g + 8, :], bc(cb.unsqueeze(1), 8, P),
                                              ALU.mult)
                    ins.then_inc(m_ready, 1)
                for t in range(NT):
                    ins = V.tensor_tensor(YS[:, t, :].rearrange("p (h d) -> p h d", d=HD),
                                          XT[:, t, :].rearrange("p (h d) -> p h d", d=HD),
                                          bc(BV[:, B_DSK:B_DSK + 16].unsqueeze(2), 16, HD), ALU.mult)
                link(ins)
                for t in range(NT):
                    dve.wait_ge(yd_sum, t + 1)
                    for b in range(2):
                        x = YS[:, t, b * CW:(b + 1) * CW]
                        ins = V.tensor_tensor(x, pt[:, 2 * t + b, :], x, ALU.add)
                dve.wait_ge(yo_sum, 1)
                for b in range(2):
                    ins = V.tensor_tensor(YOFF[:, b * CW:(b + 1) * CW].rearrange("p (h d) -> p h d", d=HD),
                                          pg[:, 2 + b, :].rearrange("p (h d) -> p h d", d=HD),
                                          bc(SD[:, 12, 8 * b:8 * b + 8].unsqueeze(2), 8, HD), ALU.mult)
                link(ins)
                link(V.tensor_tensor(YS[:, 1, :], YS[:, 1, :], YOFF[:], ALU.add))
                dve.wait_ge(z_silu, 1)
                V.tensor_tensor(YS[:], YS[:], Z1[:, :, O_Z:O_Z + SSD_W], ALU.mult).then_inc(ys_ready, 1)
                dve.wait_ge(ys_ready, 1)
                norm(1, YS[:, 1, :], SSD_W, JUNK[:, 1, :], YS[:, 1, :])

            units = [(b, t, kv) for b in range(2) for t in range(NT) for kv in range(NKV)]
            NM = AT[:, 96:160]
            SUM = AT[:, 160:224]

            RT = XT[:, 0, 0:512].rearrange("p (a h d) -> p a h d", a=4, h=16)
            CM = XT[:, 0, 512:512 + NT * NCMP]
            CX = XT[:, 0, 600:664]
            OT = XT[:, 0, 704:960].rearrange("p (h d) -> p h d", d=HD)

            def nsa():
                V.memset(PC[:], 0.0)
                dve.wait_ge(q_turned, 1)
                V.tensor_copy(QT[:, 4:8, :], pt[:, 2:4, :].rearrange("p b (c n) -> p (b c) n", n=TOK)).then_inc(q_out, 1)
                for o, h in ((O_Q, NH), (O_KS, NKV), (O_KW, NKV)):
                    for t in range(NT):
                        x = Z1[:, t, o:o + h * HD].rearrange("p (h d) -> p h d", d=HD)
                        x1, x2 = x[:, :, 0:ROPE_HALF], x[:, :, ROPE_HALF:2 * ROPE_HALF]
                        cs = bc(C[:, C_COS + t * ROPE_HALF:C_COS + (t + 1) * ROPE_HALF].unsqueeze(1), h, ROPE_HALF)
                        sn = bc(C[:, C_SIN + t * ROPE_HALF:C_SIN + (t + 1) * ROPE_HALF].unsqueeze(1), h, ROPE_HALF)
                        tmp = [RT[:, i, 0:h, :] for i in range(4)]
                        V.tensor_tensor(tmp[0], x1, cs, ALU.mult)
                        V.tensor_tensor(tmp[1], x2, sn, ALU.mult)
                        V.tensor_tensor(tmp[2], x2, cs, ALU.mult)
                        link(V.tensor_tensor(tmp[3], x1, sn, ALU.mult))
                        V.tensor_tensor(x1, tmp[0], tmp[1], ALU.subtract)
                        link(V.tensor_tensor(x2, tmp[2], tmp[3], ALU.add))
                V.memset(RT[:, 0, 0, 0:1], 0.0).then_inc(roped, 1)
                dve.wait_ge(cs_sum, 1)
                sc = SC[:].rearrange("p t (h e) i -> p t e h i", e=2)
                for t in range(NT):
                    mask = C[:, C_CMP + t * NCMP:C_CMP + (t + 1) * NCMP]
                    for e in range(2):
                        ins = V.scalar_tensor_tensor(sc[:, t, e], pg[:, e, t * 128:t * 128 + 128].rearrange("p (h i) -> p h i", i=16)[:, :, 0:NCMP],
                                                     HD ** -0.5, bc(mask.unsqueeze(1), 8, NCMP), ALU.mult, ALU.mult)
                link(ins)
                link(V.tensor_scalar(CM[:], C[:, C_CMP:C_CMP + NT * NCMP], 1.0, 1e30, ALU.subtract, ALU.mult))
                for t in range(NT):
                    ins = V.tensor_tensor(SC[:, t], SC[:, t], bc(CM[:, t * NCMP:(t + 1) * NCMP].unsqueeze(1), 16, NCMP), ALU.add)
                link(ins)
                flat = SC[:].rearrange("p t h i -> p (t h) i")
                link(V.tensor_reduce(CX[:, 0:32], flat, AX.X, ALU.max))
                V.tensor_tensor(flat, flat, bc(CX[:, 0:32].unsqueeze(2), 32, NCMP), ALU.subtract).then_inc(cs_ready, 1)
                dve.wait_ge(cs_exp, 1)
                link(V.tensor_reduce(CX[:, 32:64], flat, AX.X, ALU.add))
                link(V.reciprocal(CX[:, 0:32], CX[:, 32:64]))
                dve.wait_ge(gates, 1)
                link(V.tensor_tensor(CX[:, 32:64], CX[:, 0:32], AT[:, 0:96].rearrange("p (n g) -> p n g", g=3)[:, :, 0], ALU.mult))
                link(V.tensor_tensor(flat, flat, bc(CX[:, 32:64].unsqueeze(2), 32, NCMP), ALU.mult))
                for t in range(NT):
                    ins = V.tensor_tensor(PC[:, t, :, 0:NCMP], SC[:, t], bc(C[:, C_CMP + t * NCMP:C_CMP + (t + 1) * NCMP].unsqueeze(1), 16, NCMP),
                                          ALU.mult)
                ins.then_inc(pc_ready, 1)
                dve.wait_ge(pc_turned, 1)
                V.tensor_copy(PCT[:, 1], bank4(1)).then_inc(pct_ready, 1)
                dve.wait_ge(oc_sum, 1)
                V.tensor_copy(YA[:, 1, :].rearrange("p (b n) -> p b n", b=2), pt[:, 2:4, :]).then_inc(oc_out, 1)
                dve.wait_ge(q_turned, 2)
                V.tensor_copy(QT[:, 4:8, :], pg[:, 2:4, :].rearrange("p b (c n) -> p (b c) n", n=TOK)).then_inc(q_out, 1)
                dve.wait_ge(k_turned, 1)
                V.tensor_copy(KTT[:, 1, :, :], pt[:, 2:4, :].rearrange("p b (c n) -> p (b c) n", n=TOK)).then_inc(k_out, 1)
                dve.wait_ge(oc_out, 2)
                for u in range(18):
                    if u < 16:
                        b, t, kv = units[u]
                        nk = P * (1 + t)
                        dve.wait_ge(s_sum, u + 1)
                        if u >= 2:
                            dve.wait_ge(p_turned, u - 1)
                        mask = C[:, C_ZC + (P if t == 0 else 0):C_ZC + 2 * P]
                        for e in range(2):
                            V.tensor_tensor(S[:, u % 2, e, :, 0:nk], pg[:, 2 * (u % 2) + e, 0:2 * nk].rearrange("p (a n) -> p a n", a=2),
                                            bc(mask.unsqueeze(1), 2, nk), ALU.add).then_inc(s_masked, 1)
                        dve.wait_ge(s_masked, 2 * u + 2)
                        link(V.tensor_reduce(NM[:, 4 * u:4 * u + 4], S[:, u % 2, :, :, 0:nk].rearrange("p e a n -> p (e a) n"), AX.X, ALU.max))
                        V.tensor_scalar(NM[:, 4 * u:4 * u + 4], NM[:, 4 * u:4 * u + 4], -HD ** -0.5, None, ALU.mult).then_inc(s_max, 1)
                    if 1 <= u <= 16 and units[u - 1][1] == 1:
                        dve.wait_ge(p_turned, u)
                        if u >= 3:
                            dve.wait_ge(o_sum, u - 2)
                        V.tensor_copy(PT[:, (u - 1) % 2, 1], bank4(1)).then_inc(p_out1, 1)
                    if u >= 2:
                        v = u - 2
                        b, t, kv = units[v]
                        co = CX[:, 0:4]
                        link(V.reciprocal(co, SUM[:, 4 * v:4 * v + 4]))
                        g4 = AT[:, 48 * t + 12 * kv:48 * t + 12 * kv + 12].rearrange("p (x e g) -> p g e x", e=2, g=3)[:, 1 + b]
                        link(V.tensor_tensor(co.rearrange("p (e x) -> p e x", e=2), co.rearrange("p (e x) -> p e x", e=2), g4, ALU.mult))
                        dve.wait_ge(o_sum, v + 1)
                        tmp = OT[:]
                        link(V.tensor_tensor(tmp, pt[:, 2 + v % 2, 0:256].rearrange("p (h d) -> p h d", d=HD), bc(co.unsqueeze(2), 4, HD), ALU.mult))
                        y = YA[:, t, kv * 256:(kv + 1) * 256].rearrange("p (x e d) -> p e x d", e=2, d=HD)
                        V.tensor_tensor(y, y, tmp.rearrange("p (e x) d -> p e x d", e=2), ALU.add).then_inc(o_out, 1)
                        dve.wait_ge(o_out, v + 1)

            def ffn(g, hooks):
                N = g["N"]

                def pair(c, d):
                    for h in range(4):
                        hooks[h](c, d)
                        for j in range(4):
                            split(N + c * 16 + 4 * (h + 1) + j, d * 16, CW)

                pair(0, 0)
                with dve.Fori(0, NFF - 1) as i:
                    pair(1, i)

            def down(g, hooks, evac):
                N, S_, n = g["N"], g["S"], len(g["chunks"])
                for c in range(n):
                    for j in range(S_):
                        if c == 0 and j % 4 == 0 and j // 4 < len(hooks):
                            hooks[j // 4]()
                        split(N + c * S_ + RING + j)
                    evac(c, 0, N + (c + 1) * S_)

            F1, F2 = G["ffn1"], G["ffn2"]
            no = lambda *_: None

            def after(f):
                return lambda c, d: f(c, d) if c else None

            def f1_h(c, d):
                b = 2 * ((F1["C"] + 1) % 2)
                dve.wait_ge(step_used, F1["N"] + 16 * c + d * 16)
                chunks_read(dve, F1["C"] + 2 * c - 1 + d * 2)
                if c > 1 or not isinstance(d, int):
                    dve.wait_ge(f_turned, c - 1 + d)
                for t in range(NT):
                    V.tensor_tensor(HT[:, t, :], pg[:, b + t, :], SG[:, t, :], ALU.mult).then_inc(chunk_out[t], 1)

            def f1_lo(c, d):
                dve.wait_ge(f_hi, c + d)
                x = FH[:, ds((d + c - 1) * 4, 4), :].bitcast(F32)
                V.tensor_tensor(FL[:, ds((d + c - 1) * 4, 4), :], pt[:, 0:2, :].rearrange("p b (c n) -> p (b c) n", n=TOK), x, ALU.subtract)\
                    .then_inc(f_lo, 1)

            def f2_up(c, d):
                b = 2 * ((F2["C"] + 1) % 2)
                dve.wait_ge(step_used, F2["N"] + 16 * c + d * 16)
                dve.wait_ge(c_turned, 2 * c - 1 + d * 2)
                V.tensor_copy(UT[:, 1, :], pg[:, b + 1, :]).then_inc(chunk_out[1], 1)

            def conv_rest(src, dst, k0, nth):
                dve.wait_ge(c_first, nth)
                for j in (1, 0):
                    for k in range(4):
                        x = dst[:, k, 2 - j:TOK]
                        ins = V.scalar_tensor_tensor(x, src[:, k, 0:TOK - 2 + j], VT[:, ds(k0 + V_CW2 + j * 88 + k, 1)], x,
                                                     ALU.mult, ALU.add)
                    if j:
                        ins.then_inc(c_part, 1)
                        dve.wait_ge(c_part, nth)
                ins.then_inc(c_sum, 1)

            def f2_conv_up(c, d):
                conv_rest(pt[:, 2:4, :].rearrange("p b (c n) -> p (b c) n", n=TOK), UC, d * 4 + (c - 1) * 4 + FKT, 2 * c + d * 2)
                dve.wait_ge(c_sum, 2 * c + d * 2)
                dve.wait_ge(c_silu, c + d)
                V.tensor_tensor(UC[:], UC[:], GC[:], ALU.mult).then_inc(c_prod, 1)

            def f2_gate(c, d):
                b = 2 * (F2["C"] % 2)
                dve.wait_ge(step_used, F2["N"] + 16 * c + 8 + d * 16)
                if c:
                    dve.wait_ge(c_turned, 2 * c + d * 2)
                V.tensor_copy(UT[:, 1, :], pg[:, b + 1, :]).then_inc(chunk_out[1], 1)

            def f2_lo(c, d):
                dve.wait_ge(f_hi, NFF + c + d)
                V.tensor_tensor(FL[:, ds((d + c - 1) * 4, 4), :], UC[:], FH[:, ds((d + c - 1) * 4, 4), :].bitcast(F32), ALU.subtract)\
                    .then_inc(f_lo, 1)

            def f2_conv_gate(c, d):
                conv_rest(pt[:, 0:2, :].rearrange("p b (c n) -> p (b c) n", n=TOK), GC, d * 4 + c * 4, 2 * c + 1 + d * 2)

            def fox():
                v, e = SF_[:, 0:16], SF_[:, 16:32]
                b8 = bc(BV[:, B_BF:B_BF + 8].unsqueeze(1), 2, 8)
                link(V.tensor_tensor(v.rearrange("p (t h) -> p t h", t=2), Z2[:, :, O2_F:O2_F + 8], b8, ALU.add))
                V.scalar_tensor_tensor(e, v, -1.0, v, ALU.mult, ALU.max).then_inc(lf_ready, 1)
                dve.wait_ge(lf_ln, 1)
                V.scalar_tensor_tensor(SF_[:, 32:48], v, 0.0, e, ALU.min, ALU.subtract).then_inc(lf_ready, 1)
                dve.wait_ge(fq_turned, 2)
                V.tensor_copy(KF2[:], pg[:].rearrange("p b (c n) -> p (b c) n", n=TOK)).then_inc(fk_out, 1)
                dve.wait_ge(fc_out, 1)
                for u in range(10):
                    if u < 8:
                        t, hp = u // 4, u % 4
                        nk = P * (1 + t)
                        dve.wait_ge(fs_sum, u + 1)
                        if u >= 2:
                            dve.wait_ge(fp_turned, u - 1)
                        x = SF[:, u % 2, :, 0:nk]
                        link(V.scalar_tensor_tensor(x, pg[:, u % 4, 0:2 * nk].rearrange("p (j n) -> p j n", j=2), P ** -0.5,
                                                    CB[:, 2 * hp:2 * hp + 2, 0:nk], ALU.mult, ALU.add))
                        y = SF[:, u % 2, :, nk - P:nk]
                        link(V.tensor_tensor(y, y, bc(C[:, C_ZC + P:C_ZC + 2 * P].unsqueeze(1), 2, P), ALU.add))
                        m = SF_[:, 64 + 2 * u:66 + 2 * u]
                        link(V.tensor_reduce(m, x, AX.X, ALU.max))
                        V.tensor_scalar(m, m, -1.0, None, ALU.mult).then_inc(fs_max, 1)
                    if u >= 2:
                        w = u - 2
                        t, hp = w // 4, w % 4
                        link(V.reciprocal(SF_[:, 100:102], SF_[:, 80 + 2 * w:82 + 2 * w]))
                        dve.wait_ge(fo_sum, w + 1)
                        V.tensor_tensor(YF[:, t, hp * 256:(hp + 1) * 256].rearrange("p (j n) -> p j n", j=2),
                                        pt[:, 2 + w % 2, 0:256].rearrange("p (j n) -> p j n", j=2),
                                        bc(SF_[:, 100:102].unsqueeze(2), 2, P), ALU.mult).then_inc(fo_out, 1)
                        dve.wait_ge(fo_out, w + 1)

            def hgrn():
                f = Z2[:, :, O2_HF:O2_HF + W2]
                dve.wait_ge(hg_ln, 1)
                V.tensor_scalar(f, f, 0.0, None, ALU.min).then_inc(hg_lf, 1)
                dve.wait_ge(hg_lf, 1)
                V.tensor_tensor(f, f, LG1[:].rearrange("p (t n) -> p t n", t=2), ALU.subtract).then_inc(hg_lf, 1)
                link(V.memset(HS[:], 0.0))
                dve.wait_ge(hq_turned, 1)
                V.tensor_copy(HQ[:], pg[:].rearrange("p b (c n) -> p (b c) n", n=TOK)).then_inc(hq_out, 1)
                dve.wait_ge(hc_out, 1)
                dve.wait_ge(hk_out, 1)
                dve.wait_ge(hq_out, 1)

                def diff(l):
                    if l == 1:
                        dve.wait_ge(hg_lf, 2)
                    if l >= 2:
                        dve.wait_ge(lv_sum, lv_units(l - 2))
                    g = LG[l % 2]
                    if l == 0:
                        x = g[:].rearrange("p (h a n) -> p h a n", h=8, a=4)
                        c = CUM[:].rearrange("p (h a n) -> p h a n", h=8, a=4)
                        link(V.tensor_tensor(x[:, :, 0:2, :], c[:, :, 0:2, 63:64].to_broadcast([P, 8, 2, 64]), c[:, :, 0:2, :], ALU.subtract))
                        V.tensor_tensor(x[:, :, 0, :], x[:, :, 0, :], c[:, :, 1, 63:64].to_broadcast([P, 8, 64]), ALU.add)
                        V.tensor_tensor(x[:, :, 3, :], c[:, :, 3, :], c[:, :, 2, 63:64].to_broadcast([P, 8, 64]), ALU.add).then_inc(lv_diff, 1)
                    elif l == 1:
                        x = g[:].rearrange("p (n a b) -> p n a b", a=2, b=64)
                        c = CUM[:].rearrange("p (n a b) -> p n a b", a=2, b=64)
                        V.tensor_tensor(x[:, :, 0, :], c[:, :, 0, 63:64].to_broadcast([P, 16, 64]), c[:, :, 0, :], ALU.subtract).then_inc(lv_diff, 1)
                    else:
                        b = LEVELS[l - 1]
                        n = HG_N * TOK // (2 * b)
                        x = g[:].rearrange("p (n a b) -> p n a b", a=2, b=b)
                        c = CUM[:].rearrange("p (n a b) -> p n a b", a=2, b=b)
                        ref = c[:, :, 0, b - 1:b].to_broadcast([P, n, b])
                        V.tensor_tensor(x[:, :, 0, :], ref, c[:, :, 0, :], ALU.subtract)
                        V.tensor_tensor(x[:, :, 1, :], c[:, :, 1, :], ref, ALU.subtract).then_inc(lv_diff, 1)

                def mul(l):
                    dve.wait_ge(lv_exp, l + 1)
                    b = P if l == 0 else LEVELS[l - 1]
                    g = LG[l % 2][:].rearrange("p (n a b) -> p n a b", a=2, b=b)
                    k = HKT[:].rearrange("p h (n a b) -> p (h n) a b", a=2, b=b)
                    q = HQ[:].rearrange("p h (n a b) -> p (h n) a b", a=2, b=b)
                    V.tensor_tensor(g[:, :, 0, :], g[:, :, 0, :], k[:, :, 0, :], ALU.mult)
                    V.tensor_tensor(g[:, :, 1, :], g[:, :, 1, :], q[:, :, 1, :], ALU.mult).then_inc(lv_mul, 1)

                def take(l):
                    if l == 0:
                        dve.wait_ge(lv_sum, 1)
                        V.tensor_copy(HX[:], lv_banks(0)).then_inc(lv_out, 1)
                        return
                    for t in range(NT):
                        u = 1 + 2 * (l - 1) + t
                        dve.wait_ge(lv_sum, u + 1)
                        if u >= 3:
                            dve.wait_ge(lv_out, u - 1)
                        mask = bc(MK[:, (l - 1) * P:l * P].unsqueeze(1), 8, P)
                        V.copy_predicated(HS[:, t, :, :], mask, lv_banks(u)).then_inc(lv_out, 1)

                dve.wait_ge(consts_set, 3)
                diff(0)
                for l in range(8):
                    if l + 1 < 8:
                        diff(l + 1)
                    mul(l)
                    if l:
                        take(l - 1)
                take(7)
                take(8)
                dve.wait_ge(ho_out, 1)
                y = YG[:].rearrange("p t (h n) -> p (t h) n", n=P)
                sq = LG1[:].rearrange("p (h n) -> p h n", n=P)
                dve.wait_ge(lv_out, 17)
                link(V.tensor_tensor(sq, y, y, ALU.mult))
                V.tensor_reduce(HN[:, 0:16], sq, AX.X, ALU.add).then_inc(hn_sq, 1)
                dve.wait_ge(hn_root, 1)
                link(V.tensor_scalar(HN[:, 32:48], HN[:, 0:16], 1.0 / P, EPS, ALU.mult, ALU.add))
                refine(HN[:, 0:16], HN[:, 32:48], HN[:, 16:32], HN[:, 48:64])
                link(V.tensor_tensor(HN[:, 0:16], HN[:, 0:16], HN[:, 48:64], ALU.mult))
                link(V.tensor_tensor(y, y, bc(HN[:, 0:16].unsqueeze(2), 16, P), ALU.mult))
                link(V.tensor_tensor(y, y, bc(BV[:, B_GO:B_GO + P].unsqueeze(1), 16, P), ALU.mult))
                dve.wait_ge(hg_silu, 1)
                V.tensor_tensor(YG[:], YG[:], Z2[:, :, O2_HG:O2_HG + W2], ALU.mult).then_inc(yg_ready, 1)

            for n in range(RING):
                split(n)
            dve.wait_ge(x_landed, 16)
            norm(0, H[:, 1, :], D, XN[:, 1, :], XN[:, 1, :])
            dve.wait_ge(vec_turned, 1)
            V.tensor_copy(VT[:, 0:180], pt[:, 0, 0:180]).then_inc(vec_ready, 1)
            V.tensor_copy(VT[:, 180:V_N], pt[:, 1, 0:V_N - 180]).then_inc(vec_ready, 1)
            dve.wait_ge(vec_ready, 2)
            prep(0, lambda k: V_ATTN + k)
            stream(G["in1"], evac_copy(Z1, G["in1"]))
            if upto < 2: return
            dve.wait_ge(step_used, G["in1"]["end"])
            cmp_tokens()
            if upto < 3: return
            dve.wait_ge(bc_landed, 96)
            chunks_read(dve, G["out1"]["C"])
            dve.wait_ge(cmp_kv, 5)
            ssd()
            if upto < 4: return
            dve.wait_ge(yo_sum, 1)
            dve.wait_ge(xn0, 2)
            nsa()
            if upto < 5: return
            prep(1, lambda k: V_SSD + k if k < 8 else None)
            stream(G["out1"], evac_add(G["out1"]))
            V.memset(SM[:, 12:13], 0.0).then_inc(h_ready, 1)
            chunks_read(dve, F1["C"])
            norm(2, H[:, 1, :], D, XN[:, 1, :], XN[:, 1, :])
            prep(2, lambda k: V_FFN + k)
            if upto < 8: return
            ffn(F1, [after(f1_h), after(f1_lo), no, no])
            if upto < 9: return
            down(G["down1"], [lambda: f1_h(NFF, 0), lambda: f1_lo(NFF, 0)], evac_add(G["down1"]))
            V.memset(SM[:, 12:13], 0.0).then_inc(h_ready, 1)
            chunks_read(dve, G["in2"]["C"])
            norm(3, H[:, 1, :], D, XN[:, 1, :], None)
            if upto < 10: return
            dve.wait_ge(gain_landed, 16)
            for t in range(NT):
                link(V.scalar_tensor_tensor(H[:, t, :], H[:, t, :], SM[:, 4 + t:5 + t], GP[:], ALU.mult, ALU.mult))
            V.memset(SM[:, 12:13], 0.0).then_inc(h_ready, 1)
            norm(4, H[:, 1, :], D, XN[:, 1, :], XN[:, 1, :])
            prep(3, lambda k: V_GMIX + k)
            stream(G["in2"], evac_copy(Z2, G["in2"]))
            if upto < 12: return
            dve.wait_ge(step_used, G["in2"]["end"])
            chunks_read(dve, G["out2"]["C"])
            fox()
            if upto < 13: return
            hgrn()
            if upto < 14: return
            prep(4, lambda k: None)
            stream(G["out2"], evac_copy(MIX, G["out2"]))
            V.memset(SM[:, 12:13], 0.0).then_inc(h_ready, 1)
            chunks_read(dve, F2["C"])
            norm(5, MIX[:, 1, :], D, E[:, 1, :], None)
            add_normed(MIX, 32)
            V.memset(SM[:, 12:13], 0.0).then_inc(h_ready, 1)
            dve.wait_ge(h_ready, 6)
            norm(6, H[:, 1, :], D, XN[:, 1, :], XN[:, 1, :])
            prep(5, lambda k: V_GFFN + k)
            if upto < 17: return
            ffn(F2, [after(f2_up), after(f2_conv_up), lambda c, d: (f2_gate(c, d), after(f2_lo)(c, d)), f2_conv_gate])
            down(G["down2"], [lambda: f2_up(NFF, 0), lambda: f2_conv_up(NFF, 0), no, lambda: f2_lo(NFF, 0)],
                 evac_copy(FO, G["down2"]))
            if upto < 18: return
            V.memset(SM[:, 12:13], 0.0).then_inc(h_ready, 1)
            chunks_read(dve, G["proj"]["C"])
            norm(7, FO[:, 1, :], D, E[:, 1, :], None)
            add_normed(FO, 48)
            dve.wait_ge(h_ready, 8)
            norm(8, H[:, 1, :], D, XN[:, 1, :], XN[:, 1, :])
            dve.wait_ge(p_hi, 1)
            V.tensor_tensor(PL[:], pt[:, 3, :].rearrange("p (k n) -> p k n", k=2), PH[:].bitcast(F32), ALU.subtract).then_inc(p_lo, 1)
            prep(6, lambda k: V_GPLE + k)
            stream(G["proj"], evac_copy(E, G["proj"]))
            g = G["ple"]
            for c in range(4):
                for j in range(8):
                    split(g["N"] + c * 8 + RING + j)
                for t in range(NT):
                    dve.wait_ge(chunk_out[t], g["C"] + c + 1)
                    x = E[:, t, c * CW:(c + 1) * CW]
                    V.tensor_tensor(x, x, GS[:, t, :], ALU.mult).then_inc(e_ready, 1)
            dve.wait_ge(e_ready, 8)
            norm(9, E[:, 1, :], D, XN[:, 1, :], None)
            V.memset(SM[:, 12:13], 0.0).then_inc(h_ready, 1)
            add_normed(E, 64)

        @block.tensor
        def _(pe):
            mm, tr = nc.tensor.matmul, nc.tensor.transpose

            def step(n, d, b, kt0, w, first, last, hi=AH, lo=AL):
                pe.wait_ge(lo_ready, n + 1 + d)
                for k in range(SK):
                    wh = whi[:, n % RING, k * w:(k + 1) * w]
                    wl = wlo[:, n % RING, k * w:(k + 1) * w]
                    for t in range(NT):
                        xh = hi[:, kt0 + k, t * P:(t + 1) * P]
                        xl = lo[:, kt0 + k, t * P:(t + 1) * P]
                        o = pg[:, b + t, 0:w]
                        mm(o, xh, wh, start=first and k == 0, stop=False)
                        mm(o, xh, wl, start=False, stop=False)
                        ins = mm(o, xl, wh, start=False, stop=last and k == SK - 1)
                ins.then_inc(step_used, 1)

            def chunk(g, c, j0=0, j1=None, dc=0, dn=0, hi=AH, lo=AL, before=None):
                C_ = g["C"] + c
                w = g["chunks"][c][2]
                for j in range(j0, g["S"] if j1 is None else j1):
                    if j == 0 and (C_ >= 2 or not isinstance(dc, int)):
                        chunks_read(pe, C_ - 1 + dc)
                    if before:
                        before(j)
                    step(g["N"] + c * g["S"] + j, dn, 2 * (C_ % 2), SK * j, w, j == 0, j == g["S"] - 1, hi, lo)

            def turn(p, src):
                for g in range(KT // 2):
                    if g >= 4:
                        pe.wait_ge(a_lo, p * 8 + g - 3)
                    for k in range(2):
                        for t in range(NT):
                            ins = tr(pt[:, g % 4, (2 * k + t) * P:(2 * k + t + 1) * P], src(2 * g + k, t), ident)
                    ins.then_inc(turned, 1)

            def xn_tiles(kt, t):
                return XN[:, t, kt * P:(kt + 1) * P]

            def stream(g, p):
                n = len(g["chunks"])
                chunk(g, 0, before=lambda j: pe.wait_ge(a_lo, p * 8 + j + 1))
                chunk(g, 1)
                loops = uniform_pairs(g)
                if loops > 2:
                    with pe.Fori(0, loops - 1) as i:
                        for c in (2, 3):
                            chunk(g, c, dc=i * 2, dn=i * (2 * g["S"]))
                    done = 2 * loops
                else:
                    done = 2
                for c in range(done, n):
                    chunk(g, c)

            def cmp_tokens():
                pe.wait_ge(kv_twice, 1)
                for b in range(4):
                    for h in range(2):
                        for t in range(NT):
                            src = KVD[:, b // 2, t, 2 * (b % 2) + h].rearrange("p a d -> p (a d)")
                            ins = tr(pt[:, b, h * TOK + t * P:h * TOK + (t + 1) * P], src, ident)
                    ins.then_inc(kc_turned, 1)
                pe.wait_ge(cmpw_landed, 80)
                for i, (w, x) in enumerate(((W1K, KFK), (W1V, KFV))):
                    pe.wait_ge(kflat, 3 + 2 * i)
                    for m in range(2):
                        for k in range(KT):
                            ins = mm(pg[:, 0, (2 * i + m) * 64:(2 * i + m) * 64 + 60], w[:, k, m * P:(m + 1) * P], x[:, k, :],
                                     start=k == 0, stop=k == KT - 1)
                ins.then_inc(hid_sum, 1)
                pe.wait_ge(hid_act, 2)
                for m in range(2):
                    mm(pg[:, 1, 0:60], W2K[:, m].rearrange("p a d -> p (a d)"), HK[:, m, :], start=m == 0, stop=m == 1)
                for h in range(NKV):
                    for m in range(2):
                        ins = mm(pg[:, 2, h * HD:(h + 1) * HD], HV[:, m, h].rearrange("p g i -> p (g i)"), W2V[:, m, :],
                                 start=m == 0, stop=m == 1)
                ins.then_inc(cmp_sum, 1)

            def ssd():
                for g in range(CK1 // 2):
                    if g >= 4:
                        pe.wait_ge(cv_sum, g - 3)
                    for k in range(2):
                        for t in range(NT):
                            c0 = O_XBC + (2 * g + k) * P
                            ins = tr(pt[:, g % 4, (2 * k + t) * P:(2 * k + t + 1) * P], Z1[:, t, c0:c0 + P], ident)
                    ins.then_inc(cv_turned, 1)
                pe.wait_ge(cv_act, 4)
                for t in range(NT):
                    for k in range(8):
                        ins = tr(pg[:, 2 * t + k // 4, (k % 4) * P:(k % 4 + 1) * P], XC[:, k, t * P:(t + 1) * P], ident)
                    if t == 0:
                        ins.then_inc(xt_turned, 1)
                pe.wait_ge(cv_act, 6)
                for g in range(SSD_G):
                    ins = tr(pt[:, 0, g * P:(g + 1) * P], XC[:, 8 + g, 0:P], ident)
                ins.then_inc(xt_turned, 1)
                pe.wait_ge(adt_ready, 1)
                for t in range(NT):
                    mm(pt[:, 1, 16 * t:16 * t + 16], tri, SD[:, 2 + t, :], start=True, stop=True)
                mm(pt[:, 1, 32:48], ONES[:], SD[:, 2, :], start=True, stop=True).then_inc(acum_sum, 1)
                pe.wait_ge(xt_a, 1)
                pe.wait_ge(xt_d, 1)
                pe.wait_ge(acum_ready, 1)
                for t in range(NT):
                    dst = (pg, pt)[t]
                    for h in range(SSD_H):
                        ins = mm(dst[:, h // 4, (h % 4) * P:(h % 4 + 1) * P], bc(SD[:, 2 + t, h:h + 1], P), tri, start=True, stop=True)
                    ins.then_inc(row_sum, 1)
                pe.wait_ge(seg_ready, 1)
                for t in range(NT):
                    for g in range(SSD_G):
                        ins = mm(pg[:, 2, (2 * t + g) * P:(2 * t + g + 1) * P], XC[:, 8 + g, t * P:(t + 1) * P],
                                 XC[:, 10 + g, t * P:(t + 1) * P], start=True, stop=True)
                ins.then_inc(cb_sum, 1)
                pe.wait_ge(xs_ready, 1)
                for g in range(SSD_G):
                    ins = mm(pg[:, g, :], BT[:, g, :], XS[:, g * CW:(g + 1) * CW], start=True, stop=True)
                ins.then_inc(st_sum, 1)
                pe.wait_ge(seg_ready, 2)
                for t in range(NT):
                    pe.wait_ge(m_ready, t + 1)
                    for h in range(SSD_H):
                        ins = mm(pt[:, 2 * t + h // 8, (h % 8) * HD:(h % 8 + 1) * HD], M[:, t, h, :], XD[:, t, h * HD:(h + 1) * HD],
                                 start=True, stop=True)
                    ins.then_inc(yd_sum, 1)
                pe.wait_ge(st_ready, 1)
                for g in range(SSD_G):
                    ins = mm(pg[:, 2 + g, :], XC[:, 10 + g, P:TOK], STA[:, g, :], start=True, stop=True)
                ins.then_inc(yo_sum, 1)

            units = [(b, t, kv) for b in range(2) for t in range(NT) for kv in range(NKV)]

            def nsa():
                pe.wait_ge(ys_ready, 1)
                for h in range(8):
                    for t in range(NT):
                        ins = tr(pt[:, h // 2, (h % 2) * TOK + t * P:(h % 2) * TOK + (t + 1) * P],
                                 Z1[:, t, O_Q + h * P:O_Q + (h + 1) * P], ident)
                ins.then_inc(q_turned, 1)
                pe.wait_ge(q_out, 2)
                for t in range(NT):
                    for h in range(NH):
                        e, kv = h % 2, h // 4
                        pr = slice(64 * e, 64 * e + 64)
                        c0 = t * 128 + (h // 2) * 16
                        ins = mm(pg[:, e, c0:c0 + NCMP], QT[pr, h // 2, t * P:(t + 1) * P], KCT[pr, kv * NCMP:(kv + 1) * NCMP],
                                 start=True, stop=True)
                ins.then_inc(cs_sum, 1)
                pe.wait_ge(pc_ready, 1)
                for t in range(NT):
                    for kv in range(NKV):
                        ins = tr(pt[:, t, kv * P:(kv + 1) * P], PC[:, t, 4 * kv:4 * kv + 4, :].rearrange("p h i -> p (h i)"), ident)
                ins.then_inc(pc_turned, 1)
                pe.wait_ge(pct_ready, 2)
                for t in range(NT):
                    for kv in range(NKV):
                        dst = pg[:, 2 + kv // 2, :] if t == 0 else pt[:, 2 + kv // 2, :]
                        ins = mm(dst[:, (kv % 2) * 256:(kv % 2 + 1) * 256], PCT[:, t, kv, :], BD[:, kv].rearrange("p a d -> p (a d)"),
                                 start=True, stop=True)
                ins.then_inc(oc_sum, 1)
                pe.wait_ge(roped, 1)
                pe.wait_ge(oc_out, 2)
                for h in range(8):
                    for t in range(NT):
                        ins = tr(pg[:, h // 2, (h % 2) * TOK + t * P:(h % 2) * TOK + (t + 1) * P],
                                 Z1[:, t, O_Q + h * P:O_Q + (h + 1) * P], ident)
                ins.then_inc(q_turned, 1)
                pe.wait_ge(k_twice, 1)
                for i in range(2):
                    for kv in range(NKV):
                        for t in range(NT):
                            src = KSD[:, i, t, kv].rearrange("p a d -> p (a d)")
                            c0 = (kv % 2) * TOK + t * P
                            ins = tr(pt[:, 2 * i + kv // 2, c0:c0 + P], src, ident)
                ins.then_inc(k_turned, 1)
                pe.wait_ge(q_out, 4)
                pe.wait_ge(k_out, 2)
                for u in range(18):
                    if u < 16:
                        b, t, kv = units[u]
                        nk = P * (1 + t)
                        if u >= 2:
                            pe.wait_ge(s_masked, 2 * (u - 1))
                        for x in range(2):
                            for e in range(2):
                                pr = slice(64 * e, 64 * e + 64)
                                ins = mm(pg[:, 2 * (u % 2) + e, x * nk:(x + 1) * nk], QT[pr, 2 * kv + x, t * P:(t + 1) * P],
                                         KTT[pr, b, kv, 0:nk], start=True, stop=True)
                        ins.then_inc(s_sum, 1)
                    if 1 <= u <= 16:
                        b, t, kv = units[u - 1]
                        pe.wait_ge(s_exp, u)
                        if u >= 2:
                            pe.wait_ge(p_out0, u - 1)
                            if units[u - 2][1]:
                                pe.wait_ge(p_out1, sum(x[1] for x in units[:u - 1]))
                        for kb in range(1 + t):
                            for j in range(4):
                                ins = tr(pt[:, kb, j * P:(j + 1) * P], S[:, (u - 1) % 2, j // 2, j % 2, kb * P:(kb + 1) * P], ident)
                        ins.then_inc(p_turned, 1)
                    if u >= 2:
                        v = u - 2
                        b, t, kv = units[v]
                        o = (O_VS, O_VW)[b] + kv * HD
                        pe.wait_ge(p_out0, v + 1)
                        if t:
                            pe.wait_ge(p_out1, sum(x[1] for x in units[:v + 1]))
                        if v >= 2:
                            pe.wait_ge(o_out, v - 1)
                        for j in range(4):
                            for kb in range(1 + t):
                                ins = mm(pt[:, 2 + v % 2, j * HD:(j + 1) * HD], PT[:, v % 2, kb, j, :], Z1[:, kb, o:o + HD],
                                         start=kb == 0, stop=kb == t)
                        ins.then_inc(o_sum, 1)

            F1, F2 = G["ffn1"], G["ffn2"]

            def f1_turn(c, d):
                chunks_read(pe, F1["C"] + 2 * c + d * 2)
                if c > 1 or not isinstance(d, int):
                    pe.wait_ge(f_lo, c - 1 + d)
                for k in range(4):
                    for t in range(NT):
                        ins = tr(pt[:, k // 2, (k % 2) * TOK + t * P:(k % 2) * TOK + (t + 1) * P], HT[:, t, k * P:(k + 1) * P], ident)
                ins.then_inc(f_turned, 1)

            def f1_pair(c, d):
                dc, dn = d * 2, d * 16
                if c:
                    chunk(F1, 2 * c, 0, 4, dc, dn)
                    f1_turn(c, d)
                    chunk(F1, 2 * c, 4, 8, dc, dn)
                else:
                    chunk(F1, 0, before=lambda j: pe.wait_ge(a_lo, 16 + j + 1))
                chunk(F1, 2 * c + 1, dc=dc, dn=dn)

            def f2_turn(b0, nth):
                for k in range(4):
                    for t in range(NT):
                        ins = tr(pt[:, b0 + k // 2, (k % 2) * TOK + t * P:(k % 2) * TOK + (t + 1) * P], UT[:, t, k * P:(k + 1) * P], ident)
                ins.then_inc(c_turned, 1)

            def f2_turn_up(c, d):
                chunks_read(pe, F2["C"] + 2 * c + d * 2)
                if c > 1 or not isinstance(d, int):
                    pe.wait_ge(c_sum, 2 * (c - 1) + d * 2)
                f2_turn(2, 0)

            def f2_pair(c, d):
                dc, dn = d * 2, d * 16
                if c:
                    chunk(F2, 2 * c, 0, 4, dc, dn)
                    f2_turn_up(c, d)
                    chunk(F2, 2 * c, 4, 8, dc, dn)
                else:
                    chunk(F2, 0, before=lambda j: pe.wait_ge(a_lo, 40 + j + 1))
                chunk(F2, 2 * c + 1, 0, 4, dc, dn)
                chunks_read(pe, F2["C"] + 2 * c + 1 + d * 2)
                if c:
                    pe.wait_ge(c_sum, 2 * c - 1 + d * 2)
                f2_turn(0, 0)
                chunk(F2, 2 * c + 1, 4, 8, dc, dn)

            def pairs(f):
                f(0, 0)
                with pe.Fori(0, NFF - 1) as i:
                    f(1, i)

            def down(g, turn_last, f0):
                pe.wait_ge(f_lo, f0 + NFF - 1)
                chunk(g, 0, 0, 4, hi=FH, lo=FL)
                turn_last()
                chunk(g, 0, 4, 20, hi=FH, lo=FL)
                pe.wait_ge(f_lo, f0 + NFF)
                chunk(g, 0, 20, hi=FH, lo=FL)
                for c in range(1, 4):
                    chunk(g, c, hi=FH, lo=FL)

            def fox():
                for h in range(8):
                    for t in range(NT):
                        ins = tr(pt[:, h // 2, (h % 2) * TOK + t * P:(h % 2) * TOK + (t + 1) * P], Z2[:, t, h * P:(h + 1) * P], ident)
                ins.then_inc(fq_turned, 1)
                for h in range(8):
                    for t in range(NT):
                        ins = tr(pg[:, h // 2, (h % 2) * TOK + t * P:(h % 2) * TOK + (t + 1) * P],
                                 Z2[:, t, O2_K + h * P:O2_K + (h + 1) * P], ident)
                ins.then_inc(fq_turned, 1)
                pe.wait_ge(fq_out, 1)
                pe.wait_ge(lf_ready, 2)
                for h in range(8):
                    l0, l1 = (bc(SF_[:, 32 + 8 * t + h:33 + 8 * t + h], P) for t in range(NT))
                    o = pt[:, h // 2, (h % 2) * TOK:(h % 2 + 1) * TOK]
                    mm(o[:, 0:P], l0, tri, start=True, stop=True)
                    mm(o[:, P:TOK], l0, ONES[:], start=True, stop=False)
                    ins = mm(o[:, P:TOK], l1, tri, start=False, stop=True)
                ins.then_inc(fc_sum, 1)
                pe.wait_ge(fk_out, 1)
                pe.wait_ge(fc_out, 1)
                for u in range(10):
                    if u < 8:
                        t, hp = u // 4, u % 4
                        nk = P * (1 + t)
                        if u >= 4:
                            pe.wait_ge(fs_max, u - 3)
                        for j in range(2):
                            h = 2 * hp + j
                            ins = mm(pg[:, u % 4, j * nk:(j + 1) * nk], QT[:, h, t * P:(t + 1) * P], KF2[:, h, 0:nk], start=True, stop=True)
                        ins.then_inc(fs_sum, 1)
                    if 1 <= u <= 8:
                        t = (u - 1) // 4
                        pe.wait_ge(fs_exp, u)
                        if u >= 3:
                            pe.wait_ge(fp_out, u - 2)
                        for j in range(2):
                            for kb in range(1 + t):
                                ins = tr(pt[:, (u - 1) % 2, (2 * j + kb) * P:(2 * j + kb + 1) * P], SF[:, (u - 1) % 2, j, kb * P:(kb + 1) * P], ident)
                        ins.then_inc(fp_turned, 1)
                    if u >= 2:
                        v = u - 2
                        t, hp = v // 4, v % 4
                        pe.wait_ge(fp_out, v + 1)
                        if v >= 2:
                            pe.wait_ge(fo_out, v - 1)
                        for j in range(2):
                            o = O2_V + (2 * hp + j) * P
                            for kb in range(1 + t):
                                ins = mm(pt[:, 2 + v % 2, j * P:(j + 1) * P], PF[:, v % 2, j, kb, :], Z2[:, kb, o:o + P],
                                         start=kb == 0, stop=kb == t)
                        ins.then_inc(fo_sum, 1)

            def hgrn():
                pe.wait_ge(fo_out, 8)
                for h in range(8):
                    for t in range(NT):
                        ins = tr(pg[:, h // 2, (h % 2) * TOK + t * P:(h % 2) * TOK + (t + 1) * P],
                                 Z2[:, t, O2_HQ + h * P:O2_HQ + (h + 1) * P], ident)
                ins.then_inc(hq_turned, 1)
                pe.wait_ge(hg_sig, 1)
                for h in range(8):
                    for t in range(NT):
                        ins = tr(pt[:, h // 2, (h % 2) * TOK + t * P:(h % 2) * TOK + (t + 1) * P], YG[:, t, h * P:(h + 1) * P], ident)
                ins.then_inc(hk_turned, 1)
                pe.wait_ge(hg_lf, 2)
                pe.wait_ge(hk_out, 1)
                for h in range(8):
                    for t in range(NT):
                        c0 = O2_HF + h * P
                        ins = mm(pt[:, h // 2, (h % 2) * TOK + t * P:(h % 2) * TOK + (t + 1) * P], Z2[:, t, c0:c0 + P], tri64,
                                 start=True, stop=True)
                ins.then_inc(hc_sum, 1)
                pe.wait_ge(hc_out, 1)
                pe.wait_ge(hq_out, 1)

                def unit(u, lhs, rhs):
                    if u >= 4:
                        pe.wait_ge(lv_out, u - 3)
                    dst = lv_banks(u)
                    for h in range(8):
                        ins = mm(dst[:, h, :], lhs(h), rhs(h), start=True, stop=True)
                    ins.then_inc(lv_sum, 1)

                for l in range(8):
                    pe.wait_ge(lv_mul, l + 1)
                    g = LG[l % 2][:].rearrange("p (h n) -> p h n", h=8)
                    if l == 0:
                        unit(0, lambda h: g[:, h, 0:P], lambda h: g[:, h, P:TOK])
                    else:
                        for t in range(NT):
                            unit(1 + 2 * (l - 1) + t, lambda h: g[:, h, t * P:(t + 1) * P], lambda h: g[:, h, t * P:(t + 1) * P])
                for t in range(NT):
                    unit(15 + t, lambda h: HKT[:, h, t * P:(t + 1) * P], lambda h: HQ[:, h, t * P:(t + 1) * P])
                pe.wait_ge(lv_out, 17)
                for h in range(8):
                    v = [Z2[:, t, O2_HI + h * P:O2_HI + (h + 1) * P] for t in range(NT)]
                    c0 = (h % 4) * P
                    mm(pt[:, h // 4, c0:c0 + P], HS[:, 0, h, :], v[0], start=True, stop=True)
                    mm(pt[:, 2 + h // 4, c0:c0 + P], HX[:, h, :], v[0], start=True, stop=False)
                    ins = mm(pt[:, 2 + h // 4, c0:c0 + P], HS[:, 1, h, :], v[1], start=False, stop=True)
                ins.then_inc(ho_sum, 1)

            pe.wait_ge(const_landed, 32)
            pe.wait_ge(vec_landed, 14 * 16)
            tr(pt[:, 0, 0:100], VR[0:100, 0, :], C[0:100, 0:100])
            tr(pt[:, 0, 100:180], VR[0:80, 1, :], C[0:80, 0:80])
            for j in range(4):
                ins = tr(pt[:, 1, 88 * j:88 * j + 88], VR[0:88, 2 + j, :], C[0:88, 0:88])
            ins.then_inc(vec_turned, 1)
            pe.wait_ge(vec_ready, 2)
            pe.wait_ge(xn0, 1)
            pe.wait_ge(xn1, 1)
            turn(0, xn_tiles)
            stream(G["in1"], 0)
            if upto < 2: return
            pe.wait_ge(a_lo, 8)
            chunks_read(pe, G["out1"]["C"])
            cmp_tokens()
            if upto < 3: return
            pe.wait_ge(cmp_kv, 5)
            ssd()
            if upto < 4: return
            nsa()
            if upto < 5: return
            pe.wait_ge(o_out, 16)
            pe.wait_ge(xn0, 2)
            pe.wait_ge(xn1, 2)
            turn(1, lambda k, t: YS[:, t, k * P:(k + 1) * P] if k < 8 else YA[:, t, (k - 8) * P:(k - 7) * P])
            stream(G["out1"], 1)
            pe.wait_ge(a_lo, 16)
            pe.wait_ge(xn0, 3)
            pe.wait_ge(xn1, 3)
            turn(2, xn_tiles)
            if upto < 8: return
            pairs(f1_pair)
            if upto < 9: return
            down(G["down1"], lambda: f1_turn(NFF, 0), 0)
            if upto < 10: return
            pe.wait_ge(xn0, 4)
            pe.wait_ge(xn1, 4)
            turn(3, xn_tiles)
            stream(G["in2"], 3)
            if upto < 12: return
            chunks_read(pe, G["out2"]["C"])
            fox()
            if upto < 13: return
            hgrn()
            if upto < 14: return
            pe.wait_ge(yg_ready, 1)
            turn(4, lambda k, t: YF[:, t, k * P:(k + 1) * P] if k < 8 else YG[:, t, (k - 8) * P:(k - 7) * P])
            stream(G["out2"], 4)
            pe.wait_ge(xn0, 5)
            pe.wait_ge(xn1, 5)
            turn(5, xn_tiles)
            if upto < 17: return
            pairs(f2_pair)
            down(G["down2"], lambda: f2_turn_up(NFF, 0), NFF)
            if upto < 18: return
            pe.wait_ge(bc_landed, 96)
            for k in range(2):
                for t in range(NT):
                    ins = tr(pt[:, 3, (2 * k + t) * P:(2 * k + t + 1) * P], PIN[:, t, k * P:(k + 1) * P], ident)
            ins.then_inc(p_tr, 1)
            pe.wait_ge(p_lo, 1)
            pe.wait_ge(xn0, 6)
            pe.wait_ge(xn1, 6)
            turn(6, xn_tiles)
            for c in range(4):
                chunk(G["proj"], c, hi=PH, lo=PL)
            stream(G["ple"], 6)


def uniform_pairs(g):
    n = sum(c[2] == CW for c in g["chunks"]) // 2
    if g["S"] % RING:
        return 0
    return n if len(g["chunks"]) > 2 * n and g["chunks"][2 * n][2] == CW or n * 2 == len(g["chunks"]) else n - 1


_INS = [
    "x", "attn_norm_w", "w_in", "conv_w", "conv_b", "dt_bias", "a_log", "d_skip", "ssd_norm_w", "cmp_w1_k",
    "cmp_w2_k", "cmp_w1_v", "cmp_w2_v", "cmp_pe_k", "cmp_pe_v", "w_out", "ffn_norm_w", "w_gate", "w_up",
    "w_down", "final_norm_w", "p_2", "g_mix_pre_2", "w_in_2", "b_fox_f_2", "g_hgrn_out_2", "w_out_2",
    "g_mix_post_2", "g_ffn_pre_2", "w_up_2", "conv_w_2", "conv_b_2", "w_down_2", "g_ffn_post_2",
    "g_ple_in_2", "w_ple_gate_2", "w_ple_proj_2", "g_ple_post_2",
]


def kernel(**inputs):
    import concourse.bacc as bacc
    from concourse.bass_utils import run_bass_kernel_spmd

    nc = bacc.Bacc("TRN2", target_bir_lowering=False, num_devices=1)
    consts, masks = constants()
    arrays = {n: np.ascontiguousarray(inputs[n]) for n in _INS}
    arrays["consts"], arrays["masks"] = consts, masks
    a = {n: nc.dram_tensor(n, v.shape, mybir.dt.from_np(v.dtype), kind="ExternalInput").ap() for n, v in arrays.items()}
    a["out"] = nc.dram_tensor("out", (1, TOK, D), F32, kind="ExternalOutput").ap()
    two_blocks(nc, a)
    r = run_bass_kernel_spmd(nc, [arrays], core_ids=[0])
    return r.results[0]["out"]
```

```python
from contextlib import ExitStack

import numpy as np

import concourse.bass as bass
from concourse import mybir

F32 = mybir.dt.float32
F32R = mybir.dt.float32r
U8 = mybir.dt.uint8
ALU = mybir.AluOpType
ACT = mybir.ActivationFunctionType
AX = mybir.AxisListType
ds = bass.ds

P = 128
TOK = 256
NT = TOK // P
D = 2048
KT = D // P
EPS = 1e-6
NEG = -1e30

SSD_W = 1024
SSD_H = 16
SSD_G = 2
CONV1 = 1536
CK1 = CONV1 // P
HD = 64
NH = 16
NKV = 4
CMP_BLOCK, CMP_STRIDE, CMP_HID = 32, 16, 256
NCMP = (TOK - CMP_BLOCK) // CMP_STRIDE + 1
ROPE_HALF = HD // 4 // 2
O_Z, O_XBC = 0, SSD_W
O_DT = O_XBC + CONV1
O_Q = O_DT + SSD_H
O_KC = O_Q + NH * HD
O_VC, O_KS, O_VS, O_KW, O_VW = (O_KC + i * NKV * HD for i in range(1, 6))
O_GATE = O_KC + 6 * NKV * HD
D_IN1 = O_GATE + 3 * NH
FF = 5632
FKT = FF // P
W2 = 1024
FH_N = 8
HG_N = 8
O2_K, O2_V, O2_F = W2, 2 * W2, 3 * W2
O2_HQ = O2_F + FH_N
O2_HF, O2_HI, O2_HG = (O2_HQ + i * W2 for i in range(1, 4))
D_IN2 = O2_HG + W2
PLE = 256

CW = 512
SK = 2
RING = 4
NFF = FF // CW

C_ID, C_TRI, C_TRI64, C_ZC, C_NEGT, C_CMP = 0, 128, 256, 384, 640, 768
C_COS = C_CMP + NT * NCMP
C_SIN = C_COS + NT * ROPE_HALF
C_BLK = C_SIN + NT * ROPE_HALF
C_N = C_BLK + 4
LEVELS = (64, 32, 16, 8, 4, 2, 1, 0)

V_ATTN, V_FFN, V_GMIX, V_GFFN, V_GPLE, V_SSD, V_CB = 0, 16, 32, 48, 64, 80, 88
V_FIN, V_CW, V_PEK, V_PEV, V_CW2, V_CB2 = 100, 116, 164, 180, 196, 460
V_N = 548
B_DT, B_ALOG, B_DSK, B_BF, B_GO, B_N = 0, 16, 32, 48, 56, 184


def constants():
    c = np.zeros((P, C_N), np.float32)
    i = np.arange(P)
    c[:, C_ID:C_ID + P] = np.eye(P)
    le = i[:, None] <= i[None, :]
    c[:, C_TRI:C_TRI + P] = le
    c[:, C_TRI64:C_TRI64 + P] = le & (i[:, None] // 64 == i[None, :] // 64)
    c[:, C_ZC + P:C_ZC + 2 * P] = np.where(i[:, None] >= i[None, :], 0.0, NEG)
    c[:, C_NEGT:C_NEGT + P] = np.where(le, 0.0, NEG)
    inv = 1.0 / (np.float32(500000.0) ** (np.arange(0, 2 * ROPE_HALF, 2, dtype=np.float32) / np.float32(2 * ROPE_HALF)))
    for t in range(NT):
        pos = t * P + i
        end = np.arange(NCMP) * CMP_STRIDE + CMP_BLOCK - 1
        c[:, C_CMP + t * NCMP:C_CMP + (t + 1) * NCMP] = end[None, :] <= pos[:, None]
        ang = pos.astype(np.float32)[:, None] * inv[None, :].astype(np.float32)
        c[:, C_COS + t * ROPE_HALF:C_COS + (t + 1) * ROPE_HALF] = np.cos(ang)
        c[:, C_SIN + t * ROPE_HALF:C_SIN + (t + 1) * ROPE_HALF] = np.sin(ang)
    c[:, C_BLK:C_BLK + 4] = i[:, None] // 32 == np.arange(4)[None, :]
    m = np.zeros((P, len(LEVELS), P), np.float32)
    s, t = i[:, None], i[None, :]
    for n, b in enumerate(LEVELS):
        if b:
            m[:, n] = (s // (2 * b) == t // (2 * b)) & (s % (2 * b) < b) & (t % (2 * b) >= b)
        else:
            m[:, n] = s == t
    return c, m.reshape(P, len(LEVELS) * P)


def plan():
    full = lambda w, n: [(w, c * CW, CW) for c in range(n)]
    tail = lambda w, c0, n: [(w, c0, (n - c0) // 2), (w, c0 + (n - c0) // 2, (n - c0) // 2)]
    pairs = lambda a, b, off: [x for c in range(NFF) for x in ((a, c * CW, CW), (b, off + c * CW, CW))]
    table = [
        ("in1", full("w_in", 9) + tail("w_in", 9 * CW, D_IN1), KT),
        ("out1", full("w_out", 4), KT),
        ("ffn1", pairs("w_gate", "w_up", 0), KT),
        ("down1", full("w_down", 4), FKT),
        ("in2", full("w_in_2", 13) + tail("w_in_2", 13 * CW, D_IN2), KT),
        ("out2", full("w_out_2", 4), KT),
        ("ffn2", pairs("w_up_2", "w_up_2", FF), KT),
        ("down2", full("w_down_2", 4), FKT),
        ("proj", full("w_ple_proj_2", 4), PLE // P),
        ("ple", full("w_ple_gate_2", 4), KT),
    ]
    out, chunk, step = {}, 0, 0
    for name, chunks, kt in table:
        s = kt // SK
        out[name] = dict(chunks=chunks, S=s, C=chunk, N=step, end=step + s * len(chunks))
        chunk += len(chunks)
        step += s * len(chunks)
    widths = [c[2] for g in out.values() for c in g["chunks"] for _ in range(g["S"])]
    return out, widths


def two_blocks(nc, a, upto=99):
    G, WIDTH = plan()
    NSTEP = len(WIDTH)

    ctx = ExitStack()
    with ctx:
        def at(name, shape, dt, offset):
            size = int(np.prod(shape[1:])) * (1 if dt == U8 else 4)
            assert offset % 32 == 0 and offset + size <= nc.sbuf_usable_end, (name, offset + size)
            return nc.alloc_sbuf_tensor_at(name, shape, dt, offset=offset)

        STEP_B = SK * CW * 4
        o_ring = (nc.sbuf_base + 63) // 64 * 64
        raw = at("raw", [P, RING, SK * CW], F32, o_ring)
        whi = at("whi", [P, RING, SK * CW], F32R, o_ring + RING * STEP_B)
        wlo = at("wlo", [P, RING, SK * CW], F32R, o_ring + 2 * RING * STEP_B)
        o_h = o_ring + 3 * RING * STEP_B
        H = at("H", [P, NT, D], F32, o_h)
        o_a = o_h + NT * D * 4
        AH = at("AH", [P, KT, TOK], F32R, o_a)
        AL = at("AL", [P, KT, TOK], F32R, o_a + KT * TOK * 4)
        FO = at("FO", [P, NT, D], F32, o_a)
        PH = at("PH", [P, 2, TOK], F32R, o_a + NT * D * 4)
        PL = at("PL", [P, 2, TOK], F32R, o_a + NT * D * 4 + 2048)
        JQ = at("JQ", [P, NT, CW], F32, o_a + NT * D * 4 + 4096)
        o_c = o_a + 2 * KT * TOK * 4
        C = at("C", [P, C_N], F32, o_c)
        o_c += (C_N * 4 + 31) // 32 * 32
        MK = at("MK", [P, len(LEVELS) * P], U8, o_c)
        o_c += len(LEVELS) * P
        VT = at("VT", [P, V_N], F32, o_c)
        o_c += (V_N * 4 + 31) // 32 * 32
        BV = at("BV", [P, B_N], F32, o_c)
        o_c += B_N * 4
        PIN = at("PIN", [P, NT, PLE], F32, o_c)
        o_c += NT * PLE * 4
        ONES = at("ONES", [P, P], F32, o_c)
        o_c += P * 4
        SM = at("SM", [P, 16], F32, o_c)
        o_c += 64
        EPSC = at("EPSC", [P, 8], F32, o_c)
        o_c += 32
        PS = at("PS", [P, NT, 4], F32, o_c)
        o_c += 32
        GP = at("GP", [P, D], F32, o_c)
        o_gp = o_c
        o_b = o_gp + D * 4

        XN = at("XN", [P, NT, D], F32, o_b)
        OH1 = at("OH1", [P, KT, TOK], F32R, o_b)
        OL1 = at("OL1", [P, KT, TOK], F32R, o_b + KT * TOK * 4)
        OH2 = at("OH2", [P, KT, TOK], F32R, o_b + NT * D * 4)
        OL2 = at("OL2", [P, KT, TOK], F32R, o_b + NT * D * 4 + KT * TOK * 4)
        Z1 = at("Z1", [P, NT, D_IN1], F32, o_b)
        o_w = o_b + NT * D_IN1 * 4
        VR = at("VR", [P, 6, P], F32, o_w + 2 * 16384)
        W1K = at("W1K", [P, KT, CMP_HID], F32, o_w)
        W1V = at("W1V", [P, KT, CMP_HID], F32, o_w + 16384)
        XC = at("XC", [P, CK1, TOK], F32, o_w + 2 * 16384)
        XT = at("XT", [P, NT, SSD_W], F32, o_gp)
        BT = at("BT", [P, SSD_G, P], F32, o_w + 2 * 16384 + 12288)
        YOFF = at("YOFF", [P, SSD_W], F32, o_w + 21504)
        KSD = at("KSD", [P, 2, NT, NKV, 2, HD], F32, o_w + 8192)
        JUNK = at("JUNK", [P, NT, SSD_W], F32, o_w)
        YS = at("YS", [P, NT, SSD_W], F32, o_w + 2 * 16384)
        MF = at("MF", [P, len(LEVELS) * P], F32, o_gp)
        YA = at("YA", [P, NT, NH * HD], F32, o_w + 2 * 16384 + 8192)
        KVD = at("KVD", [P, 2, NT, NKV, 2, HD], F32, o_w + 2 * 16384)
        KFK = at("KFK", [P, KT, 60], F32, o_w + 2 * 16384)
        KFV = at("KFV", [P, KT, 60], F32, o_w + 2 * 16384 + 3840)
        o_m = o_w + 2 * 16384 + 2 * 8192
        HK = at("HK", [P, 2, 60], F32, o_m)
        HV = at("HV", [P, 2, NKV, 4, 32], F32, o_w)
        HT_ = at("HT_", [P, 2 * CMP_HID], F32, o_w + 4096)
        RK = at("RK", [P, 4, NKV, ROPE_HALF], F32, o_w + 16384)
        KCT = at("KCT", [P, 60], F32, o_m + 512)
        W2K = at("W2K", [P, 2, 2, HD], F32, o_m + 768)
        W2V = at("W2V", [P, 2, HD], F32, o_m + 1792)
        BD = at("BD", [P, NKV, 4, HD], F32, o_w + 25600)
        SD = at("SD", [P, 16, 16], F32, o_m + 2304)
        AT = at("AT", [P, 256], F32, o_w + 30720)
        M = at("M", [P, NT, SSD_H, P], F32, o_a)
        XD = at("XD", [P, NT, SSD_W], F32, o_a + 16384)
        XS = at("XS", [P, SSD_W], F32, o_a + 24576)
        STA = at("STA", [P, SSD_G, CW], F32, o_a + 28672)
        QT = at("QT", [P, 8, TOK], F32, o_a)
        KTT = at("KTT", [P, 2, NKV, TOK], F32, o_a + 8192)
        S = at("S", [P, 2, 2, 2, TOK], F32, o_a + 16384)
        PT = at("PT", [P, 2, 2, 4, P], F32, o_a + 24576)
        SC = at("SC", [P, NT, NH, NCMP], F32, o_a + 16384)
        PC = at("PC", [P, NT, NH, 32], F32, o_a + 20480)
        PCT = at("PCT", [P, NT, NKV, P], F32, o_a + 24576)
        FH = at("FH", [P, FKT, TOK], F32R, o_b)
        FL = at("FL", [P, FKT, TOK], F32R, o_b + FKT * TOK * 4)
        SG = at("SG", [P, NT, CW], F32, o_gp)
        HT = at("HT", [P, NT, CW], F32, o_gp + 4096)
        UT = at("UT", [P, NT, CW], F32, o_gp)
        GC = at("GC", [P, 4, TOK], F32, o_gp + 4096)
        UC = at("UC", [P, 4, TOK], F32, o_b + 2 * FKT * TOK * 4)
        Z2 = at("Z2", [P, NT, D_IN2], F32, o_b)
        o_y = o_b + NT * D_IN2 * 4
        YF = at("YF", [P, NT, W2], F32, o_y)
        YG = at("YG", [P, NT, W2], F32, o_y + 8192)
        o_t = o_y + 16384
        CB = at("CB", [P, FH_N, TOK], F32, o_a + 16384)
        KF2 = at("KF2", [P, FH_N, TOK], F32, o_a + 8192)
        SF = at("SF", [P, 2, 2, TOK], F32, o_t)
        PF = at("PF", [P, 2, 2, 2, P], F32, o_t + 4096)
        SF_ = at("SF_", [P, 128], F32, o_t + 8192)
        CUM = at("CUM", [P, HG_N * TOK], F32, o_a)
        HQ = at("HQ", [P, HG_N, TOK], F32, o_a + 8192)
        HKT = at("HKT", [P, HG_N, TOK], F32, o_a + 16384)
        LG0 = at("LG0", [P, HG_N * TOK], F32, o_a + 24576)
        LG1 = at("LG1", [P, HG_N * TOK], F32, o_t + 12288)
        LG = [LG0, LG1]
        HS = at("HS", [P, NT, HG_N, P], F32, o_t)
        HX = at("HX", [P, HG_N, P], F32, o_t + 8192)
        HN = at("HN", [P, 64], F32, o_t + 20480)
        MIX = at("MIX", [P, NT, D], F32, o_b)
        E = at("E", [P, NT, D], F32, o_b)
        GS = at("GS", [P, NT, CW], F32, o_b + NT * D * 4 + 2 * KT * TOK * 4)

        pg = ctx.enter_context(nc.psum_tensor("pg", [P, 4, CW], F32))
        pt = ctx.enter_context(nc.psum_tensor("pt", [P, 4, CW], F32))

        def sem(name):
            return ctx.enter_context(nc.semaphore(name))

        raw_landed = [sem(f"raw_landed{i}") for i in range(RING)]
        hi_ready, lo_ready, step_used = sem("hi_ready"), sem("lo_ready"), sem("step_used")
        chunk_out = [sem("chunk_out0"), sem("chunk_out1")]
        dve_chain, act_chain = sem("dve_chain"), sem("act_chain")
        x_landed = [sem(f"x_landed{c}") for c in range(4)]
        ident_landed, const_landed, vec_landed = sem("ident_landed"), sem("const_landed"), sem("vec_landed")
        bc_landed, cmpw_landed, gain_landed = sem("bc_landed"), sem("cmpw_landed"), sem("gain_landed")
        out_landed = sem("out_landed")
        consts_set, vec_turned, vec_ready = sem("consts_set"), sem("vec_turned"), sem("vec_ready")
        ss1, root, rstd_ready = sem("ss1"), sem("root"), sem("rstd_ready")
        sq_ready, gained = sem("sq_ready"), sem("gained")
        xn0, xn1 = sem("xn0"), sem("xn1")
        turned, a_hi, a_lo = sem("turned"), sem("a_hi"), sem("a_lo")
        h_ready, h_block = sem("h_ready"), sem("h_block")
        kv_twice, k_twice = sem("kv_twice"), sem("k_twice")
        kc_turned, kflat, hid_sum, hid_act = sem("kc_turned"), sem("kflat"), sem("hid_sum"), sem("hid_act")
        hv_zero, hid_turned, k_rot = sem("hv_zero"), sem("hid_turned"), sem("k_rot")
        cmp_sum, cmp_kv = sem("cmp_sum"), sem("cmp_kv")
        cv_turned, cv_first, cv_sum, cv_act = sem("cv_turned"), sem("cv_first"), sem("cv_sum"), sem("cv_act")
        xt_turned, xt_a, xt_d = sem("xt_turned"), sem("xt_a"), sem("xt_d")
        dt_exp, dt_u, dt_ln, alog_exp, adt_ready = sem("dt_exp"), sem("dt_u"), sem("dt_ln"), sem("alog_exp"), sem("adt_ready")
        acum_sum, acum_ready, decay_col = sem("acum_sum"), sem("acum_ready"), sem("decay_col")
        row_sum, seg_ready, seg_exp = sem("row_sum"), sem("seg_ready"), sem("seg_exp")
        cb_sum, m_ready, xs_ready = sem("cb_sum"), sem("m_ready"), sem("xs_ready")
        yd_sum, st_sum, st_ready, yo_sum, z_silu, ys_ready = (
            sem("yd_sum"), sem("st_sum"), sem("st_ready"), sem("yo_sum"), sem("z_silu"), sem("ys_ready"))
        q_turned, q_out, cs_sum, cs_ready, cs_exp = sem("q_turned"), sem("q_out"), sem("cs_sum"), sem("cs_ready"), sem("cs_exp")
        pc_ready, pc_turned, pct_ready, oc_sum, oc_out = sem("pc_ready"), sem("pc_turned"), sem("pct_ready"), sem("oc_sum"), sem("oc_out")
        gates, roped, k_turned, k_out = sem("gates"), sem("roped"), sem("k_turned"), sem("k_out")
        s_sum, s_masked, s_max, s_exp = sem("s_sum"), sem("s_masked"), sem("s_max"), sem("s_exp")
        p_turned, p_out0, p_out1, o_sum, o_out = sem("p_turned"), sem("p_out0"), sem("p_out1"), sem("o_sum"), sem("o_out")
        f_turned, f_hi, f_lo = sem("f_turned"), sem("f_hi"), sem("f_lo")
        c_turned, c_first, c_part, c_sum, c_silu, c_prod = (
            sem("c_turned"), sem("c_first"), sem("c_part"), sem("c_sum"), sem("c_silu"), sem("c_prod"))
        lf_exp, lf_ln, lf_ready = sem("lf_exp"), sem("lf_ln"), sem("lf_ready")
        fq_turned, fq_out, fk_out, fc_sum, fc_out = sem("fq_turned"), sem("fq_out"), sem("fk_out"), sem("fc_sum"), sem("fc_out")
        fs_sum, fs_ready, fs_max, fs_exp = sem("fs_sum"), sem("fs_ready"), sem("fs_max"), sem("fs_exp")
        fp_turned, fp_out, fo_sum, fo_out = sem("fp_turned"), sem("fp_out"), sem("fo_sum"), sem("fo_out")
        hg_ln, hg_sig, hg_lf = sem("hg_ln"), sem("hg_sig"), sem("hg_lf")
        hc_sum, hc_out, hq_turned, hq_out, hk_turned, hk_out = (
            sem("hc_sum"), sem("hc_out"), sem("hq_turned"), sem("hq_out"), sem("hk_turned"), sem("hk_out"))
        lv_diff, lv_exp, lv_mul, lv_sum, lv_out = sem("lv_diff"), sem("lv_exp"), sem("lv_mul"), sem("lv_sum"), sem("lv_out")
        ho_sum, ho_out, hg_silu, yg_ready, hn_sq, hn_root = (
            sem("ho_sum"), sem("ho_out"), sem("hg_silu"), sem("yg_ready"), sem("hn_sq"), sem("hn_root"))
        p_tr, p_hi, p_lo, g_sig, e_ready = sem("p_tr"), sem("p_hi"), sem("p_lo"), sem("g_sig"), sem("e_ready")

        ident = C[:, C_ID:C_ID + P]
        tri = C[:, C_TRI:C_TRI + P]
        tri64 = C[:, C_TRI64:C_TRI64 + P]

        def bank4(n):
            return pt[:, n, :].rearrange("p (b c) -> p b c", c=P)

        def bc(ap, *shape):
            return ap.to_broadcast([P, *shape])

        def chunks_read(eng, n):
            for t in range(NT):
                eng.wait_ge(chunk_out[t], n)

        def lv_units(l):
            return 1 + 2 * l

        def lv_banks(u):
            src = (pg, pt)[(u // 2) % 2]
            b = 2 * (u % 2)
            return src[:, b:b + 2, :].rearrange("p b (h n) -> p (b h) n", n=P)

        block = ctx.enter_context(nc.Block())

        @block.sync
        def _(sp):
            def load(dst, src, s):
                sp.dma_start(dst, src).then_inc(s, 16)

            x = a["x"][0].rearrange("(t p) d -> p t d", p=P)
            load(C[:, C_ID:C_ID + P], a["consts"][:, C_ID:C_ID + P], ident_landed)
            load(H[:, :, 0:CW], x[:, :, 0:CW], x_landed[0])
            rows = lambda w, r: w.rearrange("(r p) -> r p", p=P)
            r0 = 0
            for w in ("attn_norm_w", "ffn_norm_w", "g_mix_pre_2", "g_ffn_pre_2", "g_ple_in_2", "ssd_norm_w", "conv_b", "final_norm_w"):
                n = a[w].shape[-1] // P
                load(VR[r0:r0 + n, 0, :], rows(a[w][0] if w != "final_norm_w" else a[w], n), vec_landed)
                r0 += n
            load(VR[0:48, 1, :], a["conv_w"][0].rearrange("j (r p) -> (j r) p", p=P), vec_landed)
            load(VR[48:64, 1, :], a["cmp_pe_k"][0].rearrange("(t l) d -> t (l d)", l=2), vec_landed)
            load(VR[64:80, 1, :], a["cmp_pe_v"][0].rearrange("(t l) d -> t (l d)", l=2), vec_landed)
            for j in range(3):
                load(VR[0:88, 2 + j, :], rows(a["conv_w_2"][0, j], 88), vec_landed)
            load(VR[0:88, 5, :], rows(a["conv_b_2"][0], 88), vec_landed)
            for c in range(1, 4):
                load(H[:, :, c * CW:(c + 1) * CW], x[:, :, c * CW:(c + 1) * CW], x_landed[c])

            def chunk(w, c0, width, j0, j1, s, d):
                for j in range(j0, j1):
                    n = s + j
                    if n >= RING:
                        sp.wait_ge(lo_ready, n - RING + 1 + d)
                    src = a[w][0, j * SK * P:(j + 1) * SK * P, ds(c0, width)].rearrange("(k p) n -> p k n", p=P)
                    dst = raw[:, n % RING, 0:SK * width].rearrange("p (k n) -> p k n", k=SK)
                    load(dst, src, raw_landed[n % RING])

            for name, g in G.items():
                ch, S_, N = g["chunks"], g["S"], g["N"]
                if name in ("ffn1", "ffn2"):
                    (wa, ca, _), (wb, cb, _) = ch[0], ch[1]
                    with sp.Fori(0, NFF) as i:
                        chunk(wa, i * CW + ca, CW, 0, S_, N, i * (2 * S_))
                        chunk(wb, i * CW + cb, CW, 0, S_, N + S_, i * (2 * S_))
                elif name in ("in1", "in2"):
                    n = len(ch) - 2
                    chunk(ch[0][0], 0, CW, 0, S_, N, 0)
                    with sp.Fori(0, n - 1) as i:
                        chunk(ch[0][0], i * CW + CW, CW, 0, S_, N + S_, i * S_)
                    for c in (n, n + 1):
                        chunk(*ch[c], 0, S_, N + c * S_, 0)
                elif S_ == FKT // SK:
                    with sp.Fori(0, 2) as i:
                        chunk(ch[0][0], i * (2 * CW), CW, 0, S_, N, i * (2 * S_))
                        chunk(ch[0][0], i * (2 * CW) + CW, CW, 0, S_, N + S_, i * (2 * S_))
                elif S_ % RING == 0:
                    with sp.Fori(0, len(ch)) as i:
                        chunk(ch[0][0], i * CW, CW, 0, S_, N, i * S_)
                else:
                    for c in range(len(ch)):
                        chunk(*ch[c], 0, S_, N + c * S_, 0)
            if upto >= 99:
                out = a["out"][0].rearrange("(t p) d -> p t d", p=P)
                for c in range(4):
                    sp.wait_ge(h_block, 8 + c + 1)
                    load(out[:, :, c * CW:(c + 1) * CW], H[:, :, c * CW:(c + 1) * CW], out_landed)
                sp.wait_ge(out_landed, 64)

        @block.gpsimd
        def _(pool):
            def load(dst, src, s):
                pool.dma_start(dst, src).then_inc(s, 16)

            pool.memset(ONES[:], 1.0).then_inc(consts_set, 1)
            pool.memset(EPSC[:], EPS).then_inc(consts_set, 1)
            pool.wait_ge(a_lo, KT // 2)
            load(C[:, C_ID + P:C_N], a["consts"][:, C_ID + P:C_N], const_landed)
            load(MF[:], a["masks"], const_landed)
            pool.wait_ge(const_landed, 32)
            pool.tensor_copy(MK[:], MF[:]).then_inc(consts_set, 1)
            load(PIN[:], a["p_2"][0, 0].rearrange("(t p) d -> p t d", p=P), bc_landed)
            for w, o in (("dt_bias", B_DT), ("a_log", B_ALOG), ("d_skip", B_DSK), ("b_fox_f_2", B_BF), ("g_hgrn_out_2", B_GO)):
                n = a[w].shape[-1]
                load(BV[:, o:o + n], a[w][0].partition_broadcast(P), bc_landed)
            load(W1K[:], a["cmp_w1_k"][0].rearrange("(k p) n -> p k n", p=P), cmpw_landed)
            load(W1V[:], a["cmp_w1_v"][0].rearrange("(k p) n -> p k n", p=P), cmpw_landed)
            for i in range(2):
                load(W2K[:, :, i, :], a["cmp_w2_k"][0].rearrange("(k p) n -> p k n", p=P), cmpw_landed)
            load(W2V[:], a["cmp_w2_v"][0].rearrange("(k p) n -> p k n", p=P), cmpw_landed)
            def twice(dst, c0):
                for t in range(NT):
                    for h in range(NKV):
                        src = Z1[:, t, c0 + h * HD:c0 + (h + 1) * HD].unsqueeze(1).to_broadcast([P, 2, HD])
                        ins = pool.tensor_copy(dst[:, t, h], src)
                return ins

            if upto >= 2:
                chunks_read(pool, G["in1"]["C"] + 9)
                pool.wait_ge(xt_turned, 2)
                twice(KVD[:, 0], O_KC)
                twice(KVD[:, 1], O_VC).then_inc(kv_twice, 1)
            if upto >= 3:
                pool.wait_ge(hid_sum, 1)
                pool.memset(HV[:], 0.0).then_inc(hv_zero, 1)
                chunks_read(pool, G["out1"]["C"])
                n = 0
                for o in (O_KS, O_KW):
                    for t in range(NT):
                        x = Z1[:, t, o:o + NKV * HD].rearrange("p (h d) -> p h d", d=HD)
                        x1, x2 = x[:, :, 0:ROPE_HALF], x[:, :, ROPE_HALF:2 * ROPE_HALF]
                        cs = bc(C[:, C_COS + t * ROPE_HALF:C_COS + (t + 1) * ROPE_HALF].unsqueeze(1), NKV, ROPE_HALF)
                        sn = bc(C[:, C_SIN + t * ROPE_HALF:C_SIN + (t + 1) * ROPE_HALF].unsqueeze(1), NKV, ROPE_HALF)
                        pool.tensor_tensor(RK[:, 0], x1, cs, ALU.mult)
                        pool.tensor_tensor(RK[:, 1], x2, sn, ALU.mult)
                        pool.tensor_tensor(RK[:, 2], x2, cs, ALU.mult)
                        pool.tensor_tensor(RK[:, 3], x1, sn, ALU.mult).then_inc(k_rot, 1)
                        n += 1
                        pool.wait_ge(k_rot, n)
                        pool.tensor_tensor(x1, RK[:, 0], RK[:, 1], ALU.subtract)
                        pool.tensor_tensor(x2, RK[:, 2], RK[:, 3], ALU.add).then_inc(k_rot, 1)
                        n += 1
                        pool.wait_ge(k_rot, n)
                twice(KSD[:, 0], O_KS)
                twice(KSD[:, 1], O_KW).then_inc(k_twice, 1)
            if upto >= 10:
                pool.wait_ge(f_lo, NFF)
                load(GP[:], a["final_norm_w"].partition_broadcast(P), gain_landed)
                pool.wait_ge(h_ready, 1)
                load(GP[:], a["g_mix_post_2"][0].partition_broadcast(P), gain_landed)
            if upto >= 18:
                pool.wait_ge(f_lo, 2 * NFF)
                load(GP[:], a["g_ffn_post_2"][0].partition_broadcast(P), gain_landed)
                pool.wait_ge(gained, 8)
                load(GP[:], a["g_ple_post_2"][0].partition_broadcast(P), gain_landed)

        @block.scalar
        def _(act):
            A = nc.scalar.activation
            chain = [0]
            no = lambda *_: None
            norms = {G["in1"]["C"]: 1, G["in2"]["C"]: 5}

            def link(ins):
                chain[0] += 1
                ins.then_inc(act_chain, 1)
                act.wait_ge(act_chain, chain[0])

            def split(n, d=0, w=None):
                if n >= NSTEP:
                    return
                w = SK * (w or WIDTH[n])
                act.wait_ge(raw_landed[n % RING], 16 * (n // RING + 1) + d * (16 // RING))
                if n >= RING:
                    act.wait_ge(step_used, n - RING + 1 + d)
                A(whi[:, n % RING, 0:w], raw[:, n % RING, 0:w], ACT.Copy).then_inc(hi_ready, 1)

            def stream(g, evac, between={}, loop=True):
                S_, N, n = g["S"], g["N"], len(g["chunks"])

                def one(c, dc, dn):
                    for j in range(S_):
                        if isinstance(dc, int):
                            between.get((c, j), no)()
                        split(N + c * S_ + RING + j, dn)
                    evac(c, dc, N + (c + 1) * S_ + dn)

                for c in range(2):
                    one(c, 0, 0)
                loops = uniform_pairs(g)
                if loops > 2 and loop:
                    with act.Fori(0, loops - 1) as i:
                        for c in (2, 3):
                            one(c, i * 2, i * (2 * S_))
                    done = 2 * loops
                else:
                    done = 2
                for c in range(done, n):
                    one(c, 0, 0)


            def evac_copy(dst, g, scale=1.0):
                def f(c, dc, used):
                    b = 2 * ((g["C"] + c) % 2)
                    w = g["chunks"][c][2]
                    if c == 0 and isinstance(dc, int) and g["C"] in norms:
                        act.wait_ge(rstd_ready, norms[g["C"]])
                    act.wait_ge(step_used, used)
                    A(dst[:, 0, ds(dc * CW + g["chunks"][c][1], w)], pg[:, b, 0:w], ACT.Copy, scale=scale).then_inc(chunk_out[0], 1)
                return f

            def evac_squares(g, n0):
                def f(c, dc, used):
                    if c == 3:
                        A(EPSC[:, 2:3], EPSC[:, 0:1], ACT.Sqrt)
                    b = 2 * ((g["C"] + c) % 2)
                    act.wait_ge(step_used, used)
                    if n0 + c:
                        act.wait_ge(sq_ready, n0 + 2 * c)
                    for t in range(NT):
                        A(JQ[:, t, :], pg[:, b + t, :], ACT.Square, accum_out=PS[:, t, c:c + 1]).then_inc(sq_ready, 1)
                return f

            def norm(i, src, n, junk, dst):
                link(A(junk, src, ACT.Square, accum_out=SM[:, 0:1]))
                act.wait_ge(ss1, i + 1)
                A(SM[:, 2:4], SM[:, 0:2], ACT.Sqrt, scale=1.0 / n, bias=EPSC[:, 0:1]).then_inc(root, 1)
                if dst is not None:
                    act.wait_ge(rstd_ready, i + 1)
                    A(dst, src, ACT.Copy, scale=SM[:, 4:5]).then_inc(xn0, 1)

            def post_root(i):
                act.wait_ge(ss1, i + 1)
                A(SM[:, 2:4], SM[:, 0:2], ACT.Sqrt, scale=1.0 / D, bias=EPSC[:, 0:1]).then_inc(root, 1)

            def prep(p, cols, hi, c):
                for g in (2 * c, 2 * c + 1):
                    act.wait_ge(turned, p * 8 + g + 1)
                    src = pt[:, g % 4, :].rearrange("p (k n) -> p k n", k=2)
                    for k in range(2):
                        kt = 2 * g + k
                        w = cols(kt)
                        sc = 1.0 if w is None else VT[:, w:w + 1]
                        ins = A(hi[:, kt, :], src[:, k, :], ACT.Copy, scale=sc)
                    ins.then_inc(a_hi, 1)

            def behind(p, cols, hi):
                return {(c + 1, 1): lambda c=c: prep(p, cols, hi, c) for c in range(3)}

            def silu(g):
                act.wait_ge(cv_sum, g + 1)
                A(XC[:, 2 * g:2 * g + 2, :], XC[:, 2 * g:2 * g + 2, :], ACT.Silu).then_inc(cv_act, 1)

            def conv_tap(g):
                act.wait_ge(cv_turned, g + 1)
                for k in range(2):
                    kt = 2 * g + k
                    ins = A(XC[:, kt, :], pt[:, g % 4, k * TOK:(k + 1) * TOK], ACT.Identity,
                            bias=VT[:, V_CB + kt:V_CB + kt + 1], scale=VT[:, V_CW + 3 * CK1 + kt:V_CW + 3 * CK1 + kt + 1])
                ins.then_inc(cv_first, 1)

            def z_gate():
                chunks_read(act, G["in1"]["C"] + 2)
                A(Z1[:, :, O_Z:O_Z + SSD_W], Z1[:, :, O_Z:O_Z + SSD_W], ACT.Silu).then_inc(z_silu, 1)

            def x_back():
                act.wait_ge(xt_turned, 1)
                act.wait_ge(consts_set, 3)
                for b in range(2):
                    ins = A(XT[:, 0, b * CW:(b + 1) * CW], pt[:, 2 + b, :], ACT.Copy)
                ins.then_inc(xt_a, 1)

            def dt_exps():
                act.wait_ge(dt_u, 1)
                A(SD[:, 2:4, :], SD[:, 2:4, :], ACT.Exp, scale=-1.0).then_inc(dt_exp, 1)
                A(SD[:, 14, :], BV[:, B_ALOG:B_ALOG + 16], ACT.Exp).then_inc(alog_exp, 1)

            def dt_log():
                act.wait_ge(dt_u, 2)
                A(SD[:, 6:8, :], SD[:, 4:6, :], ACT.Ln).then_inc(dt_ln, 1)

            def decays():
                act.wait_ge(acum_ready, 1)
                A(SD[:, 11:13, :], SD[:, 11:13, :], ACT.Exp).then_inc(decay_col, 1)

            def ssd():
                act.wait_ge(hid_sum, 1)
                A(HT_[0:60, :], pt[0:60, 0, :], ACT.Silu).then_inc(hid_act, 1)
                act.wait_ge(seg_ready, 1)
                A(M[:, 0, :, :], M[:, 0, :, :], ACT.Exp).then_inc(seg_exp, 1)
                act.wait_ge(hid_turned, 1)
                hid = pt[:, 1, 0:256].rearrange("p (b c) -> p b c", c=64)
                A(HK[:], hid[:, 0:2, 0:60], ACT.Copy).then_inc(hid_act, 1)
                act.wait_ge(hv_zero, 1)
                for m in range(2):
                    for h in range(NKV):
                        x = hid[:, 2 + m, h * NCMP:(h + 1) * NCMP].unsqueeze(1).to_broadcast([P, 4, NCMP])
                        ins = A(HV[:, m, h, :, 0:NCMP], x, ACT.Copy)
                ins.then_inc(hid_act, 1)
                act.wait_ge(seg_ready, 2)
                A(M[:, 1, :, :], M[:, 1, :, :], ACT.Exp).then_inc(seg_exp, 1)
                act.wait_ge(cmp_sum, 1)
                A(KCT[:], pt[:, 1, 256:316], ACT.Copy).then_inc(cmp_kv, 1)
                act.wait_ge(st_sum, 1)
                A(STA[:], pg[:, 0:2, :], ACT.Copy).then_inc(st_ready, 1)
                act.wait_ge(ys_ready, 1)
                norm(1, YS[:, 0, :], SSD_W, JUNK[:, 0, :], YS[:, 0, :])

            def nsa():
                A(AT[:, 0:96].rearrange("p (t g) -> p t g", t=2), Z1[:, :, O_GATE:O_GATE + 48], ACT.Sigmoid).then_inc(gates, 1)
                act.wait_ge(q_turned, 1)
                A(QT[:, 0:4, :], pt[:, 0:2, :].rearrange("p b (c n) -> p (b c) n", n=TOK), ACT.Copy).then_inc(q_out, 1)
                act.wait_ge(cs_ready, 1)
                A(SC[:], SC[:], ACT.Exp).then_inc(cs_exp, 1)
                act.wait_ge(pc_turned, 1)
                A(PCT[:, 0], bank4(0), ACT.Copy).then_inc(pct_ready, 1)
                act.wait_ge(oc_sum, 1)
                A(YA[:, 0, :].rearrange("p (b n) -> p b n", b=2), pg[:, 2:4, :], ACT.Copy).then_inc(oc_out, 1)
                act.wait_ge(q_turned, 2)
                A(QT[:, 0:4, :], pg[:, 0:2, :].rearrange("p b (c n) -> p (b c) n", n=TOK), ACT.Copy).then_inc(q_out, 1)
                act.wait_ge(k_turned, 1)
                A(KTT[:, 0, :, :], pt[:, 0:2, :].rearrange("p b (c n) -> p (b c) n", n=TOK), ACT.Copy).then_inc(k_out, 1)
                for u in range(17):
                    if u < 16:
                        nk = P * (1 + units[u][1])
                        act.wait_ge(s_max, u + 1)
                        for j in range(4):
                            x = S[:, u % 2, j // 2, j % 2, 0:nk]
                            ins = A(x, x, ACT.Exp, bias=NM[:, 4 * u + j:4 * u + j + 1], scale=HD ** -0.5,
                                    accum_out=SUM[:, 4 * u + j:4 * u + j + 1])
                        ins.then_inc(s_exp, 1)
                    if u >= 1:
                        act.wait_ge(p_turned, u)
                        if u >= 3:
                            act.wait_ge(o_sum, u - 2)
                        A(PT[:, (u - 1) % 2, 0], bank4(0), ACT.Copy).then_inc(p_out0, 1)

            units = [(b, t, kv) for b in range(2) for t in range(NT) for kv in range(NKV)]
            NM = AT[:, 96:160]
            SUM = AT[:, 160:224]

            def ffn(g, hooks, between):
                N, S_ = g["N"], g["S"]

                def pair(c, d, between={}):
                    for h in range(4):
                        hooks[h](c, d)
                        for j in range(4):
                            between.get(4 * h + j, no)()
                            split(N + c * 16 + 4 * (h + 1) + j, d * 16, CW)

                pair(0, 0, between)
                with act.Fori(0, NFF - 1) as i:
                    pair(1, i)

            def down(g, hooks, evac, between={}):
                N, S_, n = g["N"], g["S"], len(g["chunks"])
                for c in range(n):
                    for j in range(S_):
                        if c == 0 and j % 4 == 0 and j // 4 < len(hooks):
                            hooks[j // 4]()
                        between.get((c, j), no)()
                        split(N + c * S_ + RING + j)
                    evac(c, 0, N + (c + 1) * S_)

            F1, F2 = G["ffn1"], G["ffn2"]

            def f1_hi(c, d):
                act.wait_ge(f_turned, c + d)
                A(FH[:, ds((d + c - 1) * 4, 4), :], pt[:, 0:2, :].rearrange("p b (c n) -> p (b c) n", n=TOK), ACT.Copy)\
                    .then_inc(f_hi, 1)

            def f1_silu(c, d):
                b = 2 * (F1["C"] % 2)
                act.wait_ge(step_used, F1["N"] + 16 * c + 8 + d * 16)
                if c:
                    chunks_read(act, F1["C"] + 2 * c + d * 2)
                for t in range(NT):
                    A(SG[:, t, :], pg[:, b + t, :], ACT.Silu, scale=SM[:, 4 + t:5 + t]).then_inc(chunk_out[t], 1)

            def f2_up(c, d):
                b = 2 * ((F2["C"] + 1) % 2)
                act.wait_ge(step_used, F2["N"] + 16 * c + d * 16)
                act.wait_ge(c_turned, 2 * c - 1 + d * 2)
                A(UT[:, 0, :], pg[:, b, :], ACT.Copy, scale=SM[:, 4:5]).then_inc(chunk_out[0], 1)
                act.wait_ge(c_sum, 2 * c - 1 + d * 2)
                A(GC[:], GC[:], ACT.Silu).then_inc(c_silu, 1)

            def conv_first(src, dst, k0):
                for k in range(4):
                    ins = A(dst[:, k, :], src[:, k, :], ACT.Identity, bias=VT[:, ds(k0 + V_CB2 + k, 1)],
                            scale=VT[:, ds(k0 + V_CW2 + 2 * 88 + k, 1)])
                ins.then_inc(c_first, 1)

            def f2_conv_up(c, d):
                act.wait_ge(c_turned, 2 * c + d * 2)
                conv_first(pt[:, 2:4, :].rearrange("p b (c n) -> p (b c) n", n=TOK), UC, d * 4 + (c - 1) * 4 + FKT)

            def f2_gate(c, d):
                b = 2 * (F2["C"] % 2)
                act.wait_ge(step_used, F2["N"] + 16 * c + 8 + d * 16)
                if c:
                    act.wait_ge(c_turned, 2 * c + d * 2)
                A(UT[:, 0, :], pg[:, b, :], ACT.Copy, scale=SM[:, 4:5]).then_inc(chunk_out[0], 1)

            def f2_hi(c, d):
                act.wait_ge(c_prod, c + d)
                A(FH[:, ds((d + c - 1) * 4, 4), :], UC[:], ACT.Copy).then_inc(f_hi, 1)

            def f2_conv_gate(c, d):
                act.wait_ge(c_turned, 2 * c + 1 + d * 2)
                if c:
                    act.wait_ge(c_prod, c + d)
                conv_first(pt[:, 0:2, :].rearrange("p b (c n) -> p (b c) n", n=TOK), GC, d * 4 + c * 4)

            def after(f):
                return lambda c, d: f(c, d) if c else None

            def fox():
                act.wait_ge(lf_ready, 1)
                A(SF_[:, 16:32], SF_[:, 16:32], ACT.Exp, scale=-1.0).then_inc(lf_exp, 1)
                act.wait_ge(lf_exp, 1)
                A(SF_[:, 16:32], SF_[:, 16:32], ACT.Ln, bias=1.0).then_inc(lf_ln, 1)
                act.wait_ge(fq_turned, 1)
                A(QT[:], pt[:].rearrange("p b (c n) -> p (b c) n", n=TOK), ACT.Copy).then_inc(fq_out, 1)
                act.wait_ge(fc_sum, 1)
                A(CB[:], pt[:].rearrange("p b (c n) -> p (b c) n", n=TOK), ACT.Copy, scale=-1.0).then_inc(fc_out, 1)
                for u in range(9):
                    if u < 8:
                        nk = P * (1 + u // 4)
                        act.wait_ge(fs_max, u + 1)
                        for j in range(2):
                            x = SF[:, u % 2, j, 0:nk]
                            ins = A(x, x, ACT.Exp, bias=SF_[:, 64 + 2 * u + j:65 + 2 * u + j], scale=1.0,
                                    accum_out=SF_[:, 80 + 2 * u + j:81 + 2 * u + j])
                        ins.then_inc(fs_exp, 1)
                    if u >= 1:
                        t = (u - 1) // 4
                        act.wait_ge(fp_turned, u)
                        if u >= 3:
                            act.wait_ge(fo_sum, u - 2)
                        A(PF[:, (u - 1) % 2, :, 0:t + 1, :],
                          bank4((u - 1) % 2).rearrange("p (j k) n -> p j k n", j=2)[:, :, 0:t + 1, :], ACT.Copy).then_inc(fp_out, 1)

            def hgrn():
                f = Z2[:, :, O2_HF:O2_HF + W2]
                act.wait_ge(fo_out, 8)
                A(YG[:], f, ACT.Sigmoid, scale=-1.0).then_inc(hg_sig, 1)
                tmp = LG1[:].rearrange("p (t n) -> p t n", t=2)
                link(A(tmp, f, ACT.Abs))
                link(A(tmp, tmp, ACT.Exp, scale=-1.0))
                A(tmp, tmp, ACT.Ln, bias=1.0).then_inc(hg_ln, 1)
                A(Z2[:, :, O2_HG:O2_HG + W2], Z2[:, :, O2_HG:O2_HG + W2], ACT.Silu).then_inc(hg_silu, 1)
                act.wait_ge(hk_turned, 1)
                A(HKT[:], pt[:].rearrange("p b (c n) -> p (b c) n", n=TOK), ACT.Copy).then_inc(hk_out, 1)
                act.wait_ge(hc_sum, 1)
                A(CUM[:].rearrange("p (b n) -> p b n", b=4), pt[:], ACT.Copy).then_inc(hc_out, 1)
                for l in range(8):
                    act.wait_ge(lv_diff, l + 1)
                    if l == 0:
                        q2 = lambda x: x[:].rearrange("p (h a n) -> p h a n", h=8, a=4)[:, :, 2, :]
                        A(q2(LG0), q2(CUM), ACT.Exp)
                        x = LG0[:].rearrange("p (h a n) -> p h a n", h=8, a=4)
                        A(x[:, :, 0:2, :], x[:, :, 0:2, :], ACT.Exp)
                        A(x[:, :, 3, :], x[:, :, 3, :], ACT.Exp).then_inc(lv_exp, 1)
                    elif l == 1:
                        x = LG1[:].rearrange("p (h t a n) -> p (h t) a n", h=8, t=2, a=2)
                        y = CUM[:].rearrange("p (h t a n) -> p (h t) a n", h=8, t=2, a=2)
                        A(x[:, :, 0, :], x[:, :, 0, :], ACT.Exp)
                        A(x[:, :, 1, :], y[:, :, 1, :], ACT.Exp).then_inc(lv_exp, 1)
                    else:
                        A(LG[l % 2][:], LG[l % 2][:], ACT.Exp).then_inc(lv_exp, 1)
                act.wait_ge(ho_sum, 1)
                A(YG[:], pt[:].rearrange("p (t b) n -> p t (b n)", t=2), ACT.Copy).then_inc(ho_out, 1)
                act.wait_ge(hn_sq, 1)
                A(HN[:, 16:32], HN[:, 0:16], ACT.Sqrt, scale=1.0 / P, bias=EPSC[:, 0:1]).then_inc(hn_root, 1)

            for n in range(RING):
                split(n)
            act.wait_ge(consts_set, 2)
            act.wait_ge(vec_ready, 3)
            pre0 = lambda c: lambda: prep(0, lambda k: V_ATTN + k, AH, c)
            pre0(0)()
            pre0(1)()
            stream(G["in1"], evac_copy(Z1, G["in1"], SM[:, 4:5]), {
                (0, 1): pre0(2), (0, 2): pre0(3), (0, 4): lambda: norm(0, H[:, 0, :], D, XN[:, 0, :], None),
                (3, 1): lambda: (conv_tap(0), conv_tap(1)), (3, 3): lambda: (silu(0), silu(1)), (3, 5): z_gate,
                (4, 1): lambda: (conv_tap(2), conv_tap(3)), (4, 3): lambda: (silu(2), silu(3)),
                (5, 1): lambda: (conv_tap(4), conv_tap(5)), (5, 3): lambda: (silu(4), silu(5)), (5, 5): x_back,
                (6, 4): dt_exps, (6, 6): dt_log, (7, 4): decays,
            }, loop=False)
            if upto < 3: return
            ssd()
            if upto < 4: return
            nsa()
            if upto < 5: return
            act.wait_ge(o_out, 16)
            mix1 = lambda c: lambda: prep(1, lambda k: V_SSD + k if k < 8 else None, OH1, c)
            f1_in = lambda c: lambda: prep(2, lambda k: V_FFN + k, AH, c)
            mix1(0)()
            mix1(1)()
            stream(G["out1"], no, {(0, 1): mix1(2), (0, 2): mix1(3), (1, 1): f1_in(0), (2, 1): f1_in(1), (3, 1): f1_in(2)})
            if upto < 8: return

            def norm_ffn1():
                chunks_read(act, F1["C"])
                norm(2, H[:, 0, :], D, XN[:, 0, :], None)
                act.wait_ge(rstd_ready, 3)

            ffn(F1, [no, after(f1_hi), f1_silu, no], {1: f1_in(3), 3: norm_ffn1})
            if upto < 9: return
            in2 = lambda c: lambda: prep(3, lambda k: V_GMIX + k, AH, c)
            down(G["down1"], [no, lambda: f1_hi(NFF, 0)], no, {(1, 1): in2(0), (2, 1): in2(1), (3, 1): in2(2)})
            if upto < 10: return

            def norm_final():
                chunks_read(act, G["in2"]["C"])
                norm(3, H[:, 0, :], D, XN[:, 0, :], None)

            def norm_mix():
                act.wait_ge(h_ready, 1)
                norm(4, H[:, 0, :], D, XN[:, 0, :], None)

            stream(G["in2"], evac_copy(Z2, G["in2"], SM[:, 4:5]), {(0, 1): in2(3), (0, 2): norm_final, (0, 5): norm_mix})
            if upto < 12: return
            chunks_read(act, G["out2"]["C"])
            fox()
            if upto < 13: return
            hgrn()
            if upto < 14: return
            act.wait_ge(yg_ready, 1)
            mix2 = lambda c: lambda: prep(4, lambda k: None, OH2, c)
            mix2(0)()
            mix2(1)()
            stream(G["out2"], evac_squares(G["out2"], 0), {(0, 1): mix2(2), (0, 2): mix2(3)})
            post_root(5)
            f2_in = lambda c: lambda: prep(5, lambda k: V_GFFN + k, AH, c)

            def norm_ffn2():
                act.wait_ge(h_block, 4)
                norm(6, H[:, 0, :], D, XN[:, 0, :], None)
                act.wait_ge(rstd_ready, 7)

            f2_in(0)()
            f2_in(1)()
            if upto < 17: return
            ffn(F2, [after(f2_up), after(f2_conv_up), lambda c, d: (f2_gate(c, d), after(f2_hi)(c, d)), f2_conv_gate],
                {1: f2_in(2), 2: f2_in(3), 4: norm_ffn2})

            def p_parts():
                act.wait_ge(p_tr, 1)
                A(PH[:], pt[:, 3, :].rearrange("p (k n) -> p k n", k=2), ACT.Copy).then_inc(p_hi, 1)

            down(G["down2"], [lambda: f2_up(NFF, 0), lambda: f2_conv_up(NFF, 0), no, lambda: f2_hi(NFF, 0)],
                 evac_squares(G["down2"], 8), {(1, 2): p_parts})
            if upto < 18: return
            post_root(7)
            for c in range(4):
                evac_copy(E, G["proj"])(c, 0, G["proj"]["N"] + c + 1)
                split(G["ple"]["N"] + c)
            ple_in = lambda c: lambda: prep(6, lambda k: V_GPLE + k, OH2, c)

            def norm_ple():
                act.wait_ge(h_block, 8)
                norm(8, H[:, 0, :], D, FO[:, 0, :], None)
                act.wait_ge(rstd_ready, 9)

            ple_in(0)()
            ple_in(1)()
            between = {(0, 1): ple_in(2), (0, 2): ple_in(3), (0, 4): norm_ple}

            def e_squares(c):
                act.wait_ge(e_ready, 2 * c + 2)
                act.wait_ge(sq_ready, 16 + 2 * c)
                for t in range(NT):
                    A(JQ[:, t, :], E[:, t, c * CW:(c + 1) * CW], ACT.Square, accum_out=PS[:, t, c:c + 1]).then_inc(sq_ready, 1)

            g = G["ple"]
            for c in range(4):
                for j in range(8):
                    between.get((c, j), no)()
                    split(g["N"] + c * 8 + RING + j)
                b = 2 * ((g["C"] + c) % 2)
                if c:
                    e_squares(c - 1)
                act.wait_ge(step_used, g["N"] + (c + 1) * 8)
                for t in range(NT):
                    A(GS[:, t, :], pg[:, b + t, :], ACT.Sigmoid, scale=SM[:, 4 + t:5 + t]).then_inc(chunk_out[t], 1)
            A(EPSC[:, 2:3], EPSC[:, 0:1], ACT.Sqrt)
            e_squares(3)
            post_root(9)

        @block.vector
        def _(dve):
            V = nc.vector
            chain = [0]
            no = lambda *_: None
            norms = {G["in1"]["C"]: 1, G["in2"]["C"]: 5}

            def link(ins):
                chain[0] += 1
                ins.then_inc(dve_chain, 1)
                dve.wait_ge(dve_chain, chain[0])

            def split(n, d=0, w=None):
                if n >= NSTEP:
                    return
                w = SK * (w or WIDTH[n])
                dve.wait_ge(hi_ready, n + 1 + d)
                V.tensor_tensor(wlo[:, n % RING, 0:w], raw[:, n % RING, 0:w], whi[:, n % RING, 0:w].bitcast(F32),
                                ALU.subtract).then_inc(lo_ready, 1)

            def stream(g, evac, between={}, loop=True):
                S_, N, n = g["S"], g["N"], len(g["chunks"])

                def one(c, dc, dn):
                    for j in range(S_):
                        if isinstance(dc, int):
                            between.get((c, j), no)()
                        split(N + c * S_ + RING + j, dn)
                    evac(c, dc, N + (c + 1) * S_ + dn)

                for c in range(2):
                    one(c, 0, 0)
                loops = uniform_pairs(g)
                if loops > 2 and loop:
                    with dve.Fori(0, loops - 1) as i:
                        for c in (2, 3):
                            one(c, i * 2, i * (2 * S_))
                    done = 2 * loops
                else:
                    done = 2
                for c in range(done, n):
                    one(c, 0, 0)

            def evac_copy(dst, g, scaled=False):
                def f(c, dc, used):
                    b = 2 * ((g["C"] + c) % 2)
                    w = g["chunks"][c][2]
                    dve.wait_ge(step_used, used)
                    x = dst[:, 1, ds(dc * CW + g["chunks"][c][1], w)]
                    if scaled:
                        ins = V.tensor_scalar(x, pg[:, b + 1, 0:w], SM[:, 5:6], None, ALU.mult)
                    else:
                        ins = V.tensor_copy(x, pg[:, b + 1, 0:w])
                    ins.then_inc(chunk_out[1], 1)
                return f

            def evac_gained(dst, g, n0):
                def f(c, dc, used):
                    b = 2 * ((g["C"] + c) % 2)
                    if c == 0:
                        dve.wait_ge(gain_landed, 32 if n0 == 0 else 48)
                    for t in range(NT):
                        dve.wait_ge(sq_ready, n0 + 2 * c + t + 1)
                        ins = V.tensor_tensor(dst[:, t, c * CW:(c + 1) * CW], pg[:, b + t, :], GP[:, c * CW:(c + 1) * CW], ALU.mult)
                        ins.then_inc(chunk_out[t], 1)
                    V.memset(SM[:, 12:13], 0.0).then_inc(gained, 1)
                return f

            def evac_add(g):
                def f(c, dc, used):
                    b = 2 * ((g["C"] + c) % 2)
                    dve.wait_ge(step_used, used)
                    for t in range(NT):
                        x = H[:, t, ds(dc * CW + c * CW, CW)]
                        V.tensor_tensor(x, pg[:, b + t, :], x, ALU.add).then_inc(chunk_out[t], 1)
                return f

            def refine(y, aa, root_, t1):
                link(V.reciprocal(y, root_))
                link(V.tensor_tensor(t1, y, y, ALU.mult))
                link(V.tensor_tensor(t1, t1, aa, ALU.mult))
                link(V.tensor_scalar(t1, t1, -0.5, 1.5, ALU.mult, ALU.add))

            def rstd(i, n, before=False):
                dve.wait_ge(root, i + 1)
                link(V.tensor_scalar(SM[:, 6:8], SM[:, 0:2], 1.0 / n, EPS, ALU.mult, ALU.add))
                refine(SM[:, 8:10], SM[:, 6:8], SM[:, 2:4], SM[:, 10:12])
                if before:
                    link(V.tensor_tensor(SM[:, 10:12], SM[:, 10:12], SM[:, 4:6], ALU.mult))
                V.tensor_tensor(SM[:, 4:6], SM[:, 8:10], SM[:, 10:12], ALU.mult).then_inc(rstd_ready, 1)
                dve.wait_ge(rstd_ready, i + 1)

            def norm(i, src, n, junk, dst, before=False):
                V.tensor_tensor_reduce(junk, src, src, 1.0, 0.0, ALU.mult, ALU.add, SM[:, 1:2]).then_inc(ss1, 1)
                rstd(i, n, before)
                if dst is not None:
                    V.tensor_scalar(dst, src, SM[:, 5:6], None, ALU.mult).then_inc(xn1, 1)

            def post_sums(n):
                dve.wait_ge(sq_ready, n)
                V.tensor_reduce(SM[:, 0:2], PS[:], AX.X, ALU.add).then_inc(ss1, 1)

            def post_add(x, c):
                for t in range(NT):
                    h = H[:, t, c * CW:(c + 1) * CW]
                    ins = V.scalar_tensor_tensor(h, x[:, t, c * CW:(c + 1) * CW], SM[:, 4 + t:5 + t], h, ALU.mult, ALU.add)
                ins.then_inc(h_block, 1)

            def prep(p, cols, hi, lo, c):
                for g in (2 * c, 2 * c + 1):
                    dve.wait_ge(a_hi, p * 8 + g + 1)
                    src = pt[:, g % 4, :].rearrange("p (k n) -> p k n", k=2)
                    for k in range(2):
                        kt = 2 * g + k
                        w = cols(kt)
                        sc = 1.0 if w is None else VT[:, w:w + 1]
                        ins = V.scalar_tensor_tensor(lo[:, kt, :], src[:, k, :], sc, hi[:, kt, :].bitcast(F32),
                                                     ALU.mult, ALU.subtract)
                    ins.then_inc(a_lo, 1)

            def kv_flat(b):
                dst, pe_ = (KFK, V_PEK) if b < 2 else (KFV, V_PEV)
                h0 = 2 * (b % 2)
                dve.wait_ge(kc_turned, 4)
                for l in range(2):
                    pr = slice(64 * l, 64 * l + 64)
                    src = pt[pr, b, :].rearrange("p (h a t l) -> p l h t a", h=2, l=2, t=8)[:, l]
                    for th in range(2):
                        for h in range(2):
                            o = dst[pr, 8 * th:8 * th + 8, (h0 + h) * NCMP:(h0 + h + 1) * NCMP]
                            pe2 = VT[pr, pe_ + 8 * th:pe_ + 8 * th + 8].unsqueeze(2).to_broadcast([64, 8, NCMP])
                            ins = V.tensor_tensor(o, src[:, h, :, th:th + NCMP], pe2, ALU.add)
                ins.then_inc(kflat, 1)

            def conv(g):
                dve.wait_ge(cv_first, g + 1)
                for j in (2, 1, 0):
                    for k in range(2):
                        kt = 2 * g + k
                        w = V_CW + j * CK1 + kt
                        x = XC[:, kt, 3 - j:TOK]
                        ins = V.scalar_tensor_tensor(x, pt[:, g % 4, k * TOK:k * TOK + TOK - 3 + j], VT[:, w:w + 1], x,
                                                     ALU.mult, ALU.add)
                    if j:
                        link(ins)
                ins.then_inc(cv_sum, 1)

            dt2 = lambda o: SD[:, o:o + 2, :]

            def dt_abs():
                dve.wait_ge(bc_landed, 96)
                chunks_read(dve, G["in1"]["C"] + 6)
                bias = bc(BV[:, B_DT:B_DT + 16].unsqueeze(1), 2, 16)
                link(V.tensor_tensor(dt2(0), Z1[:, :, O_DT:O_DT + 16], bias, ALU.add))
                V.scalar_tensor_tensor(dt2(2), dt2(0), -1.0, dt2(0), ALU.mult, ALU.max).then_inc(dt_u, 1)
                link(V.tensor_scalar(dt2(0), dt2(0), 0.0, None, ALU.max))

            def dt_plus():
                dve.wait_ge(dt_exp, 1)
                V.tensor_scalar(dt2(4), dt2(2), 1.0, None, ALU.add).then_inc(dt_u, 1)
                dve.wait_ge(dt_u, 2)
                link(V.tensor_scalar(dt2(8), dt2(4), -1.0, None, ALU.add))

            def dt_rest():
                dve.wait_ge(dt_ln, 1)
                link(V.tensor_scalar(dt2(4), dt2(8), 0.0, None, ALU.is_equal))
                link(V.tensor_tensor(dt2(8), dt2(8), dt2(4), ALU.add))
                link(V.tensor_tensor(dt2(6), dt2(6), dt2(4), ALU.add))
                link(V.reciprocal(dt2(8), dt2(8)))
                link(V.tensor_tensor(dt2(6), dt2(6), dt2(8), ALU.mult))
                link(V.tensor_tensor(dt2(6), dt2(6), dt2(2), ALU.mult))
                link(V.tensor_tensor(dt2(0), dt2(0), dt2(6), ALU.add))
                dve.wait_ge(alog_exp, 1)
                link(V.tensor_scalar(dt2(4), dt2(0), -1.0, None, ALU.mult))
                V.tensor_tensor(dt2(2), dt2(4), bc(SD[:, 14, :].unsqueeze(1), 2, 16), ALU.mult).then_inc(adt_ready, 1)

            def x_back():
                dve.wait_ge(xt_turned, 2)
                V.tensor_copy(BT[:].rearrange("p g n -> p (g n)"), pt[:, 2, 0:256])
                for b in range(2):
                    ins = V.tensor_copy(XT[:, 1, b * CW:(b + 1) * CW], pt[:, b, :])
                ins.then_inc(xt_d, 1)

            def a_sums():
                dve.wait_ge(acum_sum, 1)
                link(V.tensor_copy(dt2(8), pt[:, 3, 0:32].rearrange("p (t h) -> p t h", t=2)))
                link(V.tensor_copy(SD[:, 12, :], SD[:, 9, :]))
                V.tensor_tensor(SD[:, 11, :], pt[:, 3, 32:48], SD[:, 8, :], ALU.subtract).then_inc(acum_ready, 1)

            def ssd():
                dve.wait_ge(xt_a, 1)
                dve.wait_ge(xt_d, 1)
                for t in range(NT):
                    ins = V.tensor_tensor(XD[:, t, :].rearrange("p (h d) -> p h d", d=HD),
                                          XT[:, t, :].rearrange("p (h d) -> p h d", d=HD),
                                          bc(SD[:, t, :].unsqueeze(2), 16, HD), ALU.mult)
                link(ins)
                dve.wait_ge(decay_col, 1)
                V.tensor_tensor(XS[:].rearrange("p (h d) -> p h d", d=HD), XD[:, 0, :].rearrange("p (h d) -> p h d", d=HD),
                                bc(SD[:, 11, :].unsqueeze(2), 16, HD), ALU.mult).then_inc(xs_ready, 1)
                for t in range(NT):
                    dve.wait_ge(row_sum, t + 1)
                    for b in range(4):
                        ins = V.tensor_tensor(M[:, t, 4 * b:4 * b + 4, :], pg[:, b, :].rearrange("p (h n) -> p h n", h=4),
                                              bc(C[:, C_NEGT:C_NEGT + P].unsqueeze(1), 4, P), ALU.add)
                    link(ins)
                    V.tensor_tensor(M[:, t, :, :], M[:, t, :, :], bc(SD[:, 8 + t, :].unsqueeze(2), 16, P), ALU.subtract)\
                        .then_inc(seg_ready, 1)
                dve.wait_ge(cb_sum, 1)
                for t in range(NT):
                    dve.wait_ge(seg_exp, t + 1)
                    for g in range(SSD_G):
                        cb = pt[:, 3, (2 * t + g) * P:(2 * t + g + 1) * P]
                        ins = V.tensor_tensor(M[:, t, 8 * g:8 * g + 8, :], M[:, t, 8 * g:8 * g + 8, :], bc(cb.unsqueeze(1), 8, P),
                                              ALU.mult)
                    ins.then_inc(m_ready, 1)
                dve.wait_ge(cmp_sum, 1)
                for h in range(NKV):
                    V.tensor_tensor(BD[:, h, :, :], bc(pt[:, 2, h * HD:(h + 1) * HD].unsqueeze(1), 4, HD),
                                    bc(C[:, C_BLK:C_BLK + 4].unsqueeze(2), 4, HD), ALU.mult).then_inc(cmp_kv, 1)
                for t in range(NT):
                    ins = V.tensor_tensor(YS[:, t, :].rearrange("p (h d) -> p h d", d=HD),
                                          XT[:, t, :].rearrange("p (h d) -> p h d", d=HD),
                                          bc(BV[:, B_DSK:B_DSK + 16].unsqueeze(2), 16, HD), ALU.mult)
                link(ins)
                for t in range(NT):
                    dve.wait_ge(yd_sum, t + 1)
                    for b in range(2):
                        x = YS[:, t, b * CW:(b + 1) * CW]
                        ins = V.tensor_tensor(x, pt[:, 2 * t + b, :], x, ALU.add)
                dve.wait_ge(yo_sum, 1)
                for b in range(2):
                    ins = V.tensor_tensor(YOFF[:, b * CW:(b + 1) * CW].rearrange("p (h d) -> p h d", d=HD),
                                          pg[:, 2 + b, :].rearrange("p (h d) -> p h d", d=HD),
                                          bc(SD[:, 12, 8 * b:8 * b + 8].unsqueeze(2), 8, HD), ALU.mult)
                link(ins)
                link(V.tensor_tensor(YS[:, 1, :], YS[:, 1, :], YOFF[:], ALU.add))
                dve.wait_ge(z_silu, 1)
                V.tensor_tensor(YS[:], YS[:], Z1[:, :, O_Z:O_Z + SSD_W], ALU.mult).then_inc(ys_ready, 1)
                dve.wait_ge(ys_ready, 1)
                norm(1, YS[:, 1, :], SSD_W, JUNK[:, 1, :], YS[:, 1, :])

            units = [(b, t, kv) for b in range(2) for t in range(NT) for kv in range(NKV)]
            NM = AT[:, 96:160]
            SUM = AT[:, 160:224]

            RT = XT[:, 0, 0:512].rearrange("p (a h d) -> p a h d", a=4, h=16)
            CM = XT[:, 0, 512:512 + NT * NCMP]
            CX = XT[:, 0, 600:664]
            OT = XT[:, 0, 704:960].rearrange("p (h d) -> p h d", d=HD)

            def nsa():
                V.memset(PC[:], 0.0)
                dve.wait_ge(q_turned, 1)
                V.tensor_copy(QT[:, 4:8, :], pt[:, 2:4, :].rearrange("p b (c n) -> p (b c) n", n=TOK)).then_inc(q_out, 1)
                for o, h in ((O_Q, NH),):
                    for t in range(NT):
                        x = Z1[:, t, o:o + h * HD].rearrange("p (h d) -> p h d", d=HD)
                        x1, x2 = x[:, :, 0:ROPE_HALF], x[:, :, ROPE_HALF:2 * ROPE_HALF]
                        cs = bc(C[:, C_COS + t * ROPE_HALF:C_COS + (t + 1) * ROPE_HALF].unsqueeze(1), h, ROPE_HALF)
                        sn = bc(C[:, C_SIN + t * ROPE_HALF:C_SIN + (t + 1) * ROPE_HALF].unsqueeze(1), h, ROPE_HALF)
                        tmp = [RT[:, i, 0:h, :] for i in range(4)]
                        V.tensor_tensor(tmp[0], x1, cs, ALU.mult)
                        V.tensor_tensor(tmp[1], x2, sn, ALU.mult)
                        V.tensor_tensor(tmp[2], x2, cs, ALU.mult)
                        link(V.tensor_tensor(tmp[3], x1, sn, ALU.mult))
                        V.tensor_tensor(x1, tmp[0], tmp[1], ALU.subtract)
                        link(V.tensor_tensor(x2, tmp[2], tmp[3], ALU.add))
                V.memset(RT[:, 0, 0, 0:1], 0.0).then_inc(roped, 1)
                dve.wait_ge(cs_sum, 1)
                sc = SC[:].rearrange("p t (h e) i -> p t e h i", e=2)
                for t in range(NT):
                    mask = C[:, C_CMP + t * NCMP:C_CMP + (t + 1) * NCMP]
                    for e in range(2):
                        ins = V.scalar_tensor_tensor(sc[:, t, e], pg[:, e, t * 128:t * 128 + 128].rearrange("p (h i) -> p h i", i=16)[:, :, 0:NCMP],
                                                     HD ** -0.5, bc(mask.unsqueeze(1), 8, NCMP), ALU.mult, ALU.mult)
                link(ins)
                link(V.tensor_scalar(CM[:], C[:, C_CMP:C_CMP + NT * NCMP], 1.0, 1e30, ALU.subtract, ALU.mult))
                for t in range(NT):
                    ins = V.tensor_tensor(SC[:, t], SC[:, t], bc(CM[:, t * NCMP:(t + 1) * NCMP].unsqueeze(1), 16, NCMP), ALU.add)
                link(ins)
                flat = SC[:].rearrange("p t h i -> p (t h) i")
                link(V.tensor_reduce(CX[:, 0:32], flat, AX.X, ALU.max))
                V.tensor_tensor(flat, flat, bc(CX[:, 0:32].unsqueeze(2), 32, NCMP), ALU.subtract).then_inc(cs_ready, 1)
                dve.wait_ge(cs_exp, 1)
                link(V.tensor_reduce(CX[:, 32:64], flat, AX.X, ALU.add))
                link(V.reciprocal(CX[:, 0:32], CX[:, 32:64]))
                dve.wait_ge(gates, 1)
                link(V.tensor_tensor(CX[:, 32:64], CX[:, 0:32], AT[:, 0:96].rearrange("p (n g) -> p n g", g=3)[:, :, 0], ALU.mult))
                link(V.tensor_tensor(flat, flat, bc(CX[:, 32:64].unsqueeze(2), 32, NCMP), ALU.mult))
                for t in range(NT):
                    ins = V.tensor_tensor(PC[:, t, :, 0:NCMP], SC[:, t], bc(C[:, C_CMP + t * NCMP:C_CMP + (t + 1) * NCMP].unsqueeze(1), 16, NCMP),
                                          ALU.mult)
                ins.then_inc(pc_ready, 1)
                dve.wait_ge(pc_turned, 1)
                V.tensor_copy(PCT[:, 1], bank4(1)).then_inc(pct_ready, 1)
                dve.wait_ge(oc_sum, 1)
                V.tensor_copy(YA[:, 1, :].rearrange("p (b n) -> p b n", b=2), pt[:, 2:4, :]).then_inc(oc_out, 1)
                dve.wait_ge(q_turned, 2)
                V.tensor_copy(QT[:, 4:8, :], pg[:, 2:4, :].rearrange("p b (c n) -> p (b c) n", n=TOK)).then_inc(q_out, 1)
                dve.wait_ge(k_turned, 1)
                V.tensor_copy(KTT[:, 1, :, :], pt[:, 2:4, :].rearrange("p b (c n) -> p (b c) n", n=TOK)).then_inc(k_out, 1)
                dve.wait_ge(oc_out, 2)
                for u in range(18):
                    if u < 16:
                        b, t, kv = units[u]
                        nk = P * (1 + t)
                        dve.wait_ge(s_sum, u + 1)
                        if u >= 2:
                            dve.wait_ge(p_turned, u - 1)
                        mask = C[:, C_ZC + (P if t == 0 else 0):C_ZC + 2 * P]
                        for e in range(2):
                            V.tensor_tensor(S[:, u % 2, e, :, 0:nk], pg[:, 2 * (u % 2) + e, 0:2 * nk].rearrange("p (a n) -> p a n", a=2),
                                            bc(mask.unsqueeze(1), 2, nk), ALU.add).then_inc(s_masked, 1)
                        dve.wait_ge(s_masked, 2 * u + 2)
                        link(V.tensor_reduce(NM[:, 4 * u:4 * u + 4], S[:, u % 2, :, :, 0:nk].rearrange("p e a n -> p (e a) n"), AX.X, ALU.max))
                        V.tensor_scalar(NM[:, 4 * u:4 * u + 4], NM[:, 4 * u:4 * u + 4], -HD ** -0.5, None, ALU.mult).then_inc(s_max, 1)
                    if 1 <= u <= 16 and units[u - 1][1] == 1:
                        dve.wait_ge(p_turned, u)
                        if u >= 3:
                            dve.wait_ge(o_sum, u - 2)
                        V.tensor_copy(PT[:, (u - 1) % 2, 1], bank4(1)).then_inc(p_out1, 1)
                    if u >= 2:
                        v = u - 2
                        b, t, kv = units[v]
                        co = CX[:, 0:4]
                        link(V.reciprocal(co, SUM[:, 4 * v:4 * v + 4]))
                        g4 = AT[:, 48 * t + 12 * kv:48 * t + 12 * kv + 12].rearrange("p (x e g) -> p g e x", e=2, g=3)[:, 1 + b]
                        link(V.tensor_tensor(co.rearrange("p (e x) -> p e x", e=2), co.rearrange("p (e x) -> p e x", e=2), g4, ALU.mult))
                        dve.wait_ge(o_sum, v + 1)
                        tmp = OT[:]
                        link(V.tensor_tensor(tmp, pt[:, 2 + v % 2, 0:256].rearrange("p (h d) -> p h d", d=HD), bc(co.unsqueeze(2), 4, HD), ALU.mult))
                        y = YA[:, t, kv * 256:(kv + 1) * 256].rearrange("p (x e d) -> p e x d", e=2, d=HD)
                        V.tensor_tensor(y, y, tmp.rearrange("p (e x) d -> p e x d", e=2), ALU.add).then_inc(o_out, 1)
                        dve.wait_ge(o_out, v + 1)

            def ffn(g, hooks, between):
                N = g["N"]

                def pair(c, d, between={}):
                    for h in range(4):
                        hooks[h](c, d)
                        for j in range(4):
                            between.get(4 * h + j, no)()
                            split(N + c * 16 + 4 * (h + 1) + j, d * 16, CW)

                pair(0, 0, between)
                with dve.Fori(0, NFF - 1) as i:
                    pair(1, i)

            def down(g, hooks, evac, between={}):
                N, S_, n = g["N"], g["S"], len(g["chunks"])
                for c in range(n):
                    for j in range(S_):
                        if c == 0 and j % 4 == 0 and j // 4 < len(hooks):
                            hooks[j // 4]()
                        between.get((c, j), no)()
                        split(N + c * S_ + RING + j)
                    evac(c, 0, N + (c + 1) * S_)

            F1, F2 = G["ffn1"], G["ffn2"]

            def after(f):
                return lambda c, d: f(c, d) if c else None

            def f1_h(c, d):
                b = 2 * ((F1["C"] + 1) % 2)
                dve.wait_ge(step_used, F1["N"] + 16 * c + d * 16)
                chunks_read(dve, F1["C"] + 2 * c - 1 + d * 2)
                if c > 1 or not isinstance(d, int):
                    dve.wait_ge(f_turned, c - 1 + d)
                for t in range(NT):
                    V.scalar_tensor_tensor(HT[:, t, :], pg[:, b + t, :], SM[:, 4 + t:5 + t], SG[:, t, :], ALU.mult, ALU.mult)\
                        .then_inc(chunk_out[t], 1)

            def f1_lo(c, d):
                dve.wait_ge(f_hi, c + d)
                x = FH[:, ds((d + c - 1) * 4, 4), :].bitcast(F32)
                V.tensor_tensor(FL[:, ds((d + c - 1) * 4, 4), :], pt[:, 0:2, :].rearrange("p b (c n) -> p (b c) n", n=TOK), x, ALU.subtract)\
                    .then_inc(f_lo, 1)

            def f2_up(c, d):
                b = 2 * ((F2["C"] + 1) % 2)
                dve.wait_ge(step_used, F2["N"] + 16 * c + d * 16)
                dve.wait_ge(c_turned, 2 * c - 1 + d * 2)
                V.tensor_scalar(UT[:, 1, :], pg[:, b + 1, :], SM[:, 5:6], None, ALU.mult).then_inc(chunk_out[1], 1)

            def conv_rest(src, dst, k0, nth):
                dve.wait_ge(c_first, nth)
                for j in (1, 0):
                    for k in range(4):
                        x = dst[:, k, 2 - j:TOK]
                        ins = V.scalar_tensor_tensor(x, src[:, k, 0:TOK - 2 + j], VT[:, ds(k0 + V_CW2 + j * 88 + k, 1)], x,
                                                     ALU.mult, ALU.add)
                    if j:
                        ins.then_inc(c_part, 1)
                        dve.wait_ge(c_part, nth)
                ins.then_inc(c_sum, 1)

            def f2_conv_up(c, d):
                conv_rest(pt[:, 2:4, :].rearrange("p b (c n) -> p (b c) n", n=TOK), UC, d * 4 + (c - 1) * 4 + FKT, 2 * c + d * 2)
                dve.wait_ge(c_sum, 2 * c + d * 2)
                dve.wait_ge(c_silu, c + d)
                V.tensor_tensor(UC[:], UC[:], GC[:], ALU.mult).then_inc(c_prod, 1)

            def f2_gate(c, d):
                b = 2 * (F2["C"] % 2)
                dve.wait_ge(step_used, F2["N"] + 16 * c + 8 + d * 16)
                if c:
                    dve.wait_ge(c_turned, 2 * c + d * 2)
                V.tensor_scalar(UT[:, 1, :], pg[:, b + 1, :], SM[:, 5:6], None, ALU.mult).then_inc(chunk_out[1], 1)

            def f2_lo(c, d):
                dve.wait_ge(f_hi, NFF + c + d)
                V.tensor_tensor(FL[:, ds((d + c - 1) * 4, 4), :], UC[:], FH[:, ds((d + c - 1) * 4, 4), :].bitcast(F32), ALU.subtract)\
                    .then_inc(f_lo, 1)

            def f2_conv_gate(c, d):
                conv_rest(pt[:, 0:2, :].rearrange("p b (c n) -> p (b c) n", n=TOK), GC, d * 4 + c * 4, 2 * c + 1 + d * 2)

            def fox():
                v, e = SF_[:, 0:16], SF_[:, 16:32]
                b8 = bc(BV[:, B_BF:B_BF + 8].unsqueeze(1), 2, 8)
                link(V.tensor_tensor(v.rearrange("p (t h) -> p t h", t=2), Z2[:, :, O2_F:O2_F + 8], b8, ALU.add))
                V.scalar_tensor_tensor(e, v, -1.0, v, ALU.mult, ALU.max).then_inc(lf_ready, 1)
                dve.wait_ge(lf_ln, 1)
                V.scalar_tensor_tensor(SF_[:, 32:48], v, 0.0, e, ALU.min, ALU.subtract).then_inc(lf_ready, 1)
                dve.wait_ge(fq_turned, 2)
                V.tensor_copy(KF2[:], pg[:].rearrange("p b (c n) -> p (b c) n", n=TOK)).then_inc(fk_out, 1)
                dve.wait_ge(fc_out, 1)
                for u in range(10):
                    if u < 8:
                        t, hp = u // 4, u % 4
                        nk = P * (1 + t)
                        dve.wait_ge(fs_sum, u + 1)
                        if u >= 2:
                            dve.wait_ge(fp_turned, u - 1)
                        x = SF[:, u % 2, :, 0:nk]
                        link(V.scalar_tensor_tensor(x, pg[:, u % 4, 0:2 * nk].rearrange("p (j n) -> p j n", j=2), P ** -0.5,
                                                    CB[:, 2 * hp:2 * hp + 2, 0:nk], ALU.mult, ALU.add))
                        y = SF[:, u % 2, :, nk - P:nk]
                        link(V.tensor_tensor(y, y, bc(C[:, C_ZC + P:C_ZC + 2 * P].unsqueeze(1), 2, P), ALU.add))
                        m = SF_[:, 64 + 2 * u:66 + 2 * u]
                        link(V.tensor_reduce(m, x, AX.X, ALU.max))
                        V.tensor_scalar(m, m, -1.0, None, ALU.mult).then_inc(fs_max, 1)
                    if u >= 2:
                        w = u - 2
                        t, hp = w // 4, w % 4
                        link(V.reciprocal(SF_[:, 100:102], SF_[:, 80 + 2 * w:82 + 2 * w]))
                        dve.wait_ge(fo_sum, w + 1)
                        V.tensor_tensor(YF[:, t, hp * 256:(hp + 1) * 256].rearrange("p (j n) -> p j n", j=2),
                                        pt[:, 2 + w % 2, 0:256].rearrange("p (j n) -> p j n", j=2),
                                        bc(SF_[:, 100:102].unsqueeze(2), 2, P), ALU.mult).then_inc(fo_out, 1)
                        dve.wait_ge(fo_out, w + 1)

            def hgrn():
                f = Z2[:, :, O2_HF:O2_HF + W2]
                dve.wait_ge(hg_ln, 1)
                V.tensor_scalar(f, f, 0.0, None, ALU.min).then_inc(hg_lf, 1)
                dve.wait_ge(hg_lf, 1)
                V.tensor_tensor(f, f, LG1[:].rearrange("p (t n) -> p t n", t=2), ALU.subtract).then_inc(hg_lf, 1)
                link(V.memset(HS[:], 0.0))
                dve.wait_ge(hq_turned, 1)
                V.tensor_copy(HQ[:], pg[:].rearrange("p b (c n) -> p (b c) n", n=TOK)).then_inc(hq_out, 1)
                dve.wait_ge(hc_out, 1)
                dve.wait_ge(hk_out, 1)
                dve.wait_ge(hq_out, 1)

                def diff(l):
                    if l == 1:
                        dve.wait_ge(hg_lf, 2)
                    if l >= 2:
                        dve.wait_ge(lv_sum, lv_units(l - 2))
                    g = LG[l % 2]
                    if l == 0:
                        x = g[:].rearrange("p (h a n) -> p h a n", h=8, a=4)
                        c = CUM[:].rearrange("p (h a n) -> p h a n", h=8, a=4)
                        link(V.tensor_tensor(x[:, :, 0:2, :], c[:, :, 0:2, 63:64].to_broadcast([P, 8, 2, 64]), c[:, :, 0:2, :], ALU.subtract))
                        V.tensor_tensor(x[:, :, 0, :], x[:, :, 0, :], c[:, :, 1, 63:64].to_broadcast([P, 8, 64]), ALU.add)
                        V.tensor_tensor(x[:, :, 3, :], c[:, :, 3, :], c[:, :, 2, 63:64].to_broadcast([P, 8, 64]), ALU.add).then_inc(lv_diff, 1)
                    elif l == 1:
                        x = g[:].rearrange("p (n a b) -> p n a b", a=2, b=64)
                        c = CUM[:].rearrange("p (n a b) -> p n a b", a=2, b=64)
                        V.tensor_tensor(x[:, :, 0, :], c[:, :, 0, 63:64].to_broadcast([P, 16, 64]), c[:, :, 0, :], ALU.subtract).then_inc(lv_diff, 1)
                    else:
                        b = LEVELS[l - 1]
                        n = HG_N * TOK // (2 * b)
                        x = g[:].rearrange("p (n a b) -> p n a b", a=2, b=b)
                        c = CUM[:].rearrange("p (n a b) -> p n a b", a=2, b=b)
                        ref = c[:, :, 0, b - 1:b].to_broadcast([P, n, b])
                        V.tensor_tensor(x[:, :, 0, :], ref, c[:, :, 0, :], ALU.subtract)
                        V.tensor_tensor(x[:, :, 1, :], c[:, :, 1, :], ref, ALU.subtract).then_inc(lv_diff, 1)

                def mul(l):
                    dve.wait_ge(lv_exp, l + 1)
                    b = P if l == 0 else LEVELS[l - 1]
                    g = LG[l % 2][:].rearrange("p (n a b) -> p n a b", a=2, b=b)
                    k = HKT[:].rearrange("p h (n a b) -> p (h n) a b", a=2, b=b)
                    q = HQ[:].rearrange("p h (n a b) -> p (h n) a b", a=2, b=b)
                    V.tensor_tensor(g[:, :, 0, :], g[:, :, 0, :], k[:, :, 0, :], ALU.mult)
                    V.tensor_tensor(g[:, :, 1, :], g[:, :, 1, :], q[:, :, 1, :], ALU.mult).then_inc(lv_mul, 1)

                def take(l):
                    if l == 0:
                        dve.wait_ge(lv_sum, 1)
                        V.tensor_copy(HX[:], lv_banks(0)).then_inc(lv_out, 1)
                        return
                    for t in range(NT):
                        u = 1 + 2 * (l - 1) + t
                        dve.wait_ge(lv_sum, u + 1)
                        if u >= 3:
                            dve.wait_ge(lv_out, u - 1)
                        mask = bc(MK[:, (l - 1) * P:l * P].unsqueeze(1), 8, P)
                        V.copy_predicated(HS[:, t, :, :], mask, lv_banks(u)).then_inc(lv_out, 1)

                dve.wait_ge(consts_set, 3)
                diff(0)
                diff(1)
                for l in range(8):
                    mul(l)
                    if 1 <= l < 7:
                        diff(l + 1)
                    if l:
                        take(l - 1)
                take(7)
                take(8)
                dve.wait_ge(ho_out, 1)
                y = YG[:].rearrange("p t (h n) -> p (t h) n", n=P)
                sq = LG1[:].rearrange("p (h n) -> p h n", n=P)
                dve.wait_ge(lv_out, 17)
                link(V.tensor_tensor(sq, y, y, ALU.mult))
                V.tensor_reduce(HN[:, 0:16], sq, AX.X, ALU.add).then_inc(hn_sq, 1)
                dve.wait_ge(hn_root, 1)
                link(V.tensor_scalar(HN[:, 32:48], HN[:, 0:16], 1.0 / P, EPS, ALU.mult, ALU.add))
                refine(HN[:, 0:16], HN[:, 32:48], HN[:, 16:32], HN[:, 48:64])
                link(V.tensor_tensor(HN[:, 0:16], HN[:, 0:16], HN[:, 48:64], ALU.mult))
                link(V.tensor_tensor(y, y, bc(HN[:, 0:16].unsqueeze(2), 16, P), ALU.mult))
                link(V.tensor_tensor(y, y, bc(BV[:, B_GO:B_GO + P].unsqueeze(1), 16, P), ALU.mult))
                dve.wait_ge(hg_silu, 1)
                V.tensor_tensor(YG[:], YG[:], Z2[:, :, O2_HG:O2_HG + W2], ALU.mult).then_inc(yg_ready, 1)

            dve.wait_ge(vec_turned, 1)
            V.tensor_copy(VT[:, 0:196], pg[:, 0, 0:196]).then_inc(vec_ready, 1)
            V.tensor_copy(VT[:, 196:V_N], pg[:, 1, 0:V_N - 196]).then_inc(vec_ready, 1)
            dve.wait_ge(vec_ready, 2)
            g = VT[:, V_GMIX:V_GMIX + KT]
            V.tensor_tensor(g, g, VT[:, V_FIN:V_FIN + KT], ALU.mult).then_inc(vec_ready, 1)
            for n in range(RING):
                split(n)
            pre0 = lambda c: lambda: prep(0, lambda k: V_ATTN + k, AH, AL, c)
            dve.wait_ge(vec_ready, 3)
            pre0(0)()
            pre0(1)()
            stream(G["in1"], evac_copy(Z1, G["in1"], True), {
                (0, 1): pre0(2), (0, 2): pre0(3), (0, 4): lambda: norm(0, H[:, 1, :], D, XN[:, 1, :], None),
                (3, 1): lambda: conv(0), (3, 2): lambda: conv(1), (4, 1): lambda: conv(2), (4, 2): lambda: conv(3),
                (5, 1): lambda: conv(4), (5, 2): lambda: conv(5), (6, 1): x_back,
                (6, 3): dt_abs, (6, 5): dt_plus, (6, 7): dt_rest, (7, 3): a_sums,
                (10, 2): lambda: kv_flat(0), (10, 3): lambda: kv_flat(1), (10, 4): lambda: kv_flat(2), (10, 5): lambda: kv_flat(3),
            }, loop=False)
            if upto < 3: return
            dve.wait_ge(step_used, G["in1"]["end"])
            ssd()
            if upto < 4: return
            dve.wait_ge(yo_sum, 1)
            dve.wait_ge(xn0, 1)
            nsa()
            if upto < 5: return
            mix1 = lambda c: lambda: prep(1, lambda k: V_SSD + k if k < 8 else None, OH1, OL1, c)
            f1_in = lambda c: lambda: prep(2, lambda k: V_FFN + k, AH, AL, c)
            mix1(0)()
            mix1(1)()
            stream(G["out1"], evac_add(G["out1"]),
                   {(0, 1): mix1(2), (0, 2): mix1(3), (1, 1): f1_in(0), (2, 1): f1_in(1), (3, 1): f1_in(2)})
            if upto < 8: return

            def norm_ffn1():
                chunks_read(dve, F1["C"])
                norm(2, H[:, 1, :], D, XN[:, 1, :], None)

            ffn(F1, [after(f1_h), after(f1_lo), no, no], {1: f1_in(3), 3: norm_ffn1})
            if upto < 9: return
            in2 = lambda c: lambda: prep(3, lambda k: V_GMIX + k, AH, AL, c)
            down(G["down1"], [lambda: f1_h(NFF, 0), lambda: f1_lo(NFF, 0)], evac_add(G["down1"]),
                 {(1, 1): in2(0), (2, 1): in2(1), (3, 1): in2(2)})
            if upto < 10: return

            def norm_final():
                chunks_read(dve, G["in2"]["C"])
                norm(3, H[:, 1, :], D, XN[:, 1, :], None)

            def apply_final():
                dve.wait_ge(gain_landed, 16)
                for t in range(NT):
                    ins = V.scalar_tensor_tensor(H[:, t, :], H[:, t, :], SM[:, 4 + t:5 + t], GP[:], ALU.mult, ALU.mult)
                ins.then_inc(h_ready, 1)

            def norm_mix():
                dve.wait_ge(h_ready, 1)
                norm(4, H[:, 1, :], D, XN[:, 1, :], None, before=True)

            stream(G["in2"], evac_copy(Z2, G["in2"], True),
                   {(0, 1): in2(3), (0, 2): norm_final, (0, 3): apply_final, (0, 5): norm_mix})
            if upto < 12: return
            dve.wait_ge(step_used, G["in2"]["end"])
            chunks_read(dve, G["out2"]["C"])
            fox()
            if upto < 13: return
            hgrn()
            if upto < 14: return
            mix2 = lambda c: lambda: prep(4, lambda k: None, OH2, OL2, c)
            mix2(0)()
            mix2(1)()
            stream(G["out2"], evac_gained(MIX, G["out2"], 0), {(0, 1): mix2(2), (0, 2): mix2(3)})
            f2_in = lambda c: lambda: prep(5, lambda k: V_GFFN + k, AH, AL, c)
            post_sums(8)
            rstd(5, D)
            dve.wait_ge(gained, 4)
            post_add(MIX, 0)
            post_add(MIX, 1)
            f2_in(0)()
            post_add(MIX, 2)
            f2_in(1)()
            post_add(MIX, 3)
            if upto < 17: return

            def norm_ffn2():
                dve.wait_ge(h_block, 4)
                norm(6, H[:, 1, :], D, XN[:, 1, :], None)

            ffn(F2, [after(f2_up), after(f2_conv_up), lambda c, d: (f2_gate(c, d), after(f2_lo)(c, d)), f2_conv_gate],
                {1: f2_in(2), 2: f2_in(3), 4: norm_ffn2})

            def p_parts():
                dve.wait_ge(p_hi, 1)
                V.tensor_tensor(PL[:], pt[:, 3, :].rearrange("p (k n) -> p k n", k=2), PH[:].bitcast(F32), ALU.subtract).then_inc(p_lo, 1)

            down(G["down2"], [lambda: f2_up(NFF, 0), lambda: f2_conv_up(NFF, 0), no, lambda: f2_lo(NFF, 0)],
                 evac_gained(FO, G["down2"], 8), {(1, 2): p_parts})
            if upto < 18: return
            def proj(c):
                evac_copy(E, G["proj"])(c, 0, G["proj"]["N"] + c + 1)
                split(G["ple"]["N"] + c)

            post_sums(16)
            proj(0)
            rstd(7, D)
            dve.wait_ge(gained, 8)
            post_add(FO, 0)
            proj(1)
            post_add(FO, 1)
            proj(2)
            post_add(FO, 2)
            proj(3)
            post_add(FO, 3)
            ple_in = lambda c: lambda: prep(6, lambda k: V_GPLE + k, OH2, OL2, c)

            def norm_ple():
                dve.wait_ge(h_block, 8)
                norm(8, H[:, 1, :], D, FO[:, 1, :], None)

            ple_in(0)()
            ple_in(1)()
            between = {(0, 1): ple_in(2), (0, 2): ple_in(3), (0, 4): norm_ple}

            def e_gained(c):
                dve.wait_ge(gain_landed, 64)
                dve.wait_ge(sq_ready, 16 + 2 * c + 2)
                for t in range(NT):
                    x = E[:, t, c * CW:(c + 1) * CW]
                    ins = V.tensor_tensor(x, x, GP[:, c * CW:(c + 1) * CW], ALU.mult)
                ins.then_inc(gained, 1)

            g = G["ple"]
            for c in range(4):
                for j in range(8):
                    between.get((c, j), no)()
                    split(g["N"] + c * 8 + RING + j)
                for t in range(NT):
                    dve.wait_ge(chunk_out[t], g["C"] + c + 1)
                    x = E[:, t, c * CW:(c + 1) * CW]
                    V.tensor_tensor(x, x, GS[:, t, :], ALU.mult).then_inc(e_ready, 1)
                if c:
                    e_gained(c - 1)
            post_sums(24)
            e_gained(3)
            rstd(9, D)
            dve.wait_ge(gained, 12)
            for c in range(4):
                post_add(E, c)

        @block.tensor
        def _(pe):
            mm, tr = nc.tensor.matmul, nc.tensor.transpose
            no = lambda *_: None

            def step(n, d, b, kt0, w, first, last, hi=AH, lo=AL):
                pe.wait_ge(lo_ready, n + 1 + d)
                for k in range(SK):
                    wh = whi[:, n % RING, k * w:(k + 1) * w]
                    wl = wlo[:, n % RING, k * w:(k + 1) * w]
                    for t in range(NT):
                        xh = hi[:, kt0 + k, t * P:(t + 1) * P]
                        xl = lo[:, kt0 + k, t * P:(t + 1) * P]
                        o = pg[:, b + t, 0:w]
                        mm(o, xh, wh, start=first and k == 0, stop=False)
                        mm(o, xh, wl, start=False, stop=False)
                        ins = mm(o, xl, wh, start=False, stop=last and k == SK - 1)
                ins.then_inc(step_used, 1)

            def chunk(g, c, j0=0, j1=None, dc=0, dn=0, hi=AH, lo=AL, before=None):
                C_ = g["C"] + c
                w = g["chunks"][c][2]
                for j in range(j0, g["S"] if j1 is None else j1):
                    if j == 0 and (C_ >= 2 or not isinstance(dc, int)):
                        chunks_read(pe, C_ - 1 + dc)
                    if before:
                        before(j)
                    step(g["N"] + c * g["S"] + j, dn, 2 * (C_ % 2), SK * j, w, j == 0, j == g["S"] - 1, hi, lo)

            def turn(p, src, c):
                for g in (2 * c, 2 * c + 1):
                    if g >= 4:
                        pe.wait_ge(a_lo, p * 8 + g - 3)
                    for k in range(2):
                        for t in range(NT):
                            ins = tr(pt[:, g % 4, (2 * k + t) * P:(2 * k + t + 1) * P], src(2 * g + k, t), ident)
                    ins.then_inc(turned, 1)

            def h_tiles(kt, t):
                return H[:, t, kt * P:(kt + 1) * P]

            def first(p, src, quarter, hi, lo, g):
                def before(j):
                    for c in {0: (0, 1), 1: (2,), 3: (3,)}.get(j, ()):
                        quarter(c)
                        turn(p, src, c)
                    pe.wait_ge(a_lo, p * 8 + j + 1)
                chunk(g, 0, hi=hi, lo=lo, before=before)

            def last_quarter(g, p):
                def before(j):
                    if j == 1:
                        chunks_read(pe, g["C"] + 4)
                        turn(p, h_tiles, 3)
                    pe.wait_ge(a_lo, p * 8 + j + 1)
                return before

            def turning(g, p, c):
                def before(j):
                    if j == 1:
                        chunks_read(pe, g["C"] + c)
                        turn(p, h_tiles, c - 1)
                return before

            def stream(g, hooks={}, loop=True):
                n = len(g["chunks"])
                chunk(g, 1)
                loops = uniform_pairs(g)
                if loops > 2 and loop:
                    with pe.Fori(0, loops - 1) as i:
                        for c in (2, 3):
                            chunk(g, c, dc=i * 2, dn=i * (2 * g["S"]))
                    done = 2 * loops
                else:
                    done = 2
                for c in range(done, n):
                    chunk(g, c, before=lambda j: hooks.get((c, j), no)())

            def conv_turn(c):
                chunks_read(pe, G["in1"]["C"] + c + 1)
                for g in (2 * (c - 2), 2 * (c - 2) + 1):
                    if g >= 4:
                        pe.wait_ge(cv_sum, g - 3)
                    for k in range(2):
                        for t in range(NT):
                            c0 = O_XBC + (2 * g + k) * P
                            ins = tr(pt[:, g % 4, (2 * k + t) * P:(2 * k + t + 1) * P], Z1[:, t, c0:c0 + P], ident)
                    ins.then_inc(cv_turned, 1)

            def x_back0():
                pe.wait_ge(cv_act, 4)
                for k in range(8):
                    ins = tr(pt[:, 2 + k // 4, (k % 4) * P:(k % 4 + 1) * P], XC[:, k, 0:P], ident)
                ins.then_inc(xt_turned, 1)

            def x_back1():
                pe.wait_ge(cv_act, 6)
                pe.wait_ge(xt_a, 1)
                for g in range(SSD_G):
                    tr(pt[:, 2, g * P:(g + 1) * P], XC[:, 8 + g, 0:P], ident)
                for k in range(8):
                    ins = tr(pt[:, k // 4, (k % 4) * P:(k % 4 + 1) * P], XC[:, k, P:TOK], ident)
                ins.then_inc(xt_turned, 1)

            def a_sums():
                pe.wait_ge(const_landed, 32)
                pe.wait_ge(adt_ready, 1)
                for t in range(NT):
                    mm(pt[:, 3, 16 * t:16 * t + 16], tri, SD[:, 2 + t, :], start=True, stop=True)
                mm(pt[:, 3, 32:48], ONES[:], SD[:, 2, :], start=True, stop=True).then_inc(acum_sum, 1)

            def kv_turn():
                pe.wait_ge(kv_twice, 1)
                pe.wait_ge(xt_d, 1)
                pe.wait_ge(acum_ready, 1)
                for b in range(4):
                    for h in range(2):
                        for t in range(NT):
                            src = KVD[:, b // 2, t, 2 * (b % 2) + h].rearrange("p a d -> p (a d)")
                            ins = tr(pt[:, b, h * TOK + t * P:h * TOK + (t + 1) * P], src, ident)
                    ins.then_inc(kc_turned, 1)

            def ssd():
                def hidden(i):
                    w, x = ((W1K, KFK), (W1V, KFV))[i]
                    for k in range(KT):
                        ins = mm(pt[0:60, 0, i * CMP_HID:(i + 1) * CMP_HID], x[:, k, :], w[:, k, :], start=k == 0, stop=k == KT - 1)
                    return ins

                def rows(t):
                    for h in range(SSD_H):
                        ins = mm(pg[:, h // 4, (h % 4) * P:(h % 4 + 1) * P], bc(SD[:, 2 + t, h:h + 1], P), tri, start=True, stop=True)
                    ins.then_inc(row_sum, 1)

                pe.wait_ge(cmpw_landed, 80)
                pe.wait_ge(kflat, 4)
                hidden(0)
                chunks_read(pe, G["out1"]["C"])
                rows(0)
                hidden(1).then_inc(hid_sum, 1)
                for t in range(NT):
                    for g in range(SSD_G):
                        ins = mm(pt[:, 3, (2 * t + g) * P:(2 * t + g + 1) * P], XC[:, 8 + g, t * P:(t + 1) * P],
                                 XC[:, 10 + g, t * P:(t + 1) * P], start=True, stop=True)
                ins.then_inc(cb_sum, 1)
                pe.wait_ge(hid_act, 1)
                for i in range(4):
                    ins = tr(pt[:, 1, i * 64:i * 64 + 60], HT_[0:60, i * P:(i + 1) * P], C[0:60, 0:60])
                ins.then_inc(hid_turned, 1)
                pe.wait_ge(seg_ready, 1)
                rows(1)
                pe.wait_ge(hid_act, 3)
                for m in range(2):
                    mm(pt[:, 1, 256:316], W2K[:, m].rearrange("p a d -> p (a d)"), HK[:, m, :], start=m == 0, stop=m == 1)
                for h in range(NKV):
                    for m in range(2):
                        ins = mm(pt[:, 2, h * HD:(h + 1) * HD], HV[:, m, h].rearrange("p g i -> p (g i)"), W2V[:, m, :],
                                 start=m == 0, stop=m == 1)
                ins.then_inc(cmp_sum, 1)
                pe.wait_ge(xs_ready, 1)
                pe.wait_ge(seg_ready, 2)
                for g in range(SSD_G):
                    ins = mm(pg[:, g, :], BT[:, g, :], XS[:, g * CW:(g + 1) * CW], start=True, stop=True)
                ins.then_inc(st_sum, 1)
                pe.wait_ge(cmp_kv, 5)
                for t in range(NT):
                    pe.wait_ge(m_ready, t + 1)
                    for h in range(SSD_H):
                        ins = mm(pt[:, 2 * t + h // 8, (h % 8) * HD:(h % 8 + 1) * HD], M[:, t, h, :], XD[:, t, h * HD:(h + 1) * HD],
                                 start=True, stop=True)
                    ins.then_inc(yd_sum, 1)
                pe.wait_ge(st_ready, 1)
                for g in range(SSD_G):
                    ins = mm(pg[:, 2 + g, :], XC[:, 10 + g, P:TOK], STA[:, g, :], start=True, stop=True)
                ins.then_inc(yo_sum, 1)

            units = [(b, t, kv) for b in range(2) for t in range(NT) for kv in range(NKV)]

            def nsa():
                pe.wait_ge(ys_ready, 1)
                for h in range(8):
                    for t in range(NT):
                        ins = tr(pt[:, h // 2, (h % 2) * TOK + t * P:(h % 2) * TOK + (t + 1) * P],
                                 Z1[:, t, O_Q + h * P:O_Q + (h + 1) * P], ident)
                ins.then_inc(q_turned, 1)
                pe.wait_ge(q_out, 2)
                for t in range(NT):
                    for h in range(NH):
                        e, kv = h % 2, h // 4
                        pr = slice(64 * e, 64 * e + 64)
                        c0 = t * 128 + (h // 2) * 16
                        ins = mm(pg[:, e, c0:c0 + NCMP], QT[pr, h // 2, t * P:(t + 1) * P], KCT[pr, kv * NCMP:(kv + 1) * NCMP],
                                 start=True, stop=True)
                ins.then_inc(cs_sum, 1)
                pe.wait_ge(pc_ready, 1)
                for t in range(NT):
                    for kv in range(NKV):
                        ins = tr(pt[:, t, kv * P:(kv + 1) * P], PC[:, t, 4 * kv:4 * kv + 4, :].rearrange("p h i -> p (h i)"), ident)
                ins.then_inc(pc_turned, 1)
                pe.wait_ge(pct_ready, 2)
                for t in range(NT):
                    for kv in range(NKV):
                        dst = pg[:, 2 + kv // 2, :] if t == 0 else pt[:, 2 + kv // 2, :]
                        ins = mm(dst[:, (kv % 2) * 256:(kv % 2 + 1) * 256], PCT[:, t, kv, :], BD[:, kv].rearrange("p a d -> p (a d)"),
                                 start=True, stop=True)
                ins.then_inc(oc_sum, 1)
                pe.wait_ge(roped, 1)
                pe.wait_ge(oc_out, 2)
                for h in range(8):
                    for t in range(NT):
                        ins = tr(pg[:, h // 2, (h % 2) * TOK + t * P:(h % 2) * TOK + (t + 1) * P],
                                 Z1[:, t, O_Q + h * P:O_Q + (h + 1) * P], ident)
                ins.then_inc(q_turned, 1)
                pe.wait_ge(k_twice, 1)
                for i in range(2):
                    for kv in range(NKV):
                        for t in range(NT):
                            src = KSD[:, i, t, kv].rearrange("p a d -> p (a d)")
                            c0 = (kv % 2) * TOK + t * P
                            ins = tr(pt[:, 2 * i + kv // 2, c0:c0 + P], src, ident)
                ins.then_inc(k_turned, 1)
                pe.wait_ge(q_out, 4)
                pe.wait_ge(k_out, 2)
                for u in range(18):
                    if u < 16:
                        b, t, kv = units[u]
                        nk = P * (1 + t)
                        if u >= 2:
                            pe.wait_ge(s_masked, 2 * (u - 1))
                        for x in range(2):
                            for e in range(2):
                                pr = slice(64 * e, 64 * e + 64)
                                ins = mm(pg[:, 2 * (u % 2) + e, x * nk:(x + 1) * nk], QT[pr, 2 * kv + x, t * P:(t + 1) * P],
                                         KTT[pr, b, kv, 0:nk], start=True, stop=True)
                        ins.then_inc(s_sum, 1)
                    if 1 <= u <= 16:
                        b, t, kv = units[u - 1]
                        pe.wait_ge(s_exp, u)
                        if u >= 2:
                            pe.wait_ge(p_out0, u - 1)
                            if units[u - 2][1]:
                                pe.wait_ge(p_out1, sum(x[1] for x in units[:u - 1]))
                        for kb in range(1 + t):
                            for j in range(4):
                                ins = tr(pt[:, kb, j * P:(j + 1) * P], S[:, (u - 1) % 2, j // 2, j % 2, kb * P:(kb + 1) * P], ident)
                        ins.then_inc(p_turned, 1)
                    if u >= 2:
                        v = u - 2
                        b, t, kv = units[v]
                        o = (O_VS, O_VW)[b] + kv * HD
                        pe.wait_ge(p_out0, v + 1)
                        if t:
                            pe.wait_ge(p_out1, sum(x[1] for x in units[:v + 1]))
                        if v >= 2:
                            pe.wait_ge(o_out, v - 1)
                        for j in range(4):
                            for kb in range(1 + t):
                                ins = mm(pt[:, 2 + v % 2, j * HD:(j + 1) * HD], PT[:, v % 2, kb, j, :], Z1[:, kb, o:o + HD],
                                         start=kb == 0, stop=kb == t)
                        ins.then_inc(o_sum, 1)

            F1, F2 = G["ffn1"], G["ffn2"]

            def f1_turn(c, d):
                chunks_read(pe, F1["C"] + 2 * c + d * 2)
                if c > 1 or not isinstance(d, int):
                    pe.wait_ge(f_lo, c - 1 + d)
                for k in range(4):
                    for t in range(NT):
                        ins = tr(pt[:, k // 2, (k % 2) * TOK + t * P:(k % 2) * TOK + (t + 1) * P], HT[:, t, k * P:(k + 1) * P], ident)
                ins.then_inc(f_turned, 1)

            def f1_pair(c, d):
                dc, dn = d * 2, d * 16
                if c:
                    chunk(F1, 2 * c, 0, 4, dc, dn)
                    f1_turn(c, d)
                    chunk(F1, 2 * c, 4, 8, dc, dn)
                else:
                    chunk(F1, 0, before=last_quarter(G["out1"], 2))
                chunk(F1, 2 * c + 1, dc=dc, dn=dn)

            def f2_turn(b0, nth):
                for k in range(4):
                    for t in range(NT):
                        ins = tr(pt[:, b0 + k // 2, (k % 2) * TOK + t * P:(k % 2) * TOK + (t + 1) * P], UT[:, t, k * P:(k + 1) * P], ident)
                ins.then_inc(c_turned, 1)

            def f2_turn_up(c, d):
                chunks_read(pe, F2["C"] + 2 * c + d * 2)
                if c > 1 or not isinstance(d, int):
                    pe.wait_ge(c_sum, 2 * (c - 1) + d * 2)
                f2_turn(2, 0)

            def f2_pair(c, d):
                dc, dn = d * 2, d * 16
                if c:
                    chunk(F2, 2 * c, 0, 4, dc, dn)
                    f2_turn_up(c, d)
                    chunk(F2, 2 * c, 4, 8, dc, dn)
                else:
                    first(5, h_tiles, lambda q: pe.wait_ge(h_block, q + 1), AH, AL, F2)
                chunk(F2, 2 * c + 1, 0, 4, dc, dn)
                chunks_read(pe, F2["C"] + 2 * c + 1 + d * 2)
                if c:
                    pe.wait_ge(c_sum, 2 * c - 1 + d * 2)
                f2_turn(0, 0)
                chunk(F2, 2 * c + 1, 4, 8, dc, dn)

            def pairs(f):
                f(0, 0)
                with pe.Fori(0, NFF - 1) as i:
                    f(1, i)

            def down(g, turn_last, f0, before):
                pe.wait_ge(f_lo, f0 + NFF - 1)
                chunk(g, 0, 0, 4, hi=FH, lo=FL)
                turn_last()
                chunk(g, 0, 4, 20, hi=FH, lo=FL)
                pe.wait_ge(f_lo, f0 + NFF)
                chunk(g, 0, 20, hi=FH, lo=FL)
                for c in range(1, 4):
                    chunk(g, c, hi=FH, lo=FL, before=before(c))

            def fox():
                for h in range(8):
                    for t in range(NT):
                        ins = tr(pt[:, h // 2, (h % 2) * TOK + t * P:(h % 2) * TOK + (t + 1) * P], Z2[:, t, h * P:(h + 1) * P], ident)
                ins.then_inc(fq_turned, 1)
                for h in range(8):
                    for t in range(NT):
                        ins = tr(pg[:, h // 2, (h % 2) * TOK + t * P:(h % 2) * TOK + (t + 1) * P],
                                 Z2[:, t, O2_K + h * P:O2_K + (h + 1) * P], ident)
                ins.then_inc(fq_turned, 1)
                pe.wait_ge(fq_out, 1)
                pe.wait_ge(lf_ready, 2)
                for h in range(8):
                    l0, l1 = (bc(SF_[:, 32 + 8 * t + h:33 + 8 * t + h], P) for t in range(NT))
                    o = pt[:, h // 2, (h % 2) * TOK:(h % 2 + 1) * TOK]
                    mm(o[:, 0:P], l0, tri, start=True, stop=True)
                    mm(o[:, P:TOK], l0, ONES[:], start=True, stop=False)
                    ins = mm(o[:, P:TOK], l1, tri, start=False, stop=True)
                ins.then_inc(fc_sum, 1)
                pe.wait_ge(fk_out, 1)
                pe.wait_ge(fc_out, 1)
                for u in range(10):
                    if u < 8:
                        t, hp = u // 4, u % 4
                        nk = P * (1 + t)
                        if u >= 4:
                            pe.wait_ge(fs_max, u - 3)
                        for j in range(2):
                            h = 2 * hp + j
                            ins = mm(pg[:, u % 4, j * nk:(j + 1) * nk], QT[:, h, t * P:(t + 1) * P], KF2[:, h, 0:nk], start=True, stop=True)
                        ins.then_inc(fs_sum, 1)
                    if 1 <= u <= 8:
                        t = (u - 1) // 4
                        pe.wait_ge(fs_exp, u)
                        if u >= 3:
                            pe.wait_ge(fp_out, u - 2)
                        for j in range(2):
                            for kb in range(1 + t):
                                ins = tr(pt[:, (u - 1) % 2, (2 * j + kb) * P:(2 * j + kb + 1) * P], SF[:, (u - 1) % 2, j, kb * P:(kb + 1) * P], ident)
                        ins.then_inc(fp_turned, 1)
                    if u >= 2:
                        v = u - 2
                        t, hp = v // 4, v % 4
                        pe.wait_ge(fp_out, v + 1)
                        if v >= 2:
                            pe.wait_ge(fo_out, v - 1)
                        for j in range(2):
                            o = O2_V + (2 * hp + j) * P
                            for kb in range(1 + t):
                                ins = mm(pt[:, 2 + v % 2, j * P:(j + 1) * P], PF[:, v % 2, j, kb, :], Z2[:, kb, o:o + P],
                                         start=kb == 0, stop=kb == t)
                        ins.then_inc(fo_sum, 1)

            def hgrn():
                pe.wait_ge(fo_out, 8)
                for h in range(8):
                    for t in range(NT):
                        ins = tr(pg[:, h // 2, (h % 2) * TOK + t * P:(h % 2) * TOK + (t + 1) * P],
                                 Z2[:, t, O2_HQ + h * P:O2_HQ + (h + 1) * P], ident)
                ins.then_inc(hq_turned, 1)
                pe.wait_ge(hg_sig, 1)
                for h in range(8):
                    for t in range(NT):
                        ins = tr(pt[:, h // 2, (h % 2) * TOK + t * P:(h % 2) * TOK + (t + 1) * P], YG[:, t, h * P:(h + 1) * P], ident)
                ins.then_inc(hk_turned, 1)
                pe.wait_ge(hg_lf, 2)
                pe.wait_ge(hk_out, 1)
                for h in range(8):
                    for t in range(NT):
                        c0 = O2_HF + h * P
                        ins = mm(pt[:, h // 2, (h % 2) * TOK + t * P:(h % 2) * TOK + (t + 1) * P], Z2[:, t, c0:c0 + P], tri64,
                                 start=True, stop=True)
                ins.then_inc(hc_sum, 1)
                pe.wait_ge(hc_out, 1)
                pe.wait_ge(hq_out, 1)

                def unit(u, lhs, rhs):
                    if u >= 4:
                        pe.wait_ge(lv_out, u - 3)
                    dst = lv_banks(u)
                    for h in range(8):
                        ins = mm(dst[:, h, :], lhs(h), rhs(h), start=True, stop=True)
                    ins.then_inc(lv_sum, 1)

                for l in range(8):
                    pe.wait_ge(lv_mul, l + 1)
                    g = LG[l % 2][:].rearrange("p (h n) -> p h n", h=8)
                    if l == 0:
                        unit(0, lambda h: g[:, h, 0:P], lambda h: g[:, h, P:TOK])
                    else:
                        for t in range(NT):
                            unit(1 + 2 * (l - 1) + t, lambda h: g[:, h, t * P:(t + 1) * P], lambda h: g[:, h, t * P:(t + 1) * P])
                for t in range(NT):
                    unit(15 + t, lambda h: HKT[:, h, t * P:(t + 1) * P], lambda h: HQ[:, h, t * P:(t + 1) * P])
                pe.wait_ge(lv_out, 17)
                for h in range(8):
                    v = [Z2[:, t, O2_HI + h * P:O2_HI + (h + 1) * P] for t in range(NT)]
                    c0 = (h % 4) * P
                    mm(pt[:, h // 4, c0:c0 + P], HS[:, 0, h, :], v[0], start=True, stop=True)
                    mm(pt[:, 2 + h // 4, c0:c0 + P], HX[:, h, :], v[0], start=True, stop=False)
                    ins = mm(pt[:, 2 + h // 4, c0:c0 + P], HS[:, 1, h, :], v[1], start=False, stop=True)
                ins.then_inc(ho_sum, 1)

            pe.wait_ge(ident_landed, 16)
            pe.wait_ge(vec_landed, 15 * 16)
            tr(pg[:, 0, 0:116], VR[0:116, 0, :], C[0:116, 0:116])
            tr(pg[:, 0, 116:196], VR[0:80, 1, :], C[0:80, 0:80])
            for j in range(4):
                ins = tr(pg[:, 1, 88 * j:88 * j + 88], VR[0:88, 2 + j, :], C[0:88, 0:88])
            ins.then_inc(vec_turned, 1)

            def x_quarter(c):
                pe.wait_ge(x_landed[c], 16)

            pe.wait_ge(vec_ready, 3)
            first(0, h_tiles, x_quarter, AH, AL, G["in1"])
            stream(G["in1"], {(3, 1): lambda: conv_turn(2), (4, 1): lambda: conv_turn(3), (5, 1): lambda: conv_turn(4),
                              (5, 4): x_back0, (6, 1): x_back1, (7, 2): a_sums, (10, 1): kv_turn}, loop=False)
            if upto < 3: return
            ssd()
            if upto < 4: return
            nsa()
            if upto < 5: return
            pe.wait_ge(o_out, 16)
            pe.wait_ge(xn0, 1)
            pe.wait_ge(xn1, 1)
            g = G["out1"]
            first(1, lambda k, t: YS[:, t, k * P:(k + 1) * P] if k < 8 else YA[:, t, (k - 8) * P:(k - 7) * P],
                  lambda c: None, OH1, OL1, g)
            for c in range(1, 4):
                chunk(g, c, hi=OH1, lo=OL1, before=turning(g, 2, c))
            if upto < 8: return
            pairs(f1_pair)
            if upto < 9: return
            down(G["down1"], lambda: f1_turn(NFF, 0), 0, lambda c: turning(G["down1"], 3, c))
            if upto < 10: return
            chunk(G["in2"], 0, before=last_quarter(G["down1"], 3))
            stream(G["in2"])
            if upto < 12: return
            chunks_read(pe, G["out2"]["C"])
            fox()
            if upto < 13: return
            hgrn()
            if upto < 14: return
            pe.wait_ge(yg_ready, 1)
            first(4, lambda k, t: YF[:, t, k * P:(k + 1) * P] if k < 8 else YG[:, t, (k - 8) * P:(k - 7) * P],
                  lambda c: None, OH2, OL2, G["out2"])
            for c in range(1, 4):
                chunk(G["out2"], c, hi=OH2, lo=OL2)
            if upto < 17: return
            pairs(f2_pair)

            def turn_p(c):
                def before(j):
                    if c == 1 and j == 1:
                        pe.wait_ge(bc_landed, 96)
                        for k in range(2):
                            for t in range(NT):
                                ins = tr(pt[:, 3, (2 * k + t) * P:(2 * k + t + 1) * P], PIN[:, t, k * P:(k + 1) * P], ident)
                        ins.then_inc(p_tr, 1)
                return before

            down(G["down2"], lambda: f2_turn_up(NFF, 0), NFF, turn_p)
            if upto < 18: return
            pe.wait_ge(p_lo, 1)
            for c in range(4):
                chunk(G["proj"], c, hi=PH, lo=PL)
            g = G["ple"]
            first(6, h_tiles, lambda c: pe.wait_ge(h_block, 4 + c + 1), OH2, OL2, g)
            for c in range(1, 4):
                chunk(g, c, hi=OH2, lo=OL2)


def uniform_pairs(g):
    n = sum(c[2] == CW for c in g["chunks"]) // 2
    if g["S"] % RING:
        return 0
    return n if len(g["chunks"]) > 2 * n and g["chunks"][2 * n][2] == CW or n * 2 == len(g["chunks"]) else n - 1


_INS = [
    "x", "attn_norm_w", "w_in", "conv_w", "conv_b", "dt_bias", "a_log", "d_skip", "ssd_norm_w", "cmp_w1_k",
    "cmp_w2_k", "cmp_w1_v", "cmp_w2_v", "cmp_pe_k", "cmp_pe_v", "w_out", "ffn_norm_w", "w_gate", "w_up",
    "w_down", "final_norm_w", "p_2", "g_mix_pre_2", "w_in_2", "b_fox_f_2", "g_hgrn_out_2", "w_out_2",
    "g_mix_post_2", "g_ffn_pre_2", "w_up_2", "conv_w_2", "conv_b_2", "w_down_2", "g_ffn_post_2",
    "g_ple_in_2", "w_ple_gate_2", "w_ple_proj_2", "g_ple_post_2",
]


def kernel(**inputs):
    import concourse.bacc as bacc
    from concourse.bass_utils import run_bass_kernel_spmd

    nc = bacc.Bacc("TRN2", target_bir_lowering=False, num_devices=1)
    consts, masks = constants()
    arrays = {n: np.ascontiguousarray(inputs[n]) for n in _INS}
    arrays["consts"], arrays["masks"] = consts, masks
    a = {n: nc.dram_tensor(n, v.shape, mybir.dt.from_np(v.dtype), kind="ExternalInput").ap() for n, v in arrays.items()}
    a["out"] = nc.dram_tensor("out", (1, TOK, D), F32, kind="ExternalOutput").ap()
    two_blocks(nc, a)
    r = run_bass_kernel_spmd(nc, [arrays], core_ids=[0])
    return r.results[0]["out"]
```

```python
from contextlib import ExitStack

import numpy as np

import concourse.bass as bass
from concourse import mybir

F32 = mybir.dt.float32
F32R = mybir.dt.float32r
U8 = mybir.dt.uint8
ALU = mybir.AluOpType
ACT = mybir.ActivationFunctionType
AX = mybir.AxisListType
ds = bass.ds

P = 128
TOK = 256
NT = TOK // P
D = 2048
KT = D // P
EPS = 1e-6
NEG = -1e30

SSD_W = 1024
SSD_H = 16
SSD_G = 2
CONV1 = 1536
CK1 = CONV1 // P
HD = 64
NH = 16
NKV = 4
CMP_BLOCK, CMP_STRIDE, CMP_HID = 32, 16, 256
NCMP = (TOK - CMP_BLOCK) // CMP_STRIDE + 1
ROPE_HALF = HD // 4 // 2
O_Z, O_XBC = 0, SSD_W
O_DT = O_XBC + CONV1
O_Q = O_DT + SSD_H
O_KC = O_Q + NH * HD
O_VC, O_KS, O_VS, O_KW, O_VW = (O_KC + i * NKV * HD for i in range(1, 6))
O_GATE = O_KC + 6 * NKV * HD
D_IN1 = O_GATE + 3 * NH
FF = 5632
FKT = FF // P
W2 = 1024
FH_N = 8
HG_N = 8
O2_K, O2_V, O2_F = W2, 2 * W2, 3 * W2
O2_HQ = O2_F + FH_N
O2_HF, O2_HI, O2_HG = (O2_HQ + i * W2 for i in range(1, 4))
D_IN2 = O2_HG + W2
PLE = 256

CW = 512
SK = 2
RING = 4
NFF = FF // CW

C_ID, C_TRI, C_TRI64, C_ZC, C_NEGT, C_CMP = 0, 128, 256, 384, 640, 768
C_COS = C_CMP + NT * NCMP
C_SIN = C_COS + NT * ROPE_HALF
C_BLK = C_SIN + NT * ROPE_HALF
C_N = C_BLK + 4
LEVELS = (64, 32, 16, 8, 4, 2, 1, 0)

V_ATTN, V_FFN, V_GMIX, V_GFFN, V_GPLE, V_SSD, V_CB = 0, 16, 32, 48, 64, 80, 88
V_FIN, V_CW, V_PEK, V_PEV, V_CW2, V_CB2 = 100, 116, 164, 180, 196, 460
V_N = 548
B_DT, B_ALOG, B_DSK, B_BF, B_GO, B_N = 0, 16, 32, 48, 56, 184


def constants():
    c = np.zeros((P, C_N), np.float32)
    i = np.arange(P)
    c[:, C_ID:C_ID + P] = np.eye(P)
    le = i[:, None] <= i[None, :]
    c[:, C_TRI:C_TRI + P] = le
    c[:, C_TRI64:C_TRI64 + P] = le & (i[:, None] // 64 == i[None, :] // 64)
    c[:, C_ZC + P:C_ZC + 2 * P] = np.where(i[:, None] >= i[None, :], 0.0, NEG)
    c[:, C_NEGT:C_NEGT + P] = np.where(le, 0.0, NEG)
    inv = 1.0 / (np.float32(500000.0) ** (np.arange(0, 2 * ROPE_HALF, 2, dtype=np.float32) / np.float32(2 * ROPE_HALF)))
    for t in range(NT):
        pos = t * P + i
        end = np.arange(NCMP) * CMP_STRIDE + CMP_BLOCK - 1
        c[:, C_CMP + t * NCMP:C_CMP + (t + 1) * NCMP] = end[None, :] <= pos[:, None]
        ang = pos.astype(np.float32)[:, None] * inv[None, :].astype(np.float32)
        c[:, C_COS + t * ROPE_HALF:C_COS + (t + 1) * ROPE_HALF] = np.cos(ang)
        c[:, C_SIN + t * ROPE_HALF:C_SIN + (t + 1) * ROPE_HALF] = np.sin(ang)
    c[:, C_BLK:C_BLK + 4] = i[:, None] // 32 == np.arange(4)[None, :]
    m = np.zeros((P, len(LEVELS), P), np.float32)
    s, t = i[:, None], i[None, :]
    for n, b in enumerate(LEVELS):
        if b:
            m[:, n] = (s // (2 * b) == t // (2 * b)) & (s % (2 * b) < b) & (t % (2 * b) >= b)
        else:
            m[:, n] = s == t
    return c, m.reshape(P, len(LEVELS) * P)


def plan():
    full = lambda w, n: [(w, c * CW, CW) for c in range(n)]
    tail = lambda w, c0, n: [(w, c0, (n - c0) // 2), (w, c0 + (n - c0) // 2, (n - c0) // 2)]
    pairs = lambda a, b, off: [x for c in range(NFF) for x in ((a, c * CW, CW), (b, off + c * CW, CW))]
    table = [
        ("in1", full("w_in", 9) + tail("w_in", 9 * CW, D_IN1), KT),
        ("out1", full("w_out", 4), KT),
        ("ffn1", pairs("w_gate", "w_up", 0), KT),
        ("down1", full("w_down", 4), FKT),
        ("in2", full("w_in_2", 13) + tail("w_in_2", 13 * CW, D_IN2), KT),
        ("out2", full("w_out_2", 4), KT),
        ("ffn2", pairs("w_up_2", "w_up_2", FF), KT),
        ("down2", full("w_down_2", 4), FKT),
        ("proj", full("w_ple_proj_2", 4), PLE // P),
        ("ple", full("w_ple_gate_2", 4), KT),
    ]
    out, chunk, step = {}, 0, 0
    for name, chunks, kt in table:
        s = kt // SK
        out[name] = dict(chunks=chunks, S=s, C=chunk, N=step, end=step + s * len(chunks))
        chunk += len(chunks)
        step += s * len(chunks)
    widths = [c[2] for g in out.values() for c in g["chunks"] for _ in range(g["S"])]
    return out, widths


def two_blocks(nc, a, upto=99):
    G, WIDTH = plan()
    NSTEP = len(WIDTH)

    ctx = ExitStack()
    with ctx:
        def at(name, shape, dt, offset):
            size = int(np.prod(shape[1:])) * (1 if dt == U8 else 4)
            assert offset % 32 == 0 and offset + size <= nc.sbuf_usable_end, (name, offset + size)
            return nc.alloc_sbuf_tensor_at(name, shape, dt, offset=offset)

        STEP_B = SK * CW * 4
        o_ring = (nc.sbuf_base + 63) // 64 * 64
        raw = at("raw", [P, RING, SK * CW], F32, o_ring)
        whi = at("whi", [P, RING, SK * CW], F32R, o_ring + RING * STEP_B)
        wlo = at("wlo", [P, RING, SK * CW], F32R, o_ring + 2 * RING * STEP_B)
        o_h = o_ring + 3 * RING * STEP_B
        H = at("H", [P, NT, D], F32, o_h)
        o_a = o_h + NT * D * 4
        AH = at("AH", [P, KT, TOK], F32R, o_a)
        AL = at("AL", [P, KT, TOK], F32R, o_a + KT * TOK * 4)
        FO = at("FO", [P, NT, D], F32, o_a)
        PH = at("PH", [P, 2, TOK], F32R, o_a + NT * D * 4)
        PL = at("PL", [P, 2, TOK], F32R, o_a + NT * D * 4 + 2048)
        JQ = at("JQ", [P, NT, CW], F32, o_a + NT * D * 4 + 4096)
        o_c = o_a + 2 * KT * TOK * 4
        C = at("C", [P, C_N], F32, o_c)
        o_c += (C_N * 4 + 31) // 32 * 32
        MK = at("MK", [P, len(LEVELS) * P], U8, o_c)
        o_c += len(LEVELS) * P
        VT = at("VT", [P, V_N], F32, o_c)
        o_c += (V_N * 4 + 31) // 32 * 32
        BV = at("BV", [P, B_N], F32, o_c)
        o_c += B_N * 4
        PIN = at("PIN", [P, NT, PLE], F32, o_c)
        o_c += NT * PLE * 4
        ONES = at("ONES", [P, P], F32, o_c)
        o_c += P * 4
        SM = at("SM", [P, 16], F32, o_c)
        o_c += 64
        EPSC = at("EPSC", [P, 8], F32, o_c)
        o_c += 32
        PS = at("PS", [P, NT, 4], F32, o_c)
        o_c += 32
        GP = at("GP", [P, D], F32, o_c)
        o_gp = o_c
        o_b = o_gp + D * 4

        XN = at("XN", [P, NT, D], F32, o_b)
        OH1 = at("OH1", [P, KT, TOK], F32R, o_b)
        OL1 = at("OL1", [P, KT, TOK], F32R, o_b + KT * TOK * 4)
        OH2 = at("OH2", [P, KT, TOK], F32R, o_b + NT * D * 4)
        OL2 = at("OL2", [P, KT, TOK], F32R, o_b + NT * D * 4 + KT * TOK * 4)
        Z1 = at("Z1", [P, NT, D_IN1], F32, o_b)
        o_w = o_b + NT * D_IN1 * 4
        VR = at("VR", [P, 6, P], F32, o_w + 2 * 16384)
        W1K = at("W1K", [P, KT, CMP_HID], F32, o_w)
        W1V = at("W1V", [P, KT, CMP_HID], F32, o_w + 16384)
        XC = at("XC", [P, CK1, TOK], F32, o_w + 2 * 16384)
        XT = at("XT", [P, NT, SSD_W], F32, o_gp)
        BT = at("BT", [P, SSD_G, P], F32, o_w + 2 * 16384 + 12288)
        YOFF = at("YOFF", [P, SSD_W], F32, o_w + 21504)
        KSD = at("KSD", [P, 2, NT, NKV, 2, HD], F32, o_w + 8192)
        JUNK = at("JUNK", [P, NT, SSD_W], F32, o_w)
        YS = at("YS", [P, NT, SSD_W], F32, o_w + 2 * 16384)
        MF = at("MF", [P, len(LEVELS) * P], F32, o_gp)
        KVD = at("KVD", [P, 2, NT, NKV, 2, HD], F32, o_w + 2 * 16384)
        KFK = at("KFK", [P, KT, 60], F32, o_w + 2 * 16384)
        KFV = at("KFV", [P, KT, 60], F32, o_w + 2 * 16384 + 3840)
        o_m = o_w + 2 * 16384 + 2 * 8192
        HK = at("HK", [P, 2, 60], F32, o_m)
        HV = at("HV", [P, 2, NKV, 4, 32], F32, o_w)
        HT_ = at("HT_", [P, 2 * CMP_HID], F32, o_w + 4096)
        RK = at("RK", [P, 4, NKV, ROPE_HALF], F32, o_w + 2 * 16384 + 13312)
        KCB = at("KCB", [P, NKV, 32], F32, o_w + 2 * 16384 + 13824)
        W2K = at("W2K", [P, 2, 2, HD], F32, o_m + 768)
        W2V = at("W2V", [P, 2, HD], F32, o_m + 1792)
        BD = at("BD", [P, NKV, 4, HD], F32, o_w + 25600)
        SD = at("SD", [P, 16, 16], F32, o_m + 2304)
        AT = at("AT", [P, 256], F32, o_w + 30720)
        M = at("M", [P, NT, SSD_H, P], F32, o_a)
        XD = at("XD", [P, NT, SSD_W], F32, o_a + 16384)
        XS = at("XS", [P, SSD_W], F32, o_a + 24576)
        STA = at("STA", [P, SSD_G, CW], F32, o_a + 28672)
        QT = at("QT", [P, 8, TOK], F32, o_a)
        KTT = at("KTT", [P, 2, NKV, TOK], F32, o_a + 8192)
        S = at("S", [P, 3, 2, 2, TOK], F32, o_a + 16384)
        PT = at("PT", [P, 2, 2, 4, P], F32, o_w + 8192)
        SC = at("SC", [P, NT, NH, NCMP], F32, o_a + 16384)
        PC = at("PC", [P, NT, NH, 32], F32, o_a + 20480)
        PCT = at("PCT", [P, NT, NKV, P], F32, o_a + 28672)
        FH = at("FH", [P, FKT, TOK], F32R, o_b)
        FL = at("FL", [P, FKT, TOK], F32R, o_b + FKT * TOK * 4)
        SG = at("SG", [P, NT, CW], F32, o_gp)
        HT = at("HT", [P, NT, CW], F32, o_gp + 4096)
        UT = at("UT", [P, NT, CW], F32, o_gp)
        GC = at("GC", [P, 4, TOK], F32, o_gp + 4096)
        UC = at("UC", [P, 4, TOK], F32, o_b + 2 * FKT * TOK * 4)
        Z2 = at("Z2", [P, NT, D_IN2], F32, o_b)
        o_y = o_b + NT * D_IN2 * 4
        YF = at("YF", [P, NT, W2], F32, o_y)
        YG = at("YG", [P, NT, W2], F32, o_y + 8192)
        o_t = o_y + 16384
        QF = at("QF", [P, FH_N, TOK], F32, o_y + 8192)
        KF2 = at("KF2", [P, FH_N, TOK], F32, o_gp)
        CB = at("CB", [P, FH_N, TOK], F32, o_t + 12288)
        SF = at("SF", [P, 2, 2, TOK], F32, o_t)
        PF = at("PF", [P, 2, 2, 2, P], F32, o_t + 4096)
        SF_ = at("SF_", [P, 128], F32, o_t + 8192)
        CUM = at("CUM", [P, HG_N * TOK], F32, o_gp)
        HQ = at("HQ", [P, HG_N, TOK], F32, o_a + 8192)
        HKT = at("HKT", [P, HG_N, TOK], F32, o_a + 16384)
        LG0 = at("LG0", [P, HG_N * TOK], F32, o_a + 24576)
        LG1 = at("LG1", [P, HG_N * TOK], F32, o_t + 12288)
        LG = [LG0, LG1]
        HS = at("HS", [P, NT, HG_N, P], F32, o_t)
        HX = at("HX", [P, HG_N, P], F32, o_t + 8192)
        HN = at("HN", [P, 64], F32, o_t + 20480)
        MIX = at("MIX", [P, NT, D], F32, o_b)
        E = at("E", [P, NT, D], F32, o_b)
        GS = at("GS", [P, NT, CW], F32, o_b + NT * D * 4 + 2 * KT * TOK * 4)

        pg = ctx.enter_context(nc.psum_tensor("pg", [P, 4, CW], F32))
        pt = ctx.enter_context(nc.psum_tensor("pt", [P, 4, CW], F32))

        def sem(name):
            return ctx.enter_context(nc.semaphore(name))

        raw_landed = [sem(f"raw_landed{i}") for i in range(RING)]
        hi_ready, lo_ready, step_used = sem("hi_ready"), sem("lo_ready"), sem("step_used")
        chunk_out = [sem("chunk_out0"), sem("chunk_out1")]
        dve_chain, act_chain = sem("dve_chain"), sem("act_chain")
        x_landed = [sem(f"x_landed{c}") for c in range(4)]
        attn_landed = sem("attn_landed")
        ident_landed, const_landed, vec_landed = sem("ident_landed"), sem("const_landed"), sem("vec_landed")
        bc_landed, cmpw_landed, gain_landed = sem("bc_landed"), sem("cmpw_landed"), sem("gain_landed")
        out_landed = sem("out_landed")
        consts_set, vec_turned, vec_ready = sem("consts_set"), sem("vec_turned"), sem("vec_ready")
        ss1, root, rstd_ready = sem("ss1"), sem("root"), sem("rstd_ready")
        sq_ready, gained = sem("sq_ready"), sem("gained")
        xn0, xn1 = sem("xn0"), sem("xn1")
        turned, a_hi, a_lo = sem("turned"), sem("a_hi"), sem("a_lo")
        h_ready, h_block = sem("h_ready"), sem("h_block")
        kv_twice, k_twice = sem("kv_twice"), sem("k_twice")
        kc_turned, kflat, hid_sum, hid_act = sem("kc_turned"), sem("kflat"), sem("hid_sum"), sem("hid_act")
        xd_ready, yo_added = sem("xd_ready"), sem("yo_added")
        yd_read, yo_read = sem("yd_read"), sem("yo_read")
        cs_read = sem("cs_read")
        zeroed = sem("zeroed")
        hid_turned, k_rot = sem("hid_turned"), sem("k_rot")
        cmp_sum, cmp_kv = sem("cmp_sum"), sem("cmp_kv")
        cv_turned, cv_first, cv_sum, cv_act = sem("cv_turned"), sem("cv_first"), sem("cv_sum"), sem("cv_act")
        xt_turned, xt_a, xt_d = sem("xt_turned"), sem("xt_a"), sem("xt_d")
        dt_exp, dt_u, dt_ln, adt_ready = sem("dt_exp"), sem("dt_u"), sem("dt_ln"), sem("adt_ready")
        acum_sum, acum_ready, decay_col = sem("acum_sum"), sem("acum_ready"), sem("decay_col")
        row_sum, seg_ready, seg_exp = sem("row_sum"), sem("seg_ready"), sem("seg_exp")
        cb_sum, m_ready, xs_ready = sem("cb_sum"), sem("m_ready"), sem("xs_ready")
        yd_sum, st_sum, st_ready, yo_sum, z_silu, ys_ready = (
            sem("yd_sum"), sem("st_sum"), sem("st_ready"), sem("yo_sum"), sem("z_silu"), sem("ys_ready"))
        q_turned, q_out, cs_sum, cs_ready, cs_exp = sem("q_turned"), sem("q_out"), sem("cs_sum"), sem("cs_ready"), sem("cs_exp")
        pc_ready, pc_turned, pct_ready, s_scaled = sem("pc_ready"), sem("pc_turned"), sem("pct_ready"), sem("s_scaled")
        gates, roped, k_turned, k_out = sem("gates"), sem("roped"), sem("k_turned"), sem("k_out")
        s_sum, s_masked, s_max, s_exp = sem("s_sum"), sem("s_masked"), sem("s_max"), sem("s_exp")
        p_turned, p_out0, p_out1, o_sum, o_hi, o_out = (
            sem("p_turned"), sem("p_out0"), sem("p_out1"), sem("o_sum"), sem("o_hi"), sem("o_out"))
        f_turned, f_hi, f_lo = sem("f_turned"), sem("f_hi"), sem("f_lo")
        c_turned, c_first, c_part, c_sum, c_silu, c_prod = (
            sem("c_turned"), sem("c_first"), sem("c_part"), sem("c_sum"), sem("c_silu"), sem("c_prod"))
        lf_exp, lf_ln, lf_ready = sem("lf_exp"), sem("lf_ln"), sem("lf_ready")
        fq_turned, fq_out, fk_out, fc_sum, fc_out = sem("fq_turned"), sem("fq_out"), sem("fk_out"), sem("fc_sum"), sem("fc_out")
        fs_sum, fs_max, fs_exp = sem("fs_sum"), sem("fs_max"), sem("fs_exp")
        fp_turned, fp_out, fo_sum, fo_out = sem("fp_turned"), sem("fp_out"), sem("fo_sum"), sem("fo_out")
        hg_ln, hg_sig, hg_lf, hg_gate = sem("hg_ln"), sem("hg_sig"), sem("hg_lf"), sem("hg_gate")
        hc_sum, hc_out, hq_turned, hq_out, hk_turned, hk_out = (
            sem("hc_sum"), sem("hc_out"), sem("hq_turned"), sem("hq_out"), sem("hk_turned"), sem("hk_out"))
        lv_diff, lv_exp, lv_mul, lv_sum, lv_out = sem("lv_diff"), sem("lv_exp"), sem("lv_mul"), sem("lv_sum"), sem("lv_out")
        lv_mul_q = sem("lv_mul_q")
        ho_sum, ho_out, hg_silu, yg_ready, hn_sq, hn_root, ho_read = (
            sem("ho_sum"), sem("ho_out"), sem("hg_silu"), sem("yg_ready"), sem("hn_sq"), sem("hn_root"), sem("ho_read"))
        p_tr, p_hi, p_lo, e_ready = sem("p_tr"), sem("p_hi"), sem("p_lo"), sem("e_ready")

        ident = C[:, C_ID:C_ID + P]
        tri = C[:, C_TRI:C_TRI + P]
        tri64 = C[:, C_TRI64:C_TRI64 + P]

        def bank4(n):
            return pt[:, n, :].rearrange("p (b c) -> p b c", c=P)

        def bc(ap, *shape):
            return ap.to_broadcast([P, *shape])

        def chunks_read(eng, n):
            for t in range(NT):
                eng.wait_ge(chunk_out[t], n)

        def quarters(p):
            return 8 * p - (4 if p > 1 else 0)

        def lv_units(l):
            return 3 + 2 * l

        def lv_banks(u):
            src = (pg, pt)[(u // 2) % 2]
            b = 2 * (u % 2)
            return src[:, b:b + 2, :].rearrange("p b (h n) -> p (b h) n", n=P)

        def ho_banks(t):
            b = 2 * ((G["out2"]["C"] + 1) % 2)
            return pg[:, b:b + 2, :] if t == 0 else pt[:, 2:4, :]

        block = ctx.enter_context(nc.Block())

        @block.sync
        def _(sp):
            def load(dst, src, s):
                sp.dma_start(dst, src).then_inc(s, 16)

            x = a["x"][0].rearrange("(t p) d -> p t d", p=P)
            load(C[:, C_ID:C_ID + P], a["consts"][:, C_ID:C_ID + P], ident_landed)
            load(VR[0:16, 0, :], a["attn_norm_w"][0].rearrange("(r p) -> r p", p=P), attn_landed)

            def load_x(c):
                load(H[:, :, c * CW:(c + 1) * CW], x[:, :, c * CW:(c + 1) * CW], x_landed[c])

            def chunk(w, c0, width, j0, j1, s, d):
                for j in range(j0, j1):
                    n = s + j
                    if n >= RING:
                        sp.wait_ge(lo_ready, n - RING + 1 + d)
                    src = a[w][0, j * SK * P:(j + 1) * SK * P, ds(c0, width)].rearrange("(k p) n -> p k n", p=P)
                    dst = raw[:, n % RING, 0:SK * width].rearrange("p (k n) -> p k n", k=SK)
                    load(dst, src, raw_landed[n % RING])

            for j in range(RING):
                if j % 2 == 0:
                    load_x(j // 2)
                chunk("w_in", 0, CW, j, j + 1, 0, 0)
            load_x(2)
            load_x(3)

            def vectors():
                rows = lambda w, n: w.rearrange("(r p) -> r p", p=P)
                r0 = 16
                for w in ("ffn_norm_w", "g_mix_pre_2", "g_ffn_pre_2", "g_ple_in_2", "ssd_norm_w", "conv_b", "final_norm_w"):
                    n = a[w].shape[-1] // P
                    load(VR[r0:r0 + n, 0, :], rows(a[w][0] if w != "final_norm_w" else a[w], n), vec_landed)
                    r0 += n
                load(VR[0:48, 1, :], a["conv_w"][0].rearrange("j (r p) -> (j r) p", p=P), vec_landed)
                load(VR[48:64, 1, :], a["cmp_pe_k"][0].rearrange("(t l) d -> t (l d)", l=2), vec_landed)
                load(VR[64:80, 1, :], a["cmp_pe_v"][0].rearrange("(t l) d -> t (l d)", l=2), vec_landed)
                for j in range(3):
                    load(VR[0:88, 2 + j, :], rows(a["conv_w_2"][0, j], 88), vec_landed)
                load(VR[0:88, 5, :], rows(a["conv_b_2"][0], 88), vec_landed)

            for name, g in G.items():
                ch, S_, N = g["chunks"], g["S"], g["N"]
                if name in ("ffn1", "ffn2"):
                    (wa, ca, _), (wb, cb, _) = ch[0], ch[1]
                    with sp.Fori(0, NFF) as i:
                        chunk(wa, i * CW + ca, CW, 0, S_, N, i * (2 * S_))
                        chunk(wb, i * CW + cb, CW, 0, S_, N + S_, i * (2 * S_))
                elif name in ("in1", "in2"):
                    n = len(ch) - 2
                    chunk(ch[0][0], 0, CW, RING if name == "in1" else 0, S_, N, 0)
                    if name == "in1":
                        vectors()
                    with sp.Fori(0, n - 1) as i:
                        chunk(ch[0][0], i * CW + CW, CW, 0, S_, N + S_, i * S_)
                    for c in (n, n + 1):
                        chunk(*ch[c], 0, S_, N + c * S_, 0)
                elif S_ == FKT // SK:
                    with sp.Fori(0, 2) as i:
                        chunk(ch[0][0], i * (2 * CW), CW, 0, S_, N, i * (2 * S_))
                        chunk(ch[0][0], i * (2 * CW) + CW, CW, 0, S_, N + S_, i * (2 * S_))
                elif S_ % RING == 0:
                    with sp.Fori(0, len(ch)) as i:
                        chunk(ch[0][0], i * CW, CW, 0, S_, N, i * S_)
                else:
                    for c in range(len(ch)):
                        chunk(*ch[c], 0, S_, N + c * S_, 0)
            if upto >= 99:
                out = a["out"][0].rearrange("(t p) d -> p t d", p=P)
                for c in range(4):
                    sp.wait_ge(h_block, 8 + c + 1)
                    load(out[:, :, c * CW:(c + 1) * CW], H[:, :, c * CW:(c + 1) * CW], out_landed)
                sp.wait_ge(out_landed, 64)

        @block.gpsimd
        def _(pool):
            def load(dst, src, s):
                pool.dma_start(dst, src).then_inc(s, 16)

            pool.memset(ONES[:], 1.0).then_inc(consts_set, 1)
            pool.memset(EPSC[:], EPS).then_inc(consts_set, 1)
            pool.wait_ge(a_lo, KT // 2)
            load(C[:, C_ID + P:C_N], a["consts"][:, C_ID + P:C_N], const_landed)
            load(MF[:], a["masks"], const_landed)
            pool.wait_ge(const_landed, 32)
            pool.tensor_copy(MK[:], MF[:]).then_inc(consts_set, 1)
            load(PIN[:], a["p_2"][0, 0].rearrange("(t p) d -> p t d", p=P), bc_landed)
            for w, o in (("dt_bias", B_DT), ("a_log", B_ALOG), ("d_skip", B_DSK), ("b_fox_f_2", B_BF), ("g_hgrn_out_2", B_GO)):
                n = a[w].shape[-1]
                load(BV[:, o:o + n], a[w][0].partition_broadcast(P), bc_landed)
            load(W1K[:], a["cmp_w1_k"][0].rearrange("(k p) n -> p k n", p=P), cmpw_landed)
            load(W1V[:], a["cmp_w1_v"][0].rearrange("(k p) n -> p k n", p=P), cmpw_landed)
            for i in range(2):
                load(W2K[:, :, i, :], a["cmp_w2_k"][0].rearrange("(k p) n -> p k n", p=P), cmpw_landed)
            load(W2V[:], a["cmp_w2_v"][0].rearrange("(k p) n -> p k n", p=P), cmpw_landed)
            def twice(dst, c0):
                for t in range(NT):
                    for h in range(NKV):
                        src = Z1[:, t, c0 + h * HD:c0 + (h + 1) * HD].unsqueeze(1).to_broadcast([P, 2, HD])
                        ins = pool.tensor_copy(dst[:, t, h], src)
                return ins

            if upto >= 2:
                chunks_read(pool, G["in1"]["C"] + 9)
                pool.wait_ge(xt_turned, 2)
                twice(KVD[:, 0], O_KC)
                twice(KVD[:, 1], O_VC).then_inc(kv_twice, 1)
            if upto >= 3:
                pool.wait_ge(xt_turned, 2)
                pool.memset(KCB[:], 0.0).then_inc(zeroed, 1)
                pool.wait_ge(step_used, G["in1"]["end"])
                pool.wait_ge(xt_a, 1)
                pool.wait_ge(xt_d, 1)
                pool.wait_ge(decay_col, 1)
                heads = lambda x: x.rearrange("p (h d) -> p h d", d=HD)
                for t in range(NT):
                    pool.tensor_tensor(heads(XD[:, t, :]), heads(XT[:, t, :]), bc(SD[:, t, :].unsqueeze(2), 16, HD), ALU.mult)\
                        .then_inc(xd_ready, 1)
                pool.wait_ge(xd_ready, 1)
                pool.tensor_tensor(heads(XS[:]), heads(XD[:, 0, :]), bc(SD[:, 11, :].unsqueeze(2), 16, HD), ALU.mult)\
                    .then_inc(xs_ready, 1)
                chunks_read(pool, G["out1"]["C"])
                n = 0
                for o in (O_KS, O_KW):
                    for t in range(NT):
                        x = Z1[:, t, o:o + NKV * HD].rearrange("p (h d) -> p h d", d=HD)
                        x1, x2 = x[:, :, 0:ROPE_HALF], x[:, :, ROPE_HALF:2 * ROPE_HALF]
                        cs = bc(C[:, C_COS + t * ROPE_HALF:C_COS + (t + 1) * ROPE_HALF].unsqueeze(1), NKV, ROPE_HALF)
                        sn = bc(C[:, C_SIN + t * ROPE_HALF:C_SIN + (t + 1) * ROPE_HALF].unsqueeze(1), NKV, ROPE_HALF)
                        pool.tensor_tensor(RK[:, 0], x1, cs, ALU.mult)
                        pool.tensor_tensor(RK[:, 1], x2, sn, ALU.mult)
                        pool.tensor_tensor(RK[:, 2], x2, cs, ALU.mult)
                        pool.tensor_tensor(RK[:, 3], x1, sn, ALU.mult).then_inc(k_rot, 1)
                        n += 1
                        pool.wait_ge(k_rot, n)
                        pool.tensor_tensor(x1, RK[:, 0], RK[:, 1], ALU.subtract)
                        pool.tensor_tensor(x2, RK[:, 2], RK[:, 3], ALU.add).then_inc(k_rot, 1)
                        n += 1
                        pool.wait_ge(k_rot, n)
                pool.wait_ge(hid_sum, 1)
                pool.memset(HV[:], 0.0).then_inc(zeroed, 1)
                twice(KSD[:, 0], O_KS)
                twice(KSD[:, 1], O_KW).then_inc(k_twice, 1)
                pool.wait_ge(yo_read, 2)
                pool.tensor_tensor(YS[:, 1, :], YS[:, 1, :], YOFF[:], ALU.add).then_inc(yo_added, 1)
                pool.wait_ge(z_silu, 1)
                pool.tensor_tensor(YS[:, 0, :], YS[:, 0, :], Z1[:, 0, O_Z:O_Z + SSD_W], ALU.mult).then_inc(ys_ready, 1)
                pool.wait_ge(yo_added, 1)
                pool.tensor_tensor(YS[:, 1, :], YS[:, 1, :], Z1[:, 1, O_Z:O_Z + SSD_W], ALU.mult).then_inc(ys_ready, 1)
            if upto >= 10:
                pool.wait_ge(f_lo, NFF)
                load(GP[:], a["final_norm_w"].partition_broadcast(P), gain_landed)
                pool.wait_ge(fo_out, 8)
                pool.memset(HS[:], 0.0).then_inc(zeroed, 1)
                pool.wait_ge(hc_out, 1)
                pool.wait_ge(hq_out, 1)
                for l in range(1, 8):
                    b = LEVELS[l - 1]
                    g = LG[l % 2][:].rearrange("p (n a b) -> p n a b", a=2, b=b)
                    q = HQ[:].rearrange("p h (n a b) -> p (h n) a b", a=2, b=b)
                    pool.wait_ge(lv_exp, l + 1)
                    pool.tensor_tensor(g[:, :, 1, :], g[:, :, 1, :], q[:, :, 1, :], ALU.mult).then_inc(lv_mul_q, 1)
                pool.wait_ge(hg_silu, 1)
                pool.wait_ge(hk_turned, 1)
                yg = YG[:].rearrange("p t (h n) -> p t h n", n=P)
                hg = Z2[:, :, O2_HG:O2_HG + W2].rearrange("p t (h n) -> p t h n", n=P)
                for t in range(NT):
                    ins = pool.tensor_tensor(yg[:, t], hg[:, t], bc(BV[:, B_GO:B_GO + P].unsqueeze(1), 8, P), ALU.mult)
                ins.then_inc(hg_gate, 1)
                pool.wait_ge(lv_diff, 8)
                load(GP[:], a["g_mix_post_2"][0].partition_broadcast(P), gain_landed)
            if upto >= 18:
                pool.wait_ge(f_lo, 2 * NFF)
                load(GP[:], a["g_ffn_post_2"][0].partition_broadcast(P), gain_landed)
                pool.wait_ge(gained, 8)
                load(GP[:], a["g_ple_post_2"][0].partition_broadcast(P), gain_landed)

        @block.scalar
        def _(act):
            A = nc.scalar.activation
            chain = [0]
            no = lambda *_: None
            norms = {G["in1"]["C"]: 1, G["in2"]["C"]: 5}

            def link(ins):
                chain[0] += 1
                ins.then_inc(act_chain, 1)
                act.wait_ge(act_chain, chain[0])

            def split(n, d=0, w=None):
                if n >= NSTEP:
                    return
                w = SK * (w or WIDTH[n])
                act.wait_ge(raw_landed[n % RING], 16 * (n // RING + 1) + d * (16 // RING))
                if n >= RING:
                    act.wait_ge(step_used, n - RING + 1 + d)
                A(whi[:, n % RING, 0:w], raw[:, n % RING, 0:w], ACT.Copy).then_inc(hi_ready, 1)

            def stream(g, evac, between={}, loop=True):
                S_, N, n = g["S"], g["N"], len(g["chunks"])

                def one(c, dc, dn):
                    for j in range(S_):
                        if isinstance(dc, int):
                            between.get((c, j), no)()
                        split(N + c * S_ + RING + j, dn)
                    evac(c, dc, N + (c + 1) * S_ + dn)

                for c in range(2):
                    one(c, 0, 0)
                loops = uniform_pairs(g)
                if loops > 2 and loop:
                    with act.Fori(0, loops - 1) as i:
                        for c in (2, 3):
                            one(c, i * 2, i * (2 * S_))
                    done = 2 * loops
                else:
                    done = 2
                for c in range(done, n):
                    one(c, 0, 0)


            def evac_copy(dst, g, scale=1.0):
                def f(c, dc, used):
                    b = 2 * ((g["C"] + c) % 2)
                    w = g["chunks"][c][2]
                    if c == 0 and isinstance(dc, int) and g["C"] in norms:
                        act.wait_ge(rstd_ready, norms[g["C"]])
                    act.wait_ge(step_used, used)
                    A(dst[:, 0, ds(dc * CW + g["chunks"][c][1], w)], pg[:, b, 0:w], ACT.Copy, scale=scale).then_inc(chunk_out[0], 1)
                return f

            def evac_squares(g, n0):
                def f(c, dc, used):
                    if c == 3:
                        A(EPSC[:, 2:3], EPSC[:, 0:1], ACT.Sqrt)
                    b = 2 * ((g["C"] + c) % 2)
                    act.wait_ge(step_used, used)
                    if n0 + c:
                        act.wait_ge(sq_ready, n0 + 2 * c)
                    for t in range(NT):
                        A(JQ[:, t, :], pg[:, b + t, :], ACT.Square, accum_out=PS[:, t, c:c + 1]).then_inc(sq_ready, 1)
                return f

            def norm(i, src, n, junk, dst):
                link(A(junk, src, ACT.Square, accum_out=SM[:, 0:1]))
                act.wait_ge(ss1, i + 1)
                A(SM[:, 2:4], SM[:, 0:2], ACT.Sqrt, scale=1.0 / n, bias=EPSC[:, 0:1]).then_inc(root, 1)
                if dst is not None:
                    act.wait_ge(rstd_ready, i + 1)
                    A(dst, src, ACT.Copy, scale=SM[:, 4:5]).then_inc(xn0, 1)

            def post_root(i):
                act.wait_ge(ss1, i + 1)
                A(SM[:, 2:4], SM[:, 0:2], ACT.Sqrt, scale=1.0 / D, bias=EPSC[:, 0:1]).then_inc(root, 1)

            def prep(p, cols, hi, c):
                for g in (2 * c, 2 * c + 1):
                    act.wait_ge(turned, quarters(p) + g + 1)
                    src = pt[:, g % 4, :].rearrange("p (k n) -> p k n", k=2)
                    for k in range(2):
                        kt = 2 * g + k
                        w = cols(kt)
                        sc = 1.0 if w is None else VT[:, w:w + 1]
                        ins = A(hi[:, kt, :], src[:, k, :], ACT.Copy, scale=sc)
                    ins.then_inc(a_hi, 1)

            def behind(p, cols, hi):
                return {(c + 1, 1): lambda c=c: prep(p, cols, hi, c) for c in range(3)}

            def silu(g):
                act.wait_ge(cv_sum, g + 1)
                A(XC[:, 2 * g:2 * g + 2, :], XC[:, 2 * g:2 * g + 2, :], ACT.Silu).then_inc(cv_act, 1)

            def conv_tap(g):
                act.wait_ge(cv_turned, g + 1)
                act.wait_ge(vec_ready, 4)
                for k in range(2):
                    kt = 2 * g + k
                    ins = A(XC[:, kt, :], pt[:, g % 4, k * TOK:(k + 1) * TOK], ACT.Identity,
                            bias=VT[:, V_CB + kt:V_CB + kt + 1], scale=VT[:, V_CW + 3 * CK1 + kt:V_CW + 3 * CK1 + kt + 1])
                ins.then_inc(cv_first, 1)

            def z_gate():
                chunks_read(act, G["in1"]["C"] + 2)
                A(Z1[:, :, O_Z:O_Z + SSD_W], Z1[:, :, O_Z:O_Z + SSD_W], ACT.Silu).then_inc(z_silu, 1)

            def x_back():
                act.wait_ge(xt_turned, 1)
                act.wait_ge(consts_set, 3)
                for b in range(2):
                    ins = A(XT[:, 0, b * CW:(b + 1) * CW], pt[:, 2 + b, :], ACT.Copy)
                ins.then_inc(xt_a, 1)

            def dt_exps():
                act.wait_ge(dt_u, 1)
                A(SD[:, 2:4, :], SD[:, 2:4, :], ACT.Exp, scale=-1.0).then_inc(dt_exp, 1)
                A(SD[:, 14, :], BV[:, B_ALOG:B_ALOG + 16], ACT.Exp).then_inc(dt_exp, 1)

            def dt_log():
                act.wait_ge(dt_u, 2)
                A(SD[:, 6:8, :], SD[:, 4:6, :], ACT.Ln).then_inc(dt_ln, 1)

            def decays():
                act.wait_ge(acum_ready, 1)
                A(SD[:, 11:13, :], SD[:, 11:13, :], ACT.Exp).then_inc(decay_col, 1)

            def ssd():
                act.wait_ge(seg_ready, 1)
                A(M[:, 0, :, :], M[:, 0, :, :], ACT.Exp).then_inc(seg_exp, 1)
                act.wait_ge(st_sum, 1)
                A(STA[:], pt[:, 1:3, :], ACT.Copy).then_inc(st_ready, 1)
                act.wait_ge(seg_ready, 2)
                A(M[:, 1, :, :], M[:, 1, :, :], ACT.Exp).then_inc(seg_exp, 1)
                act.wait_ge(hid_sum, 1)
                A(HT_[0:60, :], pt[0:60, 0, :], ACT.Silu).then_inc(hid_act, 1)
                act.wait_ge(hid_turned, 1)
                hid = pt[:, 1, 0:256].rearrange("p (b c) -> p b c", c=64)
                A(HK[:], hid[:, 0:2, 0:60], ACT.Copy).then_inc(hid_act, 1)
                act.wait_ge(zeroed, 2)
                for m in range(2):
                    for h in range(NKV):
                        x = hid[:, 2 + m, h * NCMP:(h + 1) * NCMP].unsqueeze(1).to_broadcast([P, 4, NCMP])
                        ins = A(HV[:, m, h, :, 0:NCMP], x, ACT.Copy)
                ins.then_inc(hid_act, 1)
                act.wait_ge(cmp_sum, 1)
                act.wait_ge(zeroed, 1)
                for e in range(2):
                    pr = slice(64 * e, 64 * e + 64)
                    A(KCB[pr, :, 16 * e:16 * e + NCMP], pt[pr, 1, 256:316].rearrange("p (h i) -> p h i", h=NKV), ACT.Copy)\
                        .then_inc(cmp_kv, 1)

            def nsa():
                A(AT[:, 0:96].rearrange("p (t g) -> p t g", t=2), Z1[:, :, O_GATE:O_GATE + 48], ACT.Sigmoid).then_inc(gates, 1)
                act.wait_ge(q_turned, 1)
                A(QT[:, 0:4, :], pg[:, 0:2, :].rearrange("p b (c n) -> p (b c) n", n=TOK), ACT.Copy).then_inc(q_out, 1)
                act.wait_ge(cs_ready, 1)
                A(SC[:], SC[:], ACT.Exp).then_inc(cs_exp, 1)
                act.wait_ge(q_turned, 2)
                A(QT[:, 0:4, :], pg[:, 0:2, :].rearrange("p b (c n) -> p (b c) n", n=TOK), ACT.Copy).then_inc(q_out, 1)
                act.wait_ge(k_turned, 1)
                A(KTT[:, 0, :, :], pt[:, 0:2, :].rearrange("p b (c n) -> p (b c) n", n=TOK), ACT.Copy).then_inc(k_out, 1)
                act.wait_ge(pc_turned, 1)
                A(PCT[:, 0], bank4(0), ACT.Copy).then_inc(pct_ready, 1)
                for u in range(19):
                    if u == 4:
                        act.wait_ge(ys_ready, 2)
                        norm(1, YS[:, 0, :], SSD_W, JUNK[:, 0, :], YS[:, 0, :])
                    if u < 16:
                        nk = P * (1 + units[u][1])
                        act.wait_ge(s_max, u + 1)
                        for j in range(4):
                            x = S[:, u % 3, j // 2, j % 2, 0:nk]
                            ins = A(x, x, ACT.Exp, bias=NM[:, 4 * u + j:4 * u + j + 1], scale=HD ** -0.5,
                                    accum_out=SUM[:, 4 * u + j:4 * u + j + 1])
                        ins.then_inc(s_exp, 1)
                    if 2 <= u <= 17:
                        v = u - 2
                        act.wait_ge(p_turned, v + 1)
                        if v >= 2:
                            act.wait_ge(o_sum, v - 1)
                        A(PT[:, v % 2, 0], bank4(0), ACT.Copy).then_inc(p_out0, 1)
                    if u >= 3 and units[u - 3][0] == 1:
                        v = u - 3
                        b, t, kv = units[v]
                        act.wait_ge(o_sum, v + 1)
                        A(OH1[:, 8 + 2 * kv:10 + 2 * kv, t * P:(t + 1) * P],
                          pt[:, 2 + (v // 2) % 2, 0:256].rearrange("p (x n) -> p x n", x=2), ACT.Copy).then_inc(o_hi, 1)

            units = [(b, t, kv) for kv in range(NKV) for t in range(NT) for b in range(2)]
            NM = AT[:, 96:160]
            SUM = AT[:, 160:224]

            def ffn(g, hooks, between):
                N, S_ = g["N"], g["S"]

                def pair(c, d, between={}):
                    for h in range(4):
                        hooks[h](c, d)
                        for j in range(4):
                            between.get(4 * h + j, no)()
                            split(N + c * 16 + 4 * (h + 1) + j, d * 16, CW)

                pair(0, 0, between)
                with act.Fori(0, NFF - 1) as i:
                    pair(1, i)

            def down(g, hooks, evac, between={}):
                N, S_, n = g["N"], g["S"], len(g["chunks"])
                for c in range(n):
                    for j in range(S_):
                        if c == 0 and j % 4 == 0 and j // 4 < len(hooks):
                            hooks[j // 4]()
                        between.get((c, j), no)()
                        split(N + c * S_ + RING + j)
                    evac(c, 0, N + (c + 1) * S_)

            F1, F2 = G["ffn1"], G["ffn2"]

            def f1_hi(c, d):
                act.wait_ge(f_turned, c + d)
                A(FH[:, ds((d + c - 1) * 4, 4), :], pt[:, 0:2, :].rearrange("p b (c n) -> p (b c) n", n=TOK), ACT.Copy)\
                    .then_inc(f_hi, 1)

            def f1_silu(c, d):
                b = 2 * (F1["C"] % 2)
                act.wait_ge(step_used, F1["N"] + 16 * c + 8 + d * 16)
                if c:
                    chunks_read(act, F1["C"] + 2 * c + d * 2)
                for t in range(NT):
                    A(SG[:, t, :], pg[:, b + t, :], ACT.Silu, scale=SM[:, 4 + t:5 + t]).then_inc(chunk_out[t], 1)

            def f2_up(c, d):
                b = 2 * ((F2["C"] + 1) % 2)
                act.wait_ge(step_used, F2["N"] + 16 * c + d * 16)
                act.wait_ge(c_turned, 2 * c - 1 + d * 2)
                A(UT[:, 0, :], pg[:, b, :], ACT.Copy, scale=SM[:, 4:5]).then_inc(chunk_out[0], 1)
                act.wait_ge(c_sum, 2 * c - 1 + d * 2)
                A(GC[:], GC[:], ACT.Silu).then_inc(c_silu, 1)

            def conv_first(src, dst, k0):
                for k in range(4):
                    ins = A(dst[:, k, :], src[:, k, :], ACT.Identity, bias=VT[:, ds(k0 + V_CB2 + k, 1)],
                            scale=VT[:, ds(k0 + V_CW2 + 2 * 88 + k, 1)])
                ins.then_inc(c_first, 1)

            def f2_conv_up(c, d):
                act.wait_ge(c_turned, 2 * c + d * 2)
                conv_first(pt[:, 2:4, :].rearrange("p b (c n) -> p (b c) n", n=TOK), UC, d * 4 + (c - 1) * 4 + FKT)

            def f2_gate(c, d):
                b = 2 * (F2["C"] % 2)
                act.wait_ge(step_used, F2["N"] + 16 * c + 8 + d * 16)
                if c:
                    act.wait_ge(c_turned, 2 * c + d * 2)
                A(UT[:, 0, :], pg[:, b, :], ACT.Copy, scale=SM[:, 4:5]).then_inc(chunk_out[0], 1)

            def f2_hi(c, d):
                act.wait_ge(c_prod, c + d)
                A(FH[:, ds((d + c - 1) * 4, 4), :], UC[:], ACT.Copy).then_inc(f_hi, 1)

            def f2_conv_gate(c, d):
                act.wait_ge(c_turned, 2 * c + 1 + d * 2)
                if c:
                    act.wait_ge(c_prod, c + d)
                conv_first(pt[:, 0:2, :].rearrange("p b (c n) -> p (b c) n", n=TOK), GC, d * 4 + c * 4)

            def after(f):
                return lambda c, d: f(c, d) if c else None

            def fox_q():
                act.wait_ge(fq_turned, 1)
                A(QF[:], pt[:].rearrange("p b (c n) -> p (b c) n", n=TOK), ACT.Copy).then_inc(fq_out, 1)

            def fox_log():
                act.wait_ge(lf_ready, 1)
                A(SF_[:, 16:32], SF_[:, 16:32], ACT.Exp, scale=-1.0).then_inc(lf_exp, 1)
                act.wait_ge(lf_exp, 1)
                A(SF_[:, 16:32], SF_[:, 16:32], ACT.Ln, bias=1.0).then_inc(lf_ln, 1)

            def fox_sums():
                act.wait_ge(fc_sum, 1)
                A(CB[:], pt[:].rearrange("p b (c n) -> p (b c) n", n=TOK), ACT.Copy, scale=-1.0).then_inc(fc_out, 1)

            def fox(u):
                if u < 8:
                    nk = P * (1 + u // 4)
                    act.wait_ge(fs_max, u + 1)
                    for j in range(2):
                        x = SF[:, u % 2, j, 0:nk]
                        ins = A(x, x, ACT.Exp, bias=SF_[:, 64 + 2 * u + j:65 + 2 * u + j], scale=1.0,
                                accum_out=SF_[:, 80 + 2 * u + j:81 + 2 * u + j])
                    ins.then_inc(fs_exp, 1)
                if 1 <= u < 9:
                    t = (u - 1) // 4
                    act.wait_ge(fp_turned, u)
                    if u >= 3:
                        act.wait_ge(fo_sum, u - 2)
                    A(PF[:, (u - 1) % 2, :, 0:t + 1, :],
                      bank4(2).rearrange("p (j k) n -> p j k n", j=2)[:, :, 0:t + 1, :], ACT.Copy).then_inc(fp_out, 1)

            mix2 = lambda c: lambda: prep(4, lambda k: None, OH2, c)
            f = Z2[:, :, O2_HF:O2_HF + W2]
            tmp = LG1[:].rearrange("p (t n) -> p t n", t=2)

            def hgrn_sig():
                chunks_read(act, G["in2"]["C"] + 11)
                act.wait_ge(fo_out, 8)
                A(YG[:], f, ACT.Sigmoid, scale=-1.0).then_inc(hg_sig, 1)

            def hgrn_log():
                act.wait_ge(act_chain, chain[0])
                A(tmp, tmp, ACT.Ln, bias=1.0).then_inc(hg_ln, 1)

            def hgrn_sums():
                act.wait_ge(hc_sum, 1)
                A(CUM[:].rearrange("p (b n) -> p b n", b=4), pt[:], ACT.Copy).then_inc(hc_out, 1)

            def hgrn():
                act.wait_ge(hk_turned, 1)
                A(HKT[:], pt[:].rearrange("p b (c n) -> p (b c) n", n=TOK), ACT.Copy).then_inc(hk_out, 1)
                for l in range(8):
                    act.wait_ge(lv_diff, l + 1)
                    if l == 0:
                        q2 = lambda x: x[:].rearrange("p (h a n) -> p h a n", h=8, a=4)[:, :, 2, :]
                        A(q2(LG0), q2(CUM), ACT.Exp)
                        x = LG0[:].rearrange("p (h a n) -> p h a n", h=8, a=4)
                        A(x[:, :, 0:2, :], x[:, :, 0:2, :], ACT.Exp)
                        A(x[:, :, 3, :], x[:, :, 3, :], ACT.Exp).then_inc(lv_exp, 1)
                    elif l == 1:
                        x = LG1[:].rearrange("p (h t a n) -> p (h t) a n", h=8, t=2, a=2)
                        y = CUM[:].rearrange("p (h t a n) -> p (h t) a n", h=8, t=2, a=2)
                        A(x[:, :, 0, :], x[:, :, 0, :], ACT.Exp)
                        A(x[:, :, 1, :], y[:, :, 1, :], ACT.Exp).then_inc(lv_exp, 1)
                    else:
                        A(LG[l % 2][:], LG[l % 2][:], ACT.Exp).then_inc(lv_exp, 1)
                A(Z2[:, :, O2_HG:O2_HG + W2], Z2[:, :, O2_HG:O2_HG + W2], ACT.Silu).then_inc(hg_silu, 1)
                mix2(0)()
                A(EPSC[:, 2:3], EPSC[:, 0:1], ACT.Sqrt)
                act.wait_ge(ho_sum, 1)
                sq = LG1[:].rearrange("p (t n) -> p t n", t=2)
                for t in range(NT):
                    A(sq[:, t].rearrange("p (b n) -> p b n", b=2), ho_banks(t), ACT.Square).then_inc(ho_out, 1)
                mix2(1)()
                act.wait_ge(hn_sq, 1)
                A(HN[:, 16:32], HN[:, 0:16], ACT.Sqrt, scale=1.0 / P, bias=EPSC[:, 0:1]).then_inc(hn_root, 1)

            pre0 = lambda c: lambda: prep(0, lambda k: V_ATTN + k, AH, c)
            act.wait_ge(consts_set, 2)
            split(0)
            act.wait_ge(vec_ready, 1)
            pre0(0)()
            split(1)
            split(2)
            pre0(1)()
            split(3)
            stream(G["in1"], evac_copy(Z1, G["in1"], SM[:, 4:5]), {
                (0, 1): pre0(2), (0, 3): pre0(3), (0, 5): lambda: norm(0, H[:, 0, :], D, XN[:, 0, :], None),
                (3, 1): lambda: (conv_tap(0), conv_tap(1)), (3, 3): lambda: (silu(0), silu(1)), (3, 5): z_gate,
                (4, 1): lambda: (conv_tap(2), conv_tap(3)), (4, 3): lambda: (silu(2), silu(3)),
                (5, 1): lambda: (conv_tap(4), conv_tap(5)), (5, 3): lambda: (silu(4), silu(5)), (5, 5): x_back,
                (6, 4): dt_exps, (6, 6): dt_log, (7, 4): decays,
            }, loop=False)
            if upto < 3: return
            ssd()
            if upto < 4: return
            nsa()
            if upto < 5: return
            act.wait_ge(o_out, 8)
            mix1 = lambda c: lambda: prep(1, lambda k: V_SSD + k, OH1, c)
            f1_in = lambda c: lambda: prep(2, lambda k: V_FFN + k, AH, c)
            mix1(0)()
            mix1(1)()
            stream(G["out1"], no, {(1, 2): f1_in(0), (2, 2): f1_in(1), (3, 2): f1_in(2)})
            if upto < 8: return

            def norm_ffn1():
                chunks_read(act, F1["C"])
                norm(2, H[:, 0, :], D, XN[:, 0, :], None)
                act.wait_ge(rstd_ready, 3)

            ffn(F1, [no, after(f1_hi), f1_silu, no], {2: f1_in(3), 4: norm_ffn1})
            if upto < 9: return
            in2 = lambda c: lambda: prep(3, lambda k: V_GMIX + k, AH, c)
            down(G["down1"], [no, lambda: f1_hi(NFF, 0)], no, {(1, 2): in2(0), (2, 2): in2(1), (3, 2): in2(2)})
            if upto < 10: return

            def norm_final():
                chunks_read(act, G["in2"]["C"])
                norm(3, H[:, 0, :], D, XN[:, 0, :], None)

            def norm_mix():
                act.wait_ge(h_ready, 1)
                norm(4, H[:, 0, :], D, XN[:, 0, :], None)

            between = {(0, 2): in2(3), (0, 3): norm_final, (0, 6): norm_mix, (3, 2): fox_q, (7, 1): fox_log, (7, 5): fox_sums,
                       (11, 1): hgrn_sig, (11, 2): lambda: link(A(tmp, f, ACT.Abs)),
                       (11, 3): lambda: link(A(tmp, tmp, ACT.Exp, scale=-1.0)), (11, 4): hgrn_log, (12, 2): hgrn_sums}
            between.update({fox_place(u, 1): lambda u=u: fox(u) for u in range(10)})
            stream(G["in2"], evac_copy(Z2, G["in2"], SM[:, 4:5]), between, loop=False)
            if upto < 13: return
            chunks_read(act, G["out2"]["C"])
            hgrn()
            if upto < 14: return
            stream(G["out2"], evac_squares(G["out2"], 0), {(0, 3): mix2(2), (0, 4): mix2(3)})
            post_root(5)
            f2_in = lambda c: lambda: prep(5, lambda k: V_GFFN + k, AH, c)

            def norm_ffn2():
                act.wait_ge(h_block, 4)
                norm(6, H[:, 0, :], D, XN[:, 0, :], None)
                act.wait_ge(rstd_ready, 7)

            f2_in(0)()
            f2_in(1)()
            if upto < 17: return
            ffn(F2, [after(f2_up), after(f2_conv_up), lambda c, d: (f2_gate(c, d), after(f2_hi)(c, d)), f2_conv_gate],
                {1: f2_in(2), 2: f2_in(3), 4: norm_ffn2})

            def p_parts():
                act.wait_ge(p_tr, 1)
                A(PH[:], pt[:, 3, :].rearrange("p (k n) -> p k n", k=2), ACT.Copy).then_inc(p_hi, 1)

            down(G["down2"], [lambda: f2_up(NFF, 0), lambda: f2_conv_up(NFF, 0), no, lambda: f2_hi(NFF, 0)],
                 evac_squares(G["down2"], 8), {(1, 2): p_parts})
            if upto < 18: return
            post_root(7)
            for c in range(4):
                evac_copy(E, G["proj"])(c, 0, G["proj"]["N"] + c + 1)
                split(G["ple"]["N"] + c)
            ple_in = lambda c: lambda: prep(6, lambda k: V_GPLE + k, OH2, c)

            def norm_ple():
                act.wait_ge(h_block, 8)
                norm(8, H[:, 0, :], D, FO[:, 0, :], None)
                act.wait_ge(rstd_ready, 9)

            ple_in(0)()
            ple_in(1)()
            between = {(0, 1): ple_in(2), (0, 2): ple_in(3), (0, 4): norm_ple}

            def e_squares(c):
                act.wait_ge(e_ready, 2 * c + 2)
                act.wait_ge(sq_ready, 16 + 2 * c)
                for t in range(NT):
                    A(JQ[:, t, :], E[:, t, c * CW:(c + 1) * CW], ACT.Square, accum_out=PS[:, t, c:c + 1]).then_inc(sq_ready, 1)

            g = G["ple"]
            for c in range(4):
                for j in range(8):
                    between.get((c, j), no)()
                    split(g["N"] + c * 8 + RING + j)
                b = 2 * ((g["C"] + c) % 2)
                if c:
                    e_squares(c - 1)
                act.wait_ge(step_used, g["N"] + (c + 1) * 8)
                for t in range(NT):
                    A(GS[:, t, :], pg[:, b + t, :], ACT.Sigmoid, scale=SM[:, 4 + t:5 + t]).then_inc(chunk_out[t], 1)
            A(EPSC[:, 2:3], EPSC[:, 0:1], ACT.Sqrt)
            e_squares(3)
            post_root(9)

        @block.vector
        def _(dve):
            V = nc.vector
            chain = [0]
            no = lambda *_: None
            norms = {G["in1"]["C"]: 1, G["in2"]["C"]: 5}

            def link(ins):
                chain[0] += 1
                ins.then_inc(dve_chain, 1)
                dve.wait_ge(dve_chain, chain[0])

            def split(n, d=0, w=None):
                if n >= NSTEP:
                    return
                w = SK * (w or WIDTH[n])
                dve.wait_ge(hi_ready, n + 1 + d)
                V.tensor_tensor(wlo[:, n % RING, 0:w], raw[:, n % RING, 0:w], whi[:, n % RING, 0:w].bitcast(F32),
                                ALU.subtract).then_inc(lo_ready, 1)

            def stream(g, evac, between={}, loop=True):
                S_, N, n = g["S"], g["N"], len(g["chunks"])

                def one(c, dc, dn):
                    for j in range(S_):
                        if isinstance(dc, int):
                            between.get((c, j), no)()
                        split(N + c * S_ + RING + j, dn)
                    evac(c, dc, N + (c + 1) * S_ + dn)

                for c in range(2):
                    one(c, 0, 0)
                loops = uniform_pairs(g)
                if loops > 2 and loop:
                    with dve.Fori(0, loops - 1) as i:
                        for c in (2, 3):
                            one(c, i * 2, i * (2 * S_))
                    done = 2 * loops
                else:
                    done = 2
                for c in range(done, n):
                    one(c, 0, 0)

            def evac_copy(dst, g, scaled=False):
                def f(c, dc, used):
                    b = 2 * ((g["C"] + c) % 2)
                    w = g["chunks"][c][2]
                    dve.wait_ge(step_used, used)
                    x = dst[:, 1, ds(dc * CW + g["chunks"][c][1], w)]
                    if scaled:
                        ins = V.tensor_scalar(x, pg[:, b + 1, 0:w], SM[:, 5:6], None, ALU.mult)
                    else:
                        ins = V.tensor_copy(x, pg[:, b + 1, 0:w])
                    ins.then_inc(chunk_out[1], 1)
                return f

            def evac_gained(dst, g, n0):
                def f(c, dc, used):
                    b = 2 * ((g["C"] + c) % 2)
                    if c == 0:
                        dve.wait_ge(gain_landed, 32 if n0 == 0 else 48)
                    if c == 3:
                        post_sums(n0 + 8)
                    for t in range(NT):
                        dve.wait_ge(sq_ready, n0 + 2 * c + t + 1)
                        ins = V.tensor_tensor(dst[:, t, c * CW:(c + 1) * CW], pg[:, b + t, :], GP[:, c * CW:(c + 1) * CW], ALU.mult)
                        ins.then_inc(chunk_out[t], 1)
                    V.memset(SM[:, 12:13], 0.0).then_inc(gained, 1)
                return f

            def evac_add(g):
                def f(c, dc, used):
                    b = 2 * ((g["C"] + c) % 2)
                    dve.wait_ge(step_used, used)
                    for t in range(NT):
                        x = H[:, t, ds(dc * CW + c * CW, CW)]
                        V.tensor_tensor(x, pg[:, b + t, :], x, ALU.add).then_inc(chunk_out[t], 1)
                return f

            def refine(y, aa, root_, t1):
                link(V.reciprocal(y, root_))
                link(V.tensor_tensor(t1, y, y, ALU.mult))
                link(V.tensor_tensor(t1, t1, aa, ALU.mult))
                link(V.tensor_scalar(t1, t1, -0.5, 1.5, ALU.mult, ALU.add))

            def rstd(i, n, before=False):
                dve.wait_ge(root, i + 1)
                link(V.tensor_scalar(SM[:, 6:8], SM[:, 0:2], 1.0 / n, EPS, ALU.mult, ALU.add))
                refine(SM[:, 8:10], SM[:, 6:8], SM[:, 2:4], SM[:, 10:12])
                if before:
                    link(V.tensor_tensor(SM[:, 10:12], SM[:, 10:12], SM[:, 4:6], ALU.mult))
                V.tensor_tensor(SM[:, 4:6], SM[:, 8:10], SM[:, 10:12], ALU.mult).then_inc(rstd_ready, 1)
                dve.wait_ge(rstd_ready, i + 1)

            def norm(i, src, n, junk, dst, before=False):
                V.tensor_tensor_reduce(junk, src, src, 1.0, 0.0, ALU.mult, ALU.add, SM[:, 1:2]).then_inc(ss1, 1)
                rstd(i, n, before)
                if dst is not None:
                    V.tensor_scalar(dst, src, SM[:, 5:6], None, ALU.mult).then_inc(xn1, 1)

            def post_sums(n):
                dve.wait_ge(sq_ready, n)
                V.tensor_reduce(SM[:, 0:2], PS[:], AX.X, ALU.add).then_inc(ss1, 1)

            def post_add(x, c):
                for t in range(NT):
                    h = H[:, t, c * CW:(c + 1) * CW]
                    ins = V.scalar_tensor_tensor(h, x[:, t, c * CW:(c + 1) * CW], SM[:, 4 + t:5 + t], h, ALU.mult, ALU.add)
                ins.then_inc(h_block, 1)

            def prep(p, cols, hi, lo, c):
                for g in (2 * c, 2 * c + 1):
                    dve.wait_ge(a_hi, quarters(p) + g + 1)
                    src = pt[:, g % 4, :].rearrange("p (k n) -> p k n", k=2)
                    for k in range(2):
                        kt = 2 * g + k
                        w = cols(kt)
                        sc = 1.0 if w is None else VT[:, w:w + 1]
                        ins = V.scalar_tensor_tensor(lo[:, kt, :], src[:, k, :], sc, hi[:, kt, :].bitcast(F32),
                                                     ALU.mult, ALU.subtract)
                    ins.then_inc(a_lo, 1)

            def kv_flat(b):
                dst, pe_ = (KFK, V_PEK) if b < 2 else (KFV, V_PEV)
                h0 = 2 * (b % 2)
                dve.wait_ge(kc_turned, 4)
                for l in range(2):
                    pr = slice(64 * l, 64 * l + 64)
                    src = pt[pr, b, :].rearrange("p (h a t l) -> p l h t a", h=2, l=2, t=8)[:, l]
                    for th in range(2):
                        for h in range(2):
                            o = dst[pr, 8 * th:8 * th + 8, (h0 + h) * NCMP:(h0 + h + 1) * NCMP]
                            pe2 = VT[pr, pe_ + 8 * th:pe_ + 8 * th + 8].unsqueeze(2).to_broadcast([64, 8, NCMP])
                            ins = V.tensor_tensor(o, src[:, h, :, th:th + NCMP], pe2, ALU.add)
                ins.then_inc(kflat, 1)

            def conv(g):
                dve.wait_ge(cv_first, g + 1)
                for j in (2, 1, 0):
                    for k in range(2):
                        kt = 2 * g + k
                        w = V_CW + j * CK1 + kt
                        x = XC[:, kt, 3 - j:TOK]
                        ins = V.scalar_tensor_tensor(x, pt[:, g % 4, k * TOK:k * TOK + TOK - 3 + j], VT[:, w:w + 1], x,
                                                     ALU.mult, ALU.add)
                    if j:
                        link(ins)
                ins.then_inc(cv_sum, 1)

            dt2 = lambda o: SD[:, o:o + 2, :]

            def dt_abs():
                dve.wait_ge(bc_landed, 96)
                chunks_read(dve, G["in1"]["C"] + 6)
                bias = bc(BV[:, B_DT:B_DT + 16].unsqueeze(1), 2, 16)
                link(V.tensor_tensor(dt2(0), Z1[:, :, O_DT:O_DT + 16], bias, ALU.add))
                V.scalar_tensor_tensor(dt2(2), dt2(0), -1.0, dt2(0), ALU.mult, ALU.max).then_inc(dt_u, 1)
                link(V.tensor_scalar(dt2(0), dt2(0), 0.0, None, ALU.max))

            def dt_plus():
                dve.wait_ge(dt_exp, 1)
                V.tensor_scalar(dt2(4), dt2(2), 1.0, None, ALU.add).then_inc(dt_u, 1)
                dve.wait_ge(dt_u, 2)
                link(V.tensor_scalar(dt2(8), dt2(4), -1.0, None, ALU.add))

            def dt_rest():
                dve.wait_ge(dt_ln, 1)
                link(V.tensor_scalar(dt2(4), dt2(8), 0.0, None, ALU.is_equal))
                link(V.tensor_tensor(dt2(8), dt2(8), dt2(4), ALU.add))
                link(V.tensor_tensor(dt2(6), dt2(6), dt2(4), ALU.add))
                link(V.reciprocal(dt2(8), dt2(8)))
                link(V.tensor_tensor(dt2(6), dt2(6), dt2(8), ALU.mult))
                link(V.tensor_tensor(dt2(6), dt2(6), dt2(2), ALU.mult))
                link(V.tensor_tensor(dt2(0), dt2(0), dt2(6), ALU.add))
                dve.wait_ge(dt_exp, 2)
                link(V.tensor_scalar(dt2(4), dt2(0), -1.0, None, ALU.mult))
                V.tensor_tensor(dt2(2), dt2(4), bc(SD[:, 14, :].unsqueeze(1), 2, 16), ALU.mult).then_inc(adt_ready, 1)

            def x_back():
                dve.wait_ge(xt_turned, 2)
                V.tensor_copy(BT[:].rearrange("p g n -> p (g n)"), pt[:, 2, 0:256])
                for b in range(2):
                    ins = V.tensor_copy(XT[:, 1, b * CW:(b + 1) * CW], pt[:, b, :])
                ins.then_inc(xt_d, 1)

            def a_sums():
                dve.wait_ge(acum_sum, 1)
                link(V.tensor_copy(dt2(8), pt[:, 3, 0:32].rearrange("p (t h) -> p t h", t=2)))
                link(V.tensor_copy(SD[:, 12, :], SD[:, 9, :]))
                V.tensor_tensor(SD[:, 11, :], pt[:, 3, 32:48], SD[:, 8, :], ALU.subtract).then_inc(acum_ready, 1)

            def ssd():
                dve.wait_ge(xt_a, 1)
                dve.wait_ge(xt_d, 1)

                def segments(t):
                    dve.wait_ge(row_sum, t + 1)
                    for b in range(4):
                        ins = V.tensor_tensor(M[:, t, 4 * b:4 * b + 4, :], pg[:, b, :].rearrange("p (h n) -> p h n", h=4),
                                              bc(C[:, C_NEGT:C_NEGT + P].unsqueeze(1), 4, P), ALU.add)
                    link(ins)
                    V.tensor_tensor(M[:, t, :, :], M[:, t, :, :], bc(SD[:, 8 + t, :].unsqueeze(2), 16, P), ALU.subtract)\
                        .then_inc(seg_ready, 1)

                def decayed(t):
                    dve.wait_ge(seg_exp, t + 1)
                    for g in range(SSD_G):
                        cb = pt[:, 3, (2 * t + g) * P:(2 * t + g + 1) * P]
                        ins = V.tensor_tensor(M[:, t, 8 * g:8 * g + 8, :], M[:, t, 8 * g:8 * g + 8, :], bc(cb.unsqueeze(1), 8, P),
                                              ALU.mult)
                    ins.then_inc(m_ready, 1)

                segments(0)
                dve.wait_ge(cb_sum, 1)
                decayed(0)
                segments(1)
                decayed(1)
                dve.wait_ge(hid_sum, 1)
                for t in range(NT):
                    ins = V.tensor_tensor(YS[:, t, :].rearrange("p (h d) -> p h d", d=HD),
                                          XT[:, t, :].rearrange("p (h d) -> p h d", d=HD),
                                          bc(BV[:, B_DSK:B_DSK + 16].unsqueeze(2), 16, HD), ALU.mult)
                link(ins)
                for t in range(NT):
                    dve.wait_ge(yd_sum, t + 1)
                    for b in range(2):
                        x = YS[:, t, b * CW:(b + 1) * CW]
                        ins = V.tensor_tensor(x, pg[:, 2 * t + b, :], x, ALU.add)
                    ins.then_inc(yd_read, 1)
                dve.wait_ge(yo_sum, 1)
                for b in range(2):
                    V.tensor_tensor(YOFF[:, b * CW:(b + 1) * CW].rearrange("p (h d) -> p h d", d=HD),
                                    pt[:, 3 * b, :].rearrange("p (h d) -> p h d", d=HD),
                                    bc(SD[:, 12, 8 * b:8 * b + 8].unsqueeze(2), 8, HD), ALU.mult).then_inc(yo_read, 1)
                dve.wait_ge(cmp_sum, 1)
                for h in range(NKV):
                    V.tensor_tensor(BD[:, h, :, :], bc(pt[:, 2, h * HD:(h + 1) * HD].unsqueeze(1), 4, HD),
                                    bc(C[:, C_BLK:C_BLK + 4].unsqueeze(2), 4, HD), ALU.mult).then_inc(cmp_kv, 1)

            units = [(b, t, kv) for kv in range(NKV) for t in range(NT) for b in range(2)]
            NM = AT[:, 96:160]
            SUM = AT[:, 160:224]

            RT = XT[:, 0, 0:512].rearrange("p (a h d) -> p a h d", a=4, h=16)
            CM = XT[:, 0, 512:512 + NT * NCMP]
            CX = XT[:, 0, 600:664]

            def nsa():
                V.memset(PC[:], 0.0)
                dve.wait_ge(q_turned, 1)
                V.tensor_copy(QT[:, 4:8, :], pg[:, 2:4, :].rearrange("p b (c n) -> p (b c) n", n=TOK)).then_inc(q_out, 1)
                for o, h in ((O_Q, NH),):
                    for t in range(NT):
                        x = Z1[:, t, o:o + h * HD].rearrange("p (h d) -> p h d", d=HD)
                        x1, x2 = x[:, :, 0:ROPE_HALF], x[:, :, ROPE_HALF:2 * ROPE_HALF]
                        cs = bc(C[:, C_COS + t * ROPE_HALF:C_COS + (t + 1) * ROPE_HALF].unsqueeze(1), h, ROPE_HALF)
                        sn = bc(C[:, C_SIN + t * ROPE_HALF:C_SIN + (t + 1) * ROPE_HALF].unsqueeze(1), h, ROPE_HALF)
                        tmp = [RT[:, i, 0:h, :] for i in range(4)]
                        V.tensor_tensor(tmp[0], x1, cs, ALU.mult)
                        V.tensor_tensor(tmp[1], x2, sn, ALU.mult)
                        V.tensor_tensor(tmp[2], x2, cs, ALU.mult)
                        link(V.tensor_tensor(tmp[3], x1, sn, ALU.mult))
                        V.tensor_tensor(x1, tmp[0], tmp[1], ALU.subtract)
                        link(V.tensor_tensor(x2, tmp[2], tmp[3], ALU.add))
                V.memset(RT[:, 0, 0, 0:1], 0.0).then_inc(roped, 1)
                dve.wait_ge(cs_sum, 1)
                for t in range(NT):
                    mask = C[:, C_CMP + t * NCMP:C_CMP + (t + 1) * NCMP]
                    ins = V.scalar_tensor_tensor(SC[:, t], pt[:, 0, t * 256:t * 256 + 256].rearrange("p (h i) -> p h i", i=16)[:, :, 0:NCMP],
                                                 HD ** -0.5, bc(mask.unsqueeze(1), NH, NCMP), ALU.mult, ALU.mult)
                ins.then_inc(cs_read, 1)
                dve.wait_ge(cs_read, 1)
                link(V.tensor_scalar(CM[:], C[:, C_CMP:C_CMP + NT * NCMP], 1.0, 1e30, ALU.subtract, ALU.mult))
                for t in range(NT):
                    ins = V.tensor_tensor(SC[:, t], SC[:, t], bc(CM[:, t * NCMP:(t + 1) * NCMP].unsqueeze(1), 16, NCMP), ALU.add)
                link(ins)
                flat = SC[:].rearrange("p t h i -> p (t h) i")
                link(V.tensor_reduce(CX[:, 0:32], flat, AX.X, ALU.max))
                V.tensor_tensor(flat, flat, bc(CX[:, 0:32].unsqueeze(2), 32, NCMP), ALU.subtract).then_inc(cs_ready, 1)
                dve.wait_ge(q_turned, 2)
                V.tensor_copy(QT[:, 4:8, :], pg[:, 2:4, :].rearrange("p b (c n) -> p (b c) n", n=TOK)).then_inc(q_out, 1)
                dve.wait_ge(k_turned, 1)
                V.tensor_copy(KTT[:, 1, :, :], pt[:, 2:4, :].rearrange("p b (c n) -> p (b c) n", n=TOK)).then_inc(k_out, 1)
                dve.wait_ge(cs_exp, 1)
                link(V.tensor_reduce(CX[:, 32:64], flat, AX.X, ALU.add))
                link(V.reciprocal(CX[:, 0:32], CX[:, 32:64]))
                dve.wait_ge(gates, 1)
                link(V.tensor_tensor(CX[:, 32:64], CX[:, 0:32], AT[:, 0:96].rearrange("p (n g) -> p n g", g=3)[:, :, 0], ALU.mult))
                link(V.tensor_tensor(flat, flat, bc(CX[:, 32:64].unsqueeze(2), 32, NCMP), ALU.mult))
                for t in range(NT):
                    ins = V.tensor_tensor(PC[:, t, :, 0:NCMP], SC[:, t], bc(C[:, C_CMP + t * NCMP:C_CMP + (t + 1) * NCMP].unsqueeze(1), 16, NCMP),
                                          ALU.mult)
                ins.then_inc(pc_ready, 1)
                dve.wait_ge(pc_turned, 1)
                V.tensor_copy(PCT[:, 1], bank4(1)).then_inc(pct_ready, 1)
                for u in range(19):
                    if u == 4:
                        dve.wait_ge(ys_ready, 2)
                        norm(1, YS[:, 1, :], SSD_W, JUNK[:, 1, :], YS[:, 1, :])
                    if u < 16:
                        b, t, kv = units[u]
                        nk = P * (1 + t)
                        dve.wait_ge(s_sum, u + 1)
                        if u >= 3:
                            dve.wait_ge(p_turned, u - 2)
                        mask = C[:, C_ZC + (P if t == 0 else 0):C_ZC + 2 * P]
                        for e in range(2):
                            V.tensor_tensor(S[:, u % 3, e, :, 0:nk], pg[:, 2 * (u % 2) + e, 0:2 * nk].rearrange("p (a n) -> p a n", a=2),
                                            bc(mask.unsqueeze(1), 2, nk), ALU.add).then_inc(s_masked, 1)
                        dve.wait_ge(s_masked, 2 * u + 2)
                        link(V.tensor_reduce(NM[:, 4 * u:4 * u + 4], S[:, u % 3, :, :, 0:nk].rearrange("p e a n -> p (e a) n"), AX.X, ALU.max))
                        V.tensor_scalar(NM[:, 4 * u:4 * u + 4], NM[:, 4 * u:4 * u + 4], -HD ** -0.5, None, ALU.mult).then_inc(s_max, 1)
                    if 1 <= u <= 16:
                        v = u - 1
                        b, t, kv = units[v]
                        nk = P * (1 + t)
                        co = CX[:, 0:4]
                        dve.wait_ge(s_exp, v + 1)
                        link(V.reciprocal(co, SUM[:, 4 * v:4 * v + 4]))
                        g4 = AT[:, 48 * t + 12 * kv:48 * t + 12 * kv + 12].rearrange("p (x e g) -> p g e x", e=2, g=3)[:, 1 + b]
                        link(V.tensor_tensor(co.rearrange("p (e x) -> p e x", e=2), co.rearrange("p (e x) -> p e x", e=2), g4, ALU.mult))
                        x = S[:, v % 3, :, :, 0:nk].rearrange("p e a n -> p (e a) n")
                        V.tensor_tensor(x, x, bc(co.unsqueeze(2), 4, nk), ALU.mult).then_inc(s_scaled, 1)
                        dve.wait_ge(s_scaled, v + 1)
                    if 2 <= u <= 17 and units[u - 2][1] == 1:
                        v = u - 2
                        dve.wait_ge(p_turned, v + 1)
                        if v >= 2:
                            dve.wait_ge(o_sum, v - 1)
                        V.tensor_copy(PT[:, v % 2, 1], bank4(1)).then_inc(p_out1, 1)
                    if u >= 3 and units[u - 3][0] == 1:
                        v = u - 3
                        b, t, kv = units[v]
                        dve.wait_ge(o_hi, v // 2 + 1)
                        V.tensor_tensor(OL1[:, 8 + 2 * kv:10 + 2 * kv, t * P:(t + 1) * P],
                                        pt[:, 2 + (v // 2) % 2, 0:256].rearrange("p (x n) -> p x n", x=2),
                                        OH1[:, 8 + 2 * kv:10 + 2 * kv, t * P:(t + 1) * P].bitcast(F32), ALU.subtract).then_inc(o_out, 1)

            def ffn(g, hooks, between):
                N = g["N"]

                def pair(c, d, between={}):
                    for h in range(4):
                        hooks[h](c, d)
                        for j in range(4):
                            between.get(4 * h + j, no)()
                            split(N + c * 16 + 4 * (h + 1) + j, d * 16, CW)

                pair(0, 0, between)
                with dve.Fori(0, NFF - 1) as i:
                    pair(1, i)

            def down(g, hooks, evac, between={}):
                N, S_, n = g["N"], g["S"], len(g["chunks"])
                for c in range(n):
                    for j in range(S_):
                        if c == 0 and j % 4 == 0 and j // 4 < len(hooks):
                            hooks[j // 4]()
                        between.get((c, j), no)()
                        split(N + c * S_ + RING + j)
                    evac(c, 0, N + (c + 1) * S_)

            F1, F2 = G["ffn1"], G["ffn2"]

            def after(f):
                return lambda c, d: f(c, d) if c else None

            def f1_h(c, d):
                b = 2 * ((F1["C"] + 1) % 2)
                dve.wait_ge(step_used, F1["N"] + 16 * c + d * 16)
                chunks_read(dve, F1["C"] + 2 * c - 1 + d * 2)
                if c > 1 or not isinstance(d, int):
                    dve.wait_ge(f_turned, c - 1 + d)
                for t in range(NT):
                    V.scalar_tensor_tensor(HT[:, t, :], pg[:, b + t, :], SM[:, 4 + t:5 + t], SG[:, t, :], ALU.mult, ALU.mult)\
                        .then_inc(chunk_out[t], 1)

            def f1_lo(c, d):
                dve.wait_ge(f_hi, c + d)
                x = FH[:, ds((d + c - 1) * 4, 4), :].bitcast(F32)
                V.tensor_tensor(FL[:, ds((d + c - 1) * 4, 4), :], pt[:, 0:2, :].rearrange("p b (c n) -> p (b c) n", n=TOK), x, ALU.subtract)\
                    .then_inc(f_lo, 1)

            def f2_up(c, d):
                b = 2 * ((F2["C"] + 1) % 2)
                dve.wait_ge(step_used, F2["N"] + 16 * c + d * 16)
                dve.wait_ge(c_turned, 2 * c - 1 + d * 2)
                V.tensor_scalar(UT[:, 1, :], pg[:, b + 1, :], SM[:, 5:6], None, ALU.mult).then_inc(chunk_out[1], 1)

            def conv_rest(src, dst, k0, nth):
                dve.wait_ge(c_first, nth)
                for j in (1, 0):
                    for k in range(4):
                        x = dst[:, k, 2 - j:TOK]
                        ins = V.scalar_tensor_tensor(x, src[:, k, 0:TOK - 2 + j], VT[:, ds(k0 + V_CW2 + j * 88 + k, 1)], x,
                                                     ALU.mult, ALU.add)
                    if j:
                        ins.then_inc(c_part, 1)
                        dve.wait_ge(c_part, nth)
                ins.then_inc(c_sum, 1)

            def f2_conv_up(c, d):
                conv_rest(pt[:, 2:4, :].rearrange("p b (c n) -> p (b c) n", n=TOK), UC, d * 4 + (c - 1) * 4 + FKT, 2 * c + d * 2)
                dve.wait_ge(c_sum, 2 * c + d * 2)
                dve.wait_ge(c_silu, c + d)
                V.tensor_tensor(UC[:], UC[:], GC[:], ALU.mult).then_inc(c_prod, 1)

            def f2_gate(c, d):
                b = 2 * (F2["C"] % 2)
                dve.wait_ge(step_used, F2["N"] + 16 * c + 8 + d * 16)
                if c:
                    dve.wait_ge(c_turned, 2 * c + d * 2)
                V.tensor_scalar(UT[:, 1, :], pg[:, b + 1, :], SM[:, 5:6], None, ALU.mult).then_inc(chunk_out[1], 1)

            def f2_lo(c, d):
                dve.wait_ge(f_hi, NFF + c + d)
                V.tensor_tensor(FL[:, ds((d + c - 1) * 4, 4), :], UC[:], FH[:, ds((d + c - 1) * 4, 4), :].bitcast(F32), ALU.subtract)\
                    .then_inc(f_lo, 1)

            def f2_conv_gate(c, d):
                conv_rest(pt[:, 0:2, :].rearrange("p b (c n) -> p (b c) n", n=TOK), GC, d * 4 + c * 4, 2 * c + 1 + d * 2)

            def fox_abs():
                chunks_read(dve, G["in2"]["C"] + 7)
                v, e = SF_[:, 0:16], SF_[:, 16:32]
                b8 = bc(BV[:, B_BF:B_BF + 8].unsqueeze(1), 2, 8)
                link(V.tensor_tensor(v.rearrange("p (t h) -> p t h", t=2), Z2[:, :, O2_F:O2_F + 8], b8, ALU.add))
                V.scalar_tensor_tensor(e, v, -1.0, v, ALU.mult, ALU.max).then_inc(lf_ready, 1)

            def fox_log():
                v, e = SF_[:, 0:16], SF_[:, 16:32]
                dve.wait_ge(lf_ln, 1)
                V.scalar_tensor_tensor(SF_[:, 32:48], v, 0.0, e, ALU.min, ALU.subtract).then_inc(lf_ready, 1)

            def fox_k():
                dve.wait_ge(fq_turned, 2)
                V.tensor_copy(KF2[:], pt[:].rearrange("p b (c n) -> p (b c) n", n=TOK)).then_inc(fk_out, 1)

            def fox(u):
                if u == 0:
                    dve.wait_ge(fc_out, 1)
                if u < 8:
                    t, hp = u // 4, u % 4
                    nk = P * (1 + t)
                    dve.wait_ge(fs_sum, u + 1)
                    if u >= 2:
                        dve.wait_ge(fp_turned, u - 1)
                    x = SF[:, u % 2, :, 0:nk]
                    link(V.scalar_tensor_tensor(x, pt[:, u % 2, 0:2 * nk].rearrange("p (j n) -> p j n", j=2), P ** -0.5,
                                                CB[:, 2 * hp:2 * hp + 2, 0:nk], ALU.mult, ALU.add))
                    y = SF[:, u % 2, :, nk - P:nk]
                    link(V.tensor_tensor(y, y, bc(C[:, C_ZC + P:C_ZC + 2 * P].unsqueeze(1), 2, P), ALU.add))
                    m = SF_[:, 64 + 2 * u:66 + 2 * u]
                    link(V.tensor_reduce(m, x, AX.X, ALU.max))
                    V.tensor_scalar(m, m, -1.0, None, ALU.mult).then_inc(fs_max, 1)
                if u >= 2:
                    w = u - 2
                    t, hp = w // 4, w % 4
                    dve.wait_ge(fs_exp, w + 1)
                    link(V.reciprocal(SF_[:, 100:102], SF_[:, 80 + 2 * w:82 + 2 * w]))
                    dve.wait_ge(fo_sum, w + 1)
                    V.tensor_tensor(YF[:, t, hp * 256:(hp + 1) * 256].rearrange("p (j n) -> p j n", j=2),
                                    pt[:, 3, 0:256].rearrange("p (j n) -> p j n", j=2),
                                    bc(SF_[:, 100:102].unsqueeze(2), 2, P), ALU.mult).then_inc(fo_out, 1)
                    dve.wait_ge(fo_out, w + 1)

            mix2 = lambda c: lambda: prep(4, lambda k: None, OH2, OL2, c)

            def hgrn_min():
                f = Z2[:, :, O2_HF:O2_HF + W2]
                dve.wait_ge(hg_ln, 1)
                V.tensor_scalar(f, f, 0.0, None, ALU.min).then_inc(hg_lf, 1)

            def hgrn_logf():
                f = Z2[:, :, O2_HF:O2_HF + W2]
                dve.wait_ge(hg_lf, 1)
                V.tensor_tensor(f, f, LG1[:].rearrange("p (t n) -> p t n", t=2), ALU.subtract).then_inc(hg_lf, 1)

            def hgrn():
                dve.wait_ge(hc_out, 1)

                def diff(l):
                    if l == 1:
                        dve.wait_ge(hg_lf, 2)
                    if l >= 2:
                        dve.wait_ge(lv_sum, lv_units(l - 2))
                    g = LG[l % 2]
                    if l == 0:
                        x = g[:].rearrange("p (h a n) -> p h a n", h=8, a=4)
                        c = CUM[:].rearrange("p (h a n) -> p h a n", h=8, a=4)
                        link(V.tensor_tensor(x[:, :, 0:2, :], c[:, :, 0:2, 63:64].to_broadcast([P, 8, 2, 64]), c[:, :, 0:2, :], ALU.subtract))
                        V.tensor_tensor(x[:, :, 0, :], x[:, :, 0, :], c[:, :, 1, 63:64].to_broadcast([P, 8, 64]), ALU.add)
                        V.tensor_tensor(x[:, :, 3, :], c[:, :, 3, :], c[:, :, 2, 63:64].to_broadcast([P, 8, 64]), ALU.add).then_inc(lv_diff, 1)
                    elif l == 1:
                        x = g[:].rearrange("p (n a b) -> p n a b", a=2, b=64)
                        c = CUM[:].rearrange("p (n a b) -> p n a b", a=2, b=64)
                        V.tensor_tensor(x[:, :, 0, :], c[:, :, 0, 63:64].to_broadcast([P, 16, 64]), c[:, :, 0, :], ALU.subtract).then_inc(lv_diff, 1)
                    else:
                        b = LEVELS[l - 1]
                        n = HG_N * TOK // (2 * b)
                        x = g[:].rearrange("p (n a b) -> p n a b", a=2, b=b)
                        c = CUM[:].rearrange("p (n a b) -> p n a b", a=2, b=b)
                        ref = c[:, :, 0, b - 1:b].to_broadcast([P, n, b])
                        V.tensor_tensor(x[:, :, 0, :], ref, c[:, :, 0, :], ALU.subtract)
                        V.tensor_tensor(x[:, :, 1, :], c[:, :, 1, :], ref, ALU.subtract).then_inc(lv_diff, 1)

                def mul(l):
                    dve.wait_ge(lv_exp, l + 1)
                    b = P if l == 0 else LEVELS[l - 1]
                    g = LG[l % 2][:].rearrange("p (n a b) -> p n a b", a=2, b=b)
                    k = HKT[:].rearrange("p h (n a b) -> p (h n) a b", a=2, b=b)
                    q = HQ[:].rearrange("p h (n a b) -> p (h n) a b", a=2, b=b)
                    ins = V.tensor_tensor(g[:, :, 0, :], g[:, :, 0, :], k[:, :, 0, :], ALU.mult)
                    if l == 0:
                        ins = V.tensor_tensor(g[:, :, 1, :], g[:, :, 1, :], q[:, :, 1, :], ALU.mult)
                    ins.then_inc(lv_mul, 1)

                def take(l):
                    if l == 0:
                        dve.wait_ge(lv_sum, 3)
                        V.tensor_copy(HX[:], lv_banks(2)).then_inc(lv_out, 1)
                        return
                    for t in range(NT):
                        u = t if l == 8 else 1 + 2 * l + t
                        dve.wait_ge(lv_sum, u + 1)
                        if u >= 3:
                            dve.wait_ge(lv_out, u - 1)
                        mask = bc(MK[:, (l - 1) * P:l * P].unsqueeze(1), 8, P)
                        V.copy_predicated(HS[:, t, :, :], mask, lv_banks(u)).then_inc(lv_out, 1)

                dve.wait_ge(consts_set, 3)
                diff(0)
                dve.wait_ge(hq_turned, 1)
                V.tensor_copy(HQ[:], pg[:].rearrange("p b (c n) -> p (b c) n", n=TOK)).then_inc(hq_out, 1)
                diff(1)
                dve.wait_ge(hk_out, 1)
                dve.wait_ge(hq_out, 1)
                for l in range(8):
                    mul(l)
                    if l == 0:
                        dve.wait_ge(zeroed, 3)
                        take(8)
                    if 1 <= l < 7:
                        diff(l + 1)
                    if l:
                        take(l - 1)
                take(7)
                mix2(0)()
                y = YG[:].rearrange("p t (h n) -> p (t h) n", n=P)
                sq = LG1[:].rearrange("p (h n) -> p h n", n=P)
                dve.wait_ge(hg_gate, 1)
                for t in range(NT):
                    dve.wait_ge(ho_out, t + 1)
                    yt = YG[:, t, :].rearrange("p (b n) -> p b n", b=2)
                    V.tensor_tensor(yt, ho_banks(t), yt, ALU.mult).then_inc(ho_read, 1)
                V.tensor_reduce(HN[:, 0:16], sq, AX.X, ALU.add).then_inc(hn_sq, 1)
                mix2(1)()
                dve.wait_ge(hn_root, 1)
                link(V.tensor_scalar(HN[:, 32:48], HN[:, 0:16], 1.0 / P, EPS, ALU.mult, ALU.add))
                refine(HN[:, 0:16], HN[:, 32:48], HN[:, 16:32], HN[:, 48:64])
                link(V.tensor_tensor(HN[:, 0:16], HN[:, 0:16], HN[:, 48:64], ALU.mult))
                V.tensor_tensor(y, y, bc(HN[:, 0:16].unsqueeze(2), 16, P), ALU.mult).then_inc(yg_ready, 1)

            dve.wait_ge(vec_turned, 1)
            V.tensor_copy(VT[:, 0:16], pg[:, 0, 0:16]).then_inc(vec_ready, 1)
            dve.wait_ge(vec_ready, 1)

            def vectors():
                dve.wait_ge(vec_turned, 2)
                V.tensor_copy(VT[:, 16:196], pt[:, 0, 16:196]).then_inc(vec_ready, 1)
                V.tensor_copy(VT[:, 196:V_N], pt[:, 1, 0:V_N - 196]).then_inc(vec_ready, 1)
                dve.wait_ge(vec_ready, 3)
                g = VT[:, V_GMIX:V_GMIX + KT]
                V.tensor_tensor(g, g, VT[:, V_FIN:V_FIN + KT], ALU.mult).then_inc(vec_ready, 1)

            pre0 = lambda c: lambda: prep(0, lambda k: V_ATTN + k, AH, AL, c)
            split(0)
            pre0(0)()
            split(1)
            split(2)
            pre0(1)()
            split(3)
            stream(G["in1"], evac_copy(Z1, G["in1"], True), {
                (0, 1): pre0(2), (0, 3): pre0(3), (0, 5): lambda: norm(0, H[:, 1, :], D, XN[:, 1, :], None), (2, 2): vectors,
                (3, 1): lambda: conv(0), (3, 2): lambda: conv(1), (4, 1): lambda: conv(2), (4, 2): lambda: conv(3),
                (5, 1): lambda: conv(4), (5, 2): lambda: conv(5), (6, 1): x_back,
                (6, 3): dt_abs, (6, 5): dt_plus, (6, 7): dt_rest, (7, 3): a_sums,
                (9, 7): lambda: kv_flat(0), (10, 0): lambda: kv_flat(1), (10, 1): lambda: kv_flat(2), (10, 3): lambda: kv_flat(3),
            }, loop=False)
            if upto < 3: return
            dve.wait_ge(step_used, G["in1"]["end"])
            ssd()
            if upto < 4: return
            nsa()
            if upto < 5: return
            mix1 = lambda c: lambda: prep(1, lambda k: V_SSD + k, OH1, OL1, c)
            f1_in = lambda c: lambda: prep(2, lambda k: V_FFN + k, AH, AL, c)
            mix1(0)()
            mix1(1)()
            stream(G["out1"], evac_add(G["out1"]),
                   {(1, 2): f1_in(0), (2, 2): f1_in(1), (3, 2): f1_in(2)})
            if upto < 8: return

            def norm_ffn1():
                chunks_read(dve, F1["C"])
                norm(2, H[:, 1, :], D, XN[:, 1, :], None)

            ffn(F1, [after(f1_h), after(f1_lo), no, no], {2: f1_in(3), 4: norm_ffn1})
            if upto < 9: return
            in2 = lambda c: lambda: prep(3, lambda k: V_GMIX + k, AH, AL, c)
            down(G["down1"], [lambda: f1_h(NFF, 0), lambda: f1_lo(NFF, 0)], evac_add(G["down1"]),
                 {(1, 2): in2(0), (2, 2): in2(1), (3, 2): in2(2)})
            if upto < 10: return

            def norm_final():
                chunks_read(dve, G["in2"]["C"])
                norm(3, H[:, 1, :], D, XN[:, 1, :], None)

            def apply_final():
                dve.wait_ge(gain_landed, 16)
                for t in range(NT):
                    ins = V.scalar_tensor_tensor(H[:, t, :], H[:, t, :], SM[:, 4 + t:5 + t], GP[:], ALU.mult, ALU.mult)
                ins.then_inc(h_ready, 1)

            def norm_mix():
                dve.wait_ge(h_ready, 1)
                norm(4, H[:, 1, :], D, XN[:, 1, :], None, before=True)

            between = {(0, 2): in2(3), (0, 3): norm_final, (0, 4): apply_final, (0, 6): norm_mix, (5, 2): fox_k,
                       (7, 0): fox_abs, (7, 2): fox_log, (11, 5): hgrn_min, (11, 6): hgrn_logf}
            between.update({fox_place(u, 0): lambda u=u: fox(u) for u in range(10)})
            stream(G["in2"], evac_copy(Z2, G["in2"], True), between, loop=False)
            if upto < 13: return
            dve.wait_ge(step_used, G["in2"]["end"])
            chunks_read(dve, G["out2"]["C"])
            hgrn()
            if upto < 14: return
            stream(G["out2"], evac_gained(MIX, G["out2"], 0), {(0, 3): mix2(2), (0, 4): mix2(3)})
            f2_in = lambda c: lambda: prep(5, lambda k: V_GFFN + k, AH, AL, c)
            rstd(5, D)
            dve.wait_ge(gained, 4)
            post_add(MIX, 0)
            post_add(MIX, 1)
            f2_in(0)()
            post_add(MIX, 2)
            f2_in(1)()
            post_add(MIX, 3)
            if upto < 17: return

            def norm_ffn2():
                dve.wait_ge(h_block, 4)
                norm(6, H[:, 1, :], D, XN[:, 1, :], None)

            ffn(F2, [after(f2_up), after(f2_conv_up), lambda c, d: (f2_gate(c, d), after(f2_lo)(c, d)), f2_conv_gate],
                {1: f2_in(2), 2: f2_in(3), 4: norm_ffn2})

            def p_parts():
                dve.wait_ge(p_hi, 1)
                V.tensor_tensor(PL[:], pt[:, 3, :].rearrange("p (k n) -> p k n", k=2), PH[:].bitcast(F32), ALU.subtract).then_inc(p_lo, 1)

            down(G["down2"], [lambda: f2_up(NFF, 0), lambda: f2_conv_up(NFF, 0), no, lambda: f2_lo(NFF, 0)],
                 evac_gained(FO, G["down2"], 8), {(1, 2): p_parts})
            if upto < 18: return
            def proj(c):
                evac_copy(E, G["proj"])(c, 0, G["proj"]["N"] + c + 1)
                split(G["ple"]["N"] + c)

            proj(0)
            rstd(7, D)
            dve.wait_ge(gained, 8)
            post_add(FO, 0)
            proj(1)
            post_add(FO, 1)
            proj(2)
            post_add(FO, 2)
            proj(3)
            post_add(FO, 3)
            ple_in = lambda c: lambda: prep(6, lambda k: V_GPLE + k, OH2, OL2, c)

            def norm_ple():
                dve.wait_ge(h_block, 8)
                norm(8, H[:, 1, :], D, FO[:, 1, :], None)

            ple_in(0)()
            ple_in(1)()
            between = {(0, 1): ple_in(2), (0, 2): ple_in(3), (0, 4): norm_ple}

            def e_gained(c):
                dve.wait_ge(gain_landed, 64)
                dve.wait_ge(sq_ready, 16 + 2 * c + 2)
                for t in range(NT):
                    x = E[:, t, c * CW:(c + 1) * CW]
                    ins = V.tensor_tensor(x, x, GP[:, c * CW:(c + 1) * CW], ALU.mult)
                ins.then_inc(gained, 1)

            g = G["ple"]
            for c in range(4):
                for j in range(8):
                    between.get((c, j), no)()
                    split(g["N"] + c * 8 + RING + j)
                for t in range(NT):
                    dve.wait_ge(chunk_out[t], g["C"] + c + 1)
                    x = E[:, t, c * CW:(c + 1) * CW]
                    V.tensor_tensor(x, x, GS[:, t, :], ALU.mult).then_inc(e_ready, 1)
                if c:
                    e_gained(c - 1)
            post_sums(24)
            e_gained(3)
            rstd(9, D)
            dve.wait_ge(gained, 12)
            for c in range(4):
                post_add(E, c)

        @block.tensor
        def _(pe):
            mm, tr = nc.tensor.matmul, nc.tensor.transpose
            no = lambda *_: None

            def step(n, d, b, kt0, w, first, last, hi=AH, lo=AL):
                pe.wait_ge(lo_ready, n + 1 + d)
                for k in range(SK):
                    wh = whi[:, n % RING, k * w:(k + 1) * w]
                    wl = wlo[:, n % RING, k * w:(k + 1) * w]
                    for t in range(NT):
                        xh = hi[:, kt0 + k, t * P:(t + 1) * P]
                        xl = lo[:, kt0 + k, t * P:(t + 1) * P]
                        o = pg[:, b + t, 0:w]
                        mm(o, xh, wh, start=first and k == 0, stop=False)
                        mm(o, xh, wl, start=False, stop=False)
                        ins = mm(o, xl, wh, start=False, stop=last and k == SK - 1)
                ins.then_inc(step_used, 1)

            def chunk(g, c, j0=0, j1=None, dc=0, dn=0, hi=AH, lo=AL, before=None):
                C_ = g["C"] + c
                w = g["chunks"][c][2]
                for j in range(j0, g["S"] if j1 is None else j1):
                    if j == 0 and (C_ >= 2 or not isinstance(dc, int)):
                        chunks_read(pe, C_ - 1 + dc)
                    if before:
                        before(j)
                    step(g["N"] + c * g["S"] + j, dn, 2 * (C_ % 2), SK * j, w, j == 0, j == g["S"] - 1, hi, lo)

            def turn(p, src, c):
                for g in (2 * c, 2 * c + 1):
                    if g >= 4:
                        pe.wait_ge(a_lo, quarters(p) + g - 3)
                    for k in range(2):
                        for t in range(NT):
                            ins = tr(pt[:, g % 4, (2 * k + t) * P:(2 * k + t + 1) * P], src(2 * g + k, t), ident)
                    ins.then_inc(turned, 1)

            def h_tiles(kt, t):
                return H[:, t, kt * P:(kt + 1) * P]

            def mix2_tiles(k, t):
                return YF[:, t, k * P:(k + 1) * P] if k < 8 else YG[:, t, (k - 8) * P:(k - 7) * P]

            def first(p, src, quarter, hi, lo, g, when={0: (0, 1), 1: (2,), 3: (3,)}):
                def before(j):
                    for c in when.get(j, ()):
                        quarter(c)
                        turn(p, src, c)
                    pe.wait_ge(a_lo, quarters(p) + (min(j + 1, 4) if p == 1 else j + 1))
                chunk(g, 0, hi=hi, lo=lo, before=before)

            def last_quarter(g, p):
                def before(j):
                    if j == 2:
                        chunks_read(pe, g["C"] + 4)
                        turn(p, h_tiles, 3)
                    pe.wait_ge(a_lo, quarters(p) + j + 1)
                return before

            def turning(g, p, c):
                def before(j):
                    if j == 2:
                        chunks_read(pe, g["C"] + c)
                        turn(p, h_tiles, c - 1)
                return before

            def stream(g, hooks={}, loop=True):
                n = len(g["chunks"])
                chunk(g, 1)
                loops = uniform_pairs(g)
                if loops > 2 and loop:
                    with pe.Fori(0, loops - 1) as i:
                        for c in (2, 3):
                            chunk(g, c, dc=i * 2, dn=i * (2 * g["S"]))
                    done = 2 * loops
                else:
                    done = 2
                for c in range(done, n):
                    chunk(g, c, before=lambda j: hooks.get((c, j), no)())

            def conv_turn(c):
                chunks_read(pe, G["in1"]["C"] + c + 1)
                for g in (2 * (c - 2), 2 * (c - 2) + 1):
                    if g >= 4:
                        pe.wait_ge(cv_sum, g - 3)
                    for k in range(2):
                        for t in range(NT):
                            c0 = O_XBC + (2 * g + k) * P
                            ins = tr(pt[:, g % 4, (2 * k + t) * P:(2 * k + t + 1) * P], Z1[:, t, c0:c0 + P], ident)
                    ins.then_inc(cv_turned, 1)

            def x_back0():
                pe.wait_ge(cv_act, 4)
                for k in range(8):
                    ins = tr(pt[:, 2 + k // 4, (k % 4) * P:(k % 4 + 1) * P], XC[:, k, 0:P], ident)
                ins.then_inc(xt_turned, 1)

            def x_back1():
                pe.wait_ge(cv_act, 6)
                pe.wait_ge(xt_a, 1)
                for g in range(SSD_G):
                    tr(pt[:, 2, g * P:(g + 1) * P], XC[:, 8 + g, 0:P], ident)
                for k in range(8):
                    ins = tr(pt[:, k // 4, (k % 4) * P:(k % 4 + 1) * P], XC[:, k, P:TOK], ident)
                ins.then_inc(xt_turned, 1)

            def a_sums():
                pe.wait_ge(const_landed, 32)
                pe.wait_ge(adt_ready, 1)
                for t in range(NT):
                    mm(pt[:, 3, 16 * t:16 * t + 16], tri, SD[:, 2 + t, :], start=True, stop=True)
                mm(pt[:, 3, 32:48], ONES[:], SD[:, 2, :], start=True, stop=True).then_inc(acum_sum, 1)

            def kv_turn():
                pe.wait_ge(kv_twice, 1)
                pe.wait_ge(xt_d, 1)
                pe.wait_ge(acum_ready, 1)
                for b in range(4):
                    for h in range(2):
                        for t in range(NT):
                            src = KVD[:, b // 2, t, 2 * (b % 2) + h].rearrange("p a d -> p (a d)")
                            ins = tr(pt[:, b, h * TOK + t * P:h * TOK + (t + 1) * P], src, ident)
                    ins.then_inc(kc_turned, 1)

            def ssd():
                def hidden(i):
                    w, x = ((W1K, KFK), (W1V, KFV))[i]
                    for k in range(KT):
                        ins = mm(pt[0:60, 0, i * CMP_HID:(i + 1) * CMP_HID], x[:, k, :], w[:, k, :], start=k == 0, stop=k == KT - 1)
                    return ins

                def rows(t):
                    for h in range(SSD_H):
                        ins = mm(pg[:, h // 4, (h % 4) * P:(h % 4 + 1) * P], bc(SD[:, 2 + t, h:h + 1], P), tri, start=True, stop=True)
                    ins.then_inc(row_sum, 1)

                chunks_read(pe, G["out1"]["C"])
                pe.wait_ge(kflat, 4)
                rows(0)
                for t in range(NT):
                    for g in range(SSD_G):
                        ins = mm(pt[:, 3, (2 * t + g) * P:(2 * t + g + 1) * P], XC[:, 8 + g, t * P:(t + 1) * P],
                                 XC[:, 10 + g, t * P:(t + 1) * P], start=True, stop=True)
                ins.then_inc(cb_sum, 1)
                pe.wait_ge(cmpw_landed, 80)
                hidden(0)
                pe.wait_ge(seg_ready, 1)
                rows(1)
                pe.wait_ge(xs_ready, 1)
                for g in range(SSD_G):
                    ins = mm(pt[:, 1 + g, :], BT[:, g, :], XS[:, g * CW:(g + 1) * CW], start=True, stop=True)
                ins.then_inc(st_sum, 1)
                hidden(1).then_inc(hid_sum, 1)
                pe.wait_ge(seg_ready, 2)
                pe.wait_ge(xd_ready, 2)

                def diagonal(t):
                    pe.wait_ge(m_ready, t + 1)
                    for h in range(SSD_H):
                        ins = mm(pg[:, 2 * t + h // 8, (h % 8) * HD:(h % 8 + 1) * HD], M[:, t, h, :], XD[:, t, h * HD:(h + 1) * HD],
                                 start=True, stop=True)
                    ins.then_inc(yd_sum, 1)

                diagonal(0)
                pe.wait_ge(hid_act, 1)
                pe.wait_ge(st_ready, 1)
                for i in range(4):
                    ins = tr(pt[:, 1, i * 64:i * 64 + 60], HT_[0:60, i * P:(i + 1) * P], C[0:60, 0:60])
                ins.then_inc(hid_turned, 1)
                diagonal(1)
                for g in range(SSD_G):
                    ins = mm(pt[:, 3 * g, :], XC[:, 10 + g, P:TOK], STA[:, g, :], start=True, stop=True)
                ins.then_inc(yo_sum, 1)
                pe.wait_ge(hid_act, 3)
                for m in range(2):
                    mm(pt[:, 1, 256:316], W2K[:, m].rearrange("p a d -> p (a d)"), HK[:, m, :], start=m == 0, stop=m == 1)
                for h in range(NKV):
                    for m in range(2):
                        ins = mm(pt[:, 2, h * HD:(h + 1) * HD], HV[:, m, h].rearrange("p g i -> p (g i)"), W2V[:, m, :],
                                 start=m == 0, stop=m == 1)
                ins.then_inc(cmp_sum, 1)

            units = [(b, t, kv) for kv in range(NKV) for t in range(NT) for b in range(2)]

            def nsa():
                pe.wait_ge(yd_read, 2)
                for h in range(8):
                    for t in range(NT):
                        ins = tr(pg[:, h // 2, (h % 2) * TOK + t * P:(h % 2) * TOK + (t + 1) * P],
                                 Z1[:, t, O_Q + h * P:O_Q + (h + 1) * P], ident)
                ins.then_inc(q_turned, 1)
                pe.wait_ge(q_out, 2)
                pe.wait_ge(yo_read, 2)
                pe.wait_ge(cmp_kv, 6)
                for t in range(NT):
                    for x in range(NH // 2):
                        c0 = t * 256 + x * 32
                        ins = mm(pt[:, 0, c0:c0 + 32], QT[:, x, t * P:(t + 1) * P], KCB[:, x // 2, :], start=True, stop=True)
                ins.then_inc(cs_sum, 1)
                pe.wait_ge(roped, 1)
                for h in range(8):
                    for t in range(NT):
                        ins = tr(pg[:, h // 2, (h % 2) * TOK + t * P:(h % 2) * TOK + (t + 1) * P],
                                 Z1[:, t, O_Q + h * P:O_Q + (h + 1) * P], ident)
                ins.then_inc(q_turned, 1)
                pe.wait_ge(k_twice, 1)
                pe.wait_ge(cs_read, 1)
                for i in range(2):
                    for kv in range(NKV):
                        for t in range(NT):
                            src = KSD[:, i, t, kv].rearrange("p a d -> p (a d)")
                            c0 = (kv % 2) * TOK + t * P
                            ins = tr(pt[:, 2 * i + kv // 2, c0:c0 + P], src, ident)
                ins.then_inc(k_turned, 1)
                pe.wait_ge(k_out, 2)
                pe.wait_ge(q_out, 4)
                pe.wait_ge(pc_ready, 1)
                for t in range(NT):
                    for kv in range(NKV):
                        ins = tr(pt[:, t, kv * P:(kv + 1) * P], PC[:, t, 4 * kv:4 * kv + 4, :].rearrange("p h i -> p (h i)"), ident)
                ins.then_inc(pc_turned, 1)
                pe.wait_ge(pct_ready, 2)
                for u in range(19):
                    if u < 16:
                        b, t, kv = units[u]
                        nk = P * (1 + t)
                        if u >= 2:
                            pe.wait_ge(s_masked, 2 * (u - 1))
                        for x in range(2):
                            for e in range(2):
                                pr = slice(64 * e, 64 * e + 64)
                                ins = mm(pg[:, 2 * (u % 2) + e, x * nk:(x + 1) * nk], QT[pr, 2 * kv + x, t * P:(t + 1) * P],
                                         KTT[pr, b, kv, 0:nk], start=True, stop=True)
                        ins.then_inc(s_sum, 1)
                    if 2 <= u <= 17:
                        v = u - 2
                        t = units[v][1]
                        pe.wait_ge(s_scaled, v + 1)
                        if v >= 1:
                            pe.wait_ge(p_out0, v)
                            if units[v - 1][1]:
                                pe.wait_ge(p_out1, sum(x[1] for x in units[:v]))
                        for kb in range(1 + t):
                            for j in range(4):
                                ins = tr(pt[:, kb, j * P:(j + 1) * P], S[:, v % 3, j // 2, j % 2, kb * P:(kb + 1) * P], ident)
                        ins.then_inc(p_turned, 1)
                    if u >= 3:
                        v = u - 3
                        b, t, kv = units[v]
                        o = (O_VS, O_VW)[b] + kv * HD
                        pe.wait_ge(p_out0, v + 1)
                        if t:
                            pe.wait_ge(p_out1, sum(x[1] for x in units[:v + 1]))
                        dst = pt[:, 2 + (v // 2) % 2, :]
                        if b == 0 and v >= 4:
                            pe.wait_ge(o_out, v // 2 - 1)
                        for kb in range(1 + t):
                            for e in range(2):
                                ins = mm(dst[64 * e:64 * e + 64, 0:256], Z1[:, kb, o:o + HD],
                                         PT[:, v % 2, kb, 2 * e:2 * e + 2, :].rearrange("p x n -> p (x n)"),
                                         start=b == 0 and kb == 0, stop=b == 1 and kb == t)
                        if b == 0:
                            for j in range(4):
                                e, x = j % 2, j // 2
                                ins = mm(dst[64 * e:64 * e + 64, x * P:(x + 1) * P], BD[:, kv, j, :], PCT[:, t, kv, :],
                                         start=False, stop=False)
                        ins.then_inc(o_sum, 1)

            F1, F2 = G["ffn1"], G["ffn2"]

            def f1_turn(c, d):
                chunks_read(pe, F1["C"] + 2 * c + d * 2)
                if c > 1 or not isinstance(d, int):
                    pe.wait_ge(f_lo, c - 1 + d)
                for k in range(4):
                    for t in range(NT):
                        ins = tr(pt[:, k // 2, (k % 2) * TOK + t * P:(k % 2) * TOK + (t + 1) * P], HT[:, t, k * P:(k + 1) * P], ident)
                ins.then_inc(f_turned, 1)

            def f1_pair(c, d):
                dc, dn = d * 2, d * 16
                if c:
                    chunk(F1, 2 * c, 0, 4, dc, dn)
                    f1_turn(c, d)
                    chunk(F1, 2 * c, 4, 8, dc, dn)
                else:
                    chunk(F1, 0, before=last_quarter(G["out1"], 2))
                chunk(F1, 2 * c + 1, dc=dc, dn=dn)

            def f2_turn(b0, nth):
                for k in range(4):
                    for t in range(NT):
                        ins = tr(pt[:, b0 + k // 2, (k % 2) * TOK + t * P:(k % 2) * TOK + (t + 1) * P], UT[:, t, k * P:(k + 1) * P], ident)
                ins.then_inc(c_turned, 1)

            def f2_turn_up(c, d):
                chunks_read(pe, F2["C"] + 2 * c + d * 2)
                if c > 1 or not isinstance(d, int):
                    pe.wait_ge(c_sum, 2 * (c - 1) + d * 2)
                f2_turn(2, 0)

            def f2_pair(c, d):
                dc, dn = d * 2, d * 16
                if c:
                    chunk(F2, 2 * c, 0, 4, dc, dn)
                    f2_turn_up(c, d)
                    chunk(F2, 2 * c, 4, 8, dc, dn)
                else:
                    first(5, h_tiles, lambda q: pe.wait_ge(h_block, q + 1), AH, AL, F2)
                chunk(F2, 2 * c + 1, 0, 4, dc, dn)
                chunks_read(pe, F2["C"] + 2 * c + 1 + d * 2)
                if c:
                    pe.wait_ge(c_sum, 2 * c - 1 + d * 2)
                f2_turn(0, 0)
                chunk(F2, 2 * c + 1, 4, 8, dc, dn)

            def pairs(f):
                f(0, 0)
                with pe.Fori(0, NFF - 1) as i:
                    f(1, i)

            def down(g, turn_last, f0, before):
                pe.wait_ge(f_lo, f0 + NFF - 1)
                chunk(g, 0, 0, 4, hi=FH, lo=FL)
                turn_last()
                chunk(g, 0, 4, 20, hi=FH, lo=FL)
                pe.wait_ge(f_lo, f0 + NFF)
                chunk(g, 0, 20, hi=FH, lo=FL)
                for c in range(1, 4):
                    chunk(g, c, hi=FH, lo=FL, before=before(c))

            def fox_q():
                chunks_read(pe, G["in2"]["C"] + 2)
                for h in range(8):
                    for t in range(NT):
                        ins = tr(pt[:, h // 2, (h % 2) * TOK + t * P:(h % 2) * TOK + (t + 1) * P], Z2[:, t, h * P:(h + 1) * P], ident)
                ins.then_inc(fq_turned, 1)

            def fox_k():
                chunks_read(pe, G["in2"]["C"] + 4)
                pe.wait_ge(fq_out, 1)
                for h in range(8):
                    for t in range(NT):
                        ins = tr(pt[:, h // 2, (h % 2) * TOK + t * P:(h % 2) * TOK + (t + 1) * P],
                                 Z2[:, t, O2_K + h * P:O2_K + (h + 1) * P], ident)
                ins.then_inc(fq_turned, 1)

            def fox_sums(h0):
                pe.wait_ge(fk_out, 1)
                pe.wait_ge(lf_ready, 2)
                for h in range(h0, h0 + 4):
                    l0, l1 = (bc(SF_[:, 32 + 8 * t + h:33 + 8 * t + h], P) for t in range(NT))
                    o = pt[:, h // 2, (h % 2) * TOK:(h % 2 + 1) * TOK]
                    mm(o[:, 0:P], l0, tri, start=True, stop=True)
                    mm(o[:, P:TOK], l0, ONES[:], start=True, stop=False)
                    ins = mm(o[:, P:TOK], l1, tri, start=False, stop=True)
                if h0:
                    ins.then_inc(fc_sum, 1)

            def fox(u):
                if u == 0:
                    pe.wait_ge(fc_out, 1)
                if u < 8:
                    t, hp = u // 4, u % 4
                    nk = P * (1 + t)
                    if u >= 2:
                        pe.wait_ge(fs_max, u - 1)
                    for j in range(2):
                        h = 2 * hp + j
                        ins = mm(pt[:, u % 2, j * nk:(j + 1) * nk], QF[:, h, t * P:(t + 1) * P], KF2[:, h, 0:nk], start=True, stop=True)
                    ins.then_inc(fs_sum, 1)
                if 1 <= u <= 8:
                    t = (u - 1) // 4
                    pe.wait_ge(fs_exp, u)
                    if u >= 2:
                        pe.wait_ge(fp_out, u - 1)
                    for j in range(2):
                        for kb in range(1 + t):
                            ins = tr(pt[:, 2, (2 * j + kb) * P:(2 * j + kb + 1) * P], SF[:, (u - 1) % 2, j, kb * P:(kb + 1) * P], ident)
                    ins.then_inc(fp_turned, 1)
                if u >= 2:
                    v = u - 2
                    t, hp = v // 4, v % 4
                    pe.wait_ge(fp_out, v + 1)
                    if v >= 1:
                        pe.wait_ge(fo_out, v)
                    for j in range(2):
                        o = O2_V + (2 * hp + j) * P
                        for kb in range(1 + t):
                            ins = mm(pt[:, 3, j * P:(j + 1) * P], PF[:, v % 2, j, kb, :], Z2[:, kb, o:o + P],
                                     start=kb == 0, stop=kb == t)
                    ins.then_inc(fo_sum, 1)

            def hgrn_sums():
                pe.wait_ge(hg_lf, 2)
                for h in range(8):
                    for t in range(NT):
                        c0 = O2_HF + h * P
                        ins = mm(pt[:, h // 2, (h % 2) * TOK + t * P:(h % 2) * TOK + (t + 1) * P], Z2[:, t, c0:c0 + P], tri64,
                                 start=True, stop=True)
                ins.then_inc(hc_sum, 1)

            def hgrn():
                pe.wait_ge(hc_out, 1)
                for h in range(8):
                    for t in range(NT):
                        ins = tr(pt[:, h // 2, (h % 2) * TOK + t * P:(h % 2) * TOK + (t + 1) * P], YG[:, t, h * P:(h + 1) * P], ident)
                ins.then_inc(hk_turned, 1)
                chunks_read(pe, G["out2"]["C"])
                for h in range(8):
                    for t in range(NT):
                        ins = tr(pg[:, h // 2, (h % 2) * TOK + t * P:(h % 2) * TOK + (t + 1) * P],
                                 Z2[:, t, O2_HQ + h * P:O2_HQ + (h + 1) * P], ident)
                ins.then_inc(hq_turned, 1)
                pe.wait_ge(hq_out, 1)
                pe.wait_ge(hk_out, 1)

                def unit(u, lhs, rhs):
                    if u >= 4:
                        pe.wait_ge(lv_out, u - 3)
                    dst = lv_banks(u)
                    for h in range(8):
                        ins = mm(dst[:, h, :], lhs(h), rhs(h), start=True, stop=True)
                    ins.then_inc(lv_sum, 1)

                for t in range(NT):
                    unit(t, lambda h: HKT[:, h, t * P:(t + 1) * P], lambda h: HQ[:, h, t * P:(t + 1) * P])
                for l in range(8):
                    pe.wait_ge(lv_mul, l + 1)
                    if l:
                        pe.wait_ge(lv_mul_q, l)
                    g = LG[l % 2][:].rearrange("p (h n) -> p h n", h=8)
                    if l == 0:
                        unit(2, lambda h: g[:, h, 0:P], lambda h: g[:, h, P:TOK])
                    else:
                        for t in range(NT):
                            unit(1 + 2 * l + t, lambda h: g[:, h, t * P:(t + 1) * P], lambda h: g[:, h, t * P:(t + 1) * P])
                pe.wait_ge(lv_out, 15)
                turn(4, mix2_tiles, 0)
                pe.wait_ge(lv_out, 17)
                for h in range(8):
                    v = [Z2[:, t, O2_HI + h * P:O2_HI + (h + 1) * P] for t in range(NT)]
                    c0 = (h % 4) * P
                    mm(ho_banks(0)[:, h // 4, c0:c0 + P], HS[:, 0, h, :], v[0], start=True, stop=True)
                    mm(ho_banks(1)[:, h // 4, c0:c0 + P], HX[:, h, :], v[0], start=True, stop=False)
                    ins = mm(ho_banks(1)[:, h // 4, c0:c0 + P], HS[:, 1, h, :], v[1], start=False, stop=True)
                ins.then_inc(ho_sum, 1)

            pe.wait_ge(ident_landed, 16)
            pe.wait_ge(attn_landed, 16)
            tr(pg[:, 0, 0:16], VR[0:16, 0, :], C[0:16, 0:16]).then_inc(vec_turned, 1)

            def vectors():
                pe.wait_ge(vec_landed, 14 * 16)
                tr(pt[:, 0, 0:116], VR[0:116, 0, :], C[0:116, 0:116])
                tr(pt[:, 0, 116:196], VR[0:80, 1, :], C[0:80, 0:80])
                for j in range(4):
                    ins = tr(pt[:, 1, 88 * j:88 * j + 88], VR[0:88, 2 + j, :], C[0:88, 0:88])
                ins.then_inc(vec_turned, 1)

            def x_quarter(c):
                pe.wait_ge(x_landed[c], 16)

            pe.wait_ge(vec_ready, 1)
            first(0, h_tiles, x_quarter, AH, AL, G["in1"], {0: (0,), 2: (1,), 4: (2,), 6: (3,)})
            stream(G["in1"], {(2, 1): vectors, (3, 1): lambda: conv_turn(2), (4, 1): lambda: conv_turn(3), (5, 1): lambda: conv_turn(4),
                              (5, 4): x_back0, (6, 1): x_back1, (7, 2): a_sums, (9, 7): kv_turn}, loop=False)
            if upto < 3: return
            ssd()
            if upto < 4: return
            nsa()
            if upto < 5: return
            pe.wait_ge(o_out, 8)
            pe.wait_ge(xn0, 1)
            pe.wait_ge(xn1, 1)
            g = G["out1"]
            first(1, lambda k, t: YS[:, t, k * P:(k + 1) * P], lambda c: None, OH1, OL1, g, {0: (0, 1)})
            for c in range(1, 4):
                chunk(g, c, hi=OH1, lo=OL1, before=turning(g, 2, c))
            if upto < 8: return
            pairs(f1_pair)
            if upto < 9: return
            down(G["down1"], lambda: f1_turn(NFF, 0), 0, lambda c: turning(G["down1"], 3, c))
            if upto < 10: return
            chunk(G["in2"], 0, before=last_quarter(G["down1"], 3))
            hooks = {(3, 1): fox_q, (5, 1): fox_k, (7, 3): lambda: fox_sums(0), (7, 4): lambda: fox_sums(4), (12, 1): hgrn_sums}
            hooks.update({fox_place(u, 0): lambda u=u: fox(u) for u in range(10)})
            stream(G["in2"], hooks, loop=False)
            if upto < 13: return
            hgrn()
            if upto < 14: return

            def mix2_ready(c):
                if c == 1:
                    pe.wait_ge(ho_read, 2)
                if c == 2:
                    pe.wait_ge(yg_ready, 1)

            first(4, mix2_tiles, mix2_ready, OH2, OL2, G["out2"], {1: (1,), 4: (2, 3)})
            for c in range(1, 4):
                chunk(G["out2"], c, hi=OH2, lo=OL2)
            if upto < 17: return
            pairs(f2_pair)

            def turn_p(c):
                def before(j):
                    if c == 1 and j == 1:
                        pe.wait_ge(bc_landed, 96)
                        for k in range(2):
                            for t in range(NT):
                                ins = tr(pt[:, 3, (2 * k + t) * P:(2 * k + t + 1) * P], PIN[:, t, k * P:(k + 1) * P], ident)
                        ins.then_inc(p_tr, 1)
                return before

            down(G["down2"], lambda: f2_turn_up(NFF, 0), NFF, turn_p)
            if upto < 18: return
            pe.wait_ge(p_lo, 1)
            for c in range(4):
                chunk(G["proj"], c, hi=PH, lo=PL)
            g = G["ple"]
            first(6, h_tiles, lambda c: pe.wait_ge(h_block, 4 + c + 1), OH2, OL2, g)
            for c in range(1, 4):
                chunk(g, c, hi=OH2, lo=OL2)


def fox_place(u, later):
    return 8 + u // 4, 2 * (u % 4) + later


def uniform_pairs(g):
    n = sum(c[2] == CW for c in g["chunks"]) // 2
    if g["S"] % RING:
        return 0
    return n if len(g["chunks"]) > 2 * n and g["chunks"][2 * n][2] == CW or n * 2 == len(g["chunks"]) else n - 1


_INS = [
    "x", "attn_norm_w", "w_in", "conv_w", "conv_b", "dt_bias", "a_log", "d_skip", "ssd_norm_w", "cmp_w1_k",
    "cmp_w2_k", "cmp_w1_v", "cmp_w2_v", "cmp_pe_k", "cmp_pe_v", "w_out", "ffn_norm_w", "w_gate", "w_up",
    "w_down", "final_norm_w", "p_2", "g_mix_pre_2", "w_in_2", "b_fox_f_2", "g_hgrn_out_2", "w_out_2",
    "g_mix_post_2", "g_ffn_pre_2", "w_up_2", "conv_w_2", "conv_b_2", "w_down_2", "g_ffn_post_2",
    "g_ple_in_2", "w_ple_gate_2", "w_ple_proj_2", "g_ple_post_2",
]


def kernel(**inputs):
    import concourse.bacc as bacc
    from concourse.bass_utils import run_bass_kernel_spmd

    nc = bacc.Bacc("TRN2", target_bir_lowering=False, num_devices=1)
    consts, masks = constants()
    arrays = {n: np.ascontiguousarray(inputs[n]) for n in _INS}
    arrays["consts"], arrays["masks"] = consts, masks
    a = {n: nc.dram_tensor(n, v.shape, mybir.dt.from_np(v.dtype), kind="ExternalInput").ap() for n, v in arrays.items()}
    a["out"] = nc.dram_tensor("out", (1, TOK, D), F32, kind="ExternalOutput").ap()
    two_blocks(nc, a)
    r = run_bass_kernel_spmd(nc, [arrays], core_ids=[0])
    return r.results[0]["out"]
```
